# Optimizing a Trainium2 kernel written in Bass

```python
import math
import jax
import jax.numpy as jnp
from jax import lax
import numpy as np

D_MODEL = 1024
BATCH = 1
SEQ = 256
DEPTH = 2

GRID_W = 64
CTX_LEN = 256
ROPE_BASE = 10000.0
NORM_EPS = 1e-6
LB_FLOOR = 1e-30
Q_BLOCK = 128
CHUNK = 64

GLA_HEADS = 4
GLA_DK = 32
GLA_DV = 64
GLA_GATE_RANK = 16
GLA_GATE_NORM = 16.0
HG_HEADS = 4
HG_DIM = 64
MLA_HEADS = 4
MLA_Q_RANK = 192
MLA_KV_RANK = 128
MLA_NOPE = 64
MLA_ROPE = 32
MLA_DV = 64
DIFF_HEADS = 4
DIFF_DQK = 32
DIFF_DV = 64
PEER_HEADS = 8
PEER_NKEYS = 128
PEER_N_EXPERTS = PEER_NKEYS * PEER_NKEYS
PEER_DQ = 256
PEER_TOPK = 16
TOKEN_BLOCK = 128

GLA_COLS = (GLA_HEADS * GLA_DK, GLA_HEADS * GLA_DK, GLA_HEADS * GLA_DV, GLA_HEADS * GLA_DV, GLA_GATE_RANK, GLA_GATE_RANK)
HG_COLS = (HG_HEADS * HG_DIM,) * 5
MLA_COLS = (MLA_Q_RANK, MLA_KV_RANK, MLA_ROPE)
DIFF_COLS = (DIFF_HEADS * 2 * DIFF_DQK, DIFF_HEADS * 2 * DIFF_DQK, DIFF_HEADS * DIFF_DV)
MIXER_COLS = (sum(GLA_COLS), sum(HG_COLS), sum(MLA_COLS), sum(DIFF_COLS))
IN_COLS = sum(MIXER_COLS)
MIX_WIDTH = GLA_HEADS * GLA_DV + HG_HEADS * HG_DIM + MLA_HEADS * MLA_DV + DIFF_HEADS * DIFF_DV

kernel_name = 'hybrid_prefix_dit_gla_hgrn2_mla_diff_peer'

def rms_norm(x, g):
    xf = x.astype(jnp.float32)
    y = xf * lax.rsqrt(jnp.mean(xf * xf, axis=-1, keepdims=True) + NORM_EPS)
    return (y * g.astype(jnp.float32)).astype(x.dtype)

def modulate(h, shift, scale):
    return h * (1 + scale) + shift

def split_cols(a, sizes):
    return jnp.split(a, np.cumsum(sizes)[:-1].tolist(), axis=-1)

def to_heads(a, n):
    B, L, _ = a.shape
    return a.reshape(B, L, n, -1).transpose(0, 2, 1, 3)

def bhld(a):
    return a.transpose(0, 2, 1, 3)

def merge_heads(a):
    B, n, L, d = a.shape
    return a.transpose(0, 2, 1, 3).reshape(B, L, n * d)

def rope_1d(x, pos):
    half = x.shape[-1] // 2
    freqs = ROPE_BASE ** (-jnp.arange(half, dtype=jnp.float32) / half)
    ang = pos.astype(jnp.float32)[:, None, None] * freqs
    cos, sin = jnp.cos(ang), jnp.sin(ang)
    x1 = x[..., :half].astype(jnp.float32)
    x2 = x[..., half:].astype(jnp.float32)
    return jnp.concatenate([x1 * cos - x2 * sin, x1 * sin + x2 * cos], axis=-1).astype(x.dtype)

def rope_2d(x, rows, cols):
    h = x.shape[-1] // 2
    return jnp.concatenate([rope_1d(x[..., :h], rows), rope_1d(x[..., h:], cols)], axis=-1)

def blocked_attention(q, k, v, scale):
    B, H, S, dq = q.shape
    dv = v.shape[-1]
    nb = S // Q_BLOCK
    qb = q.reshape(B, H, nb, Q_BLOCK, dq).transpose(2, 0, 1, 3, 4)

    def one(qi):
        s = jnp.einsum('bhqd,bhkd->bhqk', qi, k).astype(jnp.float32) * scale
        p = jax.nn.softmax(s, axis=-1)
        return jnp.einsum('bhqk,bhkv->bhqv', p.astype(v.dtype), v)

    o = lax.map(one, qb)
    return o.transpose(1, 2, 0, 3, 4).reshape(B, H, S, dv)

def gated_chunk_scan(q, k, v, log_g, s0):
    B, H, L, dk = q.shape
    dv = v.shape[-1]
    n = L // CHUNK

    def chunks(a):
        return a.reshape(B, H, n, CHUNK, a.shape[-1]).transpose(2, 0, 1, 3, 4)

    lower = jnp.tril(jnp.ones((CHUNK, CHUNK), dtype=bool))[:, :, None]

    def step(state, inp):
        qi, ki, vi, gi = [a.astype(jnp.float32) for a in inp]
        b = jnp.cumsum(gi, axis=2)
        inter = jnp.einsum('bhtk,bhkv->bhtv', qi * jnp.exp(b), state)
        rel = b[:, :, :, None, :] - b[:, :, None, :, :]
        decay = jnp.where(lower, jnp.exp(jnp.where(lower, rel, 0.0)), 0.0)
        scores = jnp.einsum('bhtk,bhsk,bhtsk->bhts', qi, ki, decay)
        intra = jnp.einsum('bhts,bhsv->bhtv', scores, vi)
        b_end = b[:, :, -1:, :]
        new_state = (jnp.exp(b_end[:, :, 0, :])[..., None] * state
                     + jnp.einsum('bhsk,bhsv->bhkv', ki * jnp.exp(b_end - b), vi))
        return new_state, inter + intra

    s_final, o = lax.scan(step, s0.astype(jnp.float32), (chunks(q), chunks(k), chunks(v), chunks(log_g)))
    o = o.transpose(1, 2, 0, 3, 4).reshape(B, H, L, dv)
    return o.astype(v.dtype), s_final

def bidirectional_prefix_scan(ctx_in, lat_in):
    q_c, kf_c, kb_c, v_c, gf_c, gb_c = ctx_in
    q_l, kf_l, kb_l, v_l, gf_l, gb_l = lat_in
    B, H, _, dk = q_c.shape
    dv = v_c.shape[-1]
    zero = jnp.zeros((B, H, dk, dv), jnp.float32)

    def flip(a):
        return jnp.flip(a, axis=2)

    o_cf, s_f = gated_chunk_scan(q_c, kf_c, v_c, gf_c, zero)
    o_cb, s_b = gated_chunk_scan(flip(q_c), flip(kb_c), flip(v_c), flip(gb_c), zero)
    o_lf, _ = gated_chunk_scan(q_l, kf_l, v_l, gf_l, s_f)
    o_lb, _ = gated_chunk_scan(flip(q_l), flip(kb_l), flip(v_l), flip(gb_l), s_b)
    return o_cf + flip(o_cb), o_lf + flip(o_lb)

def gla_mixer(p_c, p_l, w_gate, b_gate, g_norm, need_ctx):
    def prep(p):
        q, k, v, r, zf, zb = split_cols(p, GLA_COLS)
        gf = jax.nn.log_sigmoid((zf @ w_gate[0] + b_gate[0]).astype(jnp.float32)) / GLA_GATE_NORM
        gb = jax.nn.log_sigmoid((zb @ w_gate[1] + b_gate[1]).astype(jnp.float32)) / GLA_GATE_NORM
        q = to_heads(q * GLA_DK ** -0.5, GLA_HEADS)
        k = to_heads(k, GLA_HEADS)
        return (q, k, k, to_heads(v, GLA_HEADS), to_heads(gf, GLA_HEADS), to_heads(gb, GLA_HEADS)), r

    c_in, r_c = prep(p_c)
    l_in, r_l = prep(p_l)
    o_c, o_l = bidirectional_prefix_scan(c_in, l_in)

    def finish(o, r):
        return merge_heads(rms_norm(o, g_norm)) * jax.nn.silu(r)

    return (finish(o_c, r_c) if need_ctx else None), finish(o_l, r_l)

def hgrn2_mixer(p_c, p_l, lb, g_norm, need_ctx):
    lb = lb.astype(jnp.float32)
    log_lb = jnp.log(jnp.maximum(lb, LB_FLOOR))
    log_1mlb = jnp.log1p(-lb)

    def gates(z):
        z = z.astype(jnp.float32)
        log_f = jnp.logaddexp(log_lb, log_1mlb + jax.nn.log_sigmoid(z))
        k = (1.0 - lb) * jax.nn.sigmoid(-z)
        return to_heads(k, HG_HEADS), to_heads(log_f, HG_HEADS)

    def prep(p):
        q, i, og, zf, zb = split_cols(p, HG_COLS)
        kf, gf = gates(zf)
        kb, gb = gates(zb)
        return (to_heads(jax.nn.silu(q), HG_HEADS), kf, kb, to_heads(i, HG_HEADS), gf, gb), og

    c_in, og_c = prep(p_c)
    l_in, og_l = prep(p_l)
    o_c, o_l = bidirectional_prefix_scan(c_in, l_in)

    def finish(o, og):
        return merge_heads(rms_norm(o, g_norm)) * jax.nn.silu(og)

    return (finish(o_c, og_c) if need_ctx else None), finish(o_l, og_l)

def mla_mixer(p_c, p_l, g_q, g_kv, w_uq, w_ukv, pos, need_ctx):
    def prep(p, grid_pos):
        B, L, _ = p.shape
        c_q, c_kv, k_rope = split_cols(p, MLA_COLS)
        q = (rms_norm(c_q, g_q) @ w_uq).reshape(B, L, MLA_HEADS, MLA_NOPE + MLA_ROPE)
        kv = (rms_norm(c_kv, g_kv) @ w_ukv).reshape(B, L, MLA_HEADS, MLA_NOPE + MLA_DV)
        q_nope, q_rope = q[..., :MLA_NOPE], q[..., MLA_NOPE:]
        k_nope, v = kv[..., :MLA_NOPE], kv[..., MLA_NOPE:]
        k_rope = k_rope[:, :, None, :]
        if grid_pos is not None:
            q_rope = rope_2d(q_rope, *grid_pos)
            k_rope = rope_2d(k_rope, *grid_pos)
        q = jnp.concatenate([q_nope, q_rope], axis=-1)
        k = jnp.concatenate([k_nope, jnp.broadcast_to(k_rope, (B, L, MLA_HEADS, MLA_ROPE))], axis=-1)
        return bhld(q), bhld(k), bhld(v)

    scale = (MLA_NOPE + MLA_ROPE) ** -0.5
    q_c, k_c, v_c = prep(p_c, None)
    q_l, k_l, v_l = prep(p_l, pos)
    o_l = blocked_attention(q_l, jnp.concatenate([k_c, k_l], axis=2), jnp.concatenate([v_c, v_l], axis=2), scale)
    o_c = merge_heads(blocked_attention(q_c, k_c, v_c, scale)) if need_ctx else None
    return o_c, merge_heads(o_l)

def diff_mixer(p_c, p_l, lam_params, g_norm, lambda_init, pos, need_ctx):
    lq1, lk1, lq2, lk2 = lam_params[0], lam_params[1], lam_params[2], lam_params[3]
    lam = (jnp.exp(jnp.sum(lq1 * lk1).astype(jnp.float32)) - jnp.exp(jnp.sum(lq2 * lk2).astype(jnp.float32))
           + lambda_init)

    def prep(p, grid_pos):
        B, L, _ = p.shape
        q, k, v = split_cols(p, DIFF_COLS)
        q = q.reshape(B, L, 2 * DIFF_HEADS, DIFF_DQK)
        k = k.reshape(B, L, 2 * DIFF_HEADS, DIFF_DQK)
        v = jnp.repeat(v.reshape(B, L, DIFF_HEADS, DIFF_DV), 2, axis=2)
        if grid_pos is not None:
            q = rope_2d(q, *grid_pos)
            k = rope_2d(k, *grid_pos)
        return bhld(q), bhld(k), bhld(v)

    def finish(o):
        B, _, L, dv = o.shape
        o = o.reshape(B, DIFF_HEADS, 2, L, dv)
        o = o[:, :, 0] - lam.astype(o.dtype) * o[:, :, 1]
        return merge_heads(rms_norm(o, g_norm) * (1.0 - lambda_init))

    scale = DIFF_DQK ** -0.5
    q_c, k_c, v_c = prep(p_c, None)
    q_l, k_l, v_l = prep(p_l, pos)
    o_l = blocked_attention(q_l, jnp.concatenate([k_c, k_l], axis=2), jnp.concatenate([v_c, v_l], axis=2), scale)
    o_c = finish(blocked_attention(q_c, k_c, v_c, scale)) if need_ctx else None
    return o_c, finish(o_l)

def peer_ffn(h, w_q, keys, u, v):
    B, L, D = h.shape
    tok = h.reshape(-1, TOKEN_BLOCK, D)

    def one(xb):
        T = xb.shape[0]
        q = (xb @ w_q).reshape(T, PEER_HEADS, 2, PEER_DQ // 2)
        s = jnp.einsum('thpd,hpnd->thpn', q, keys).astype(jnp.float32)
        s_top, i_top = lax.top_k(s, PEER_TOPK)
        cand = (s_top[:, :, 0, :, None] + s_top[:, :, 1, None, :]).reshape(T, PEER_HEADS, -1)
        cidx = (i_top[:, :, 0, :, None] * PEER_NKEYS + i_top[:, :, 1, None, :]).reshape(T, PEER_HEADS, -1)
        best, sel = lax.top_k(cand, PEER_TOPK)
        eidx = jnp.take_along_axis(cidx, sel, axis=-1)
        g = jax.nn.softmax(best, axis=-1)
        act = jax.nn.gelu(jnp.einsum('td,thkd->thk', xb, u[eidx]).astype(jnp.float32))
        return jnp.einsum('thk,thkd->td', (g * act).astype(v.dtype), v[eidx]).astype(h.dtype)

    return lax.map(one, tok).reshape(B, L, D)

def setup_inputs(seed: int = 0) -> dict:
    key = jax.random.key(seed)
    ks = jax.random.split(key, 26)
    D = D_MODEL

    def nrm(k, shape, scale):
        return jax.random.normal(k, shape, jnp.float32) * scale

    def gain(k, shape):
        return 1.0 + nrm(k, shape, 0.02)

    return {
        'x': nrm(ks[0], (BATCH, SEQ, D), 1.0),
        'c': nrm(ks[1], (BATCH, D), 1.0),
        'ctx': nrm(ks[2], (BATCH, CTX_LEN, D), 1.0),
        'c_ctx': nrm(ks[3], (D,), 1.0),
        'ada_w': nrm(ks[4], (DEPTH, D, 6 * D), 0.5 * D ** -0.5),
        'ada_b': nrm(ks[5], (DEPTH, 6 * D), 0.02),
        'norm_mix_g': gain(ks[6], (DEPTH, D)),
        'norm_ffn_g': gain(ks[7], (DEPTH, D)),
        'w_in': nrm(ks[8], (DEPTH, D, IN_COLS), D ** -0.5),
        'w_out': nrm(ks[9], (DEPTH, MIX_WIDTH, D), MIX_WIDTH ** -0.5),
        'gla_gate_w': nrm(ks[10], (DEPTH, 2, GLA_GATE_RANK, GLA_HEADS * GLA_DK), GLA_GATE_RANK ** -0.5),
        'gla_gate_b': nrm(ks[11], (DEPTH, 2, GLA_HEADS * GLA_DK), 0.1),
        'gla_norm_g': gain(ks[12], (DEPTH, GLA_DV)),
        'hgrn_lb_raw': nrm(ks[13], (DEPTH, HG_HEADS * HG_DIM), 0.1),
        'hgrn_norm_g': gain(ks[14], (DEPTH, HG_DIM)),
        'mla_q_norm_g': gain(ks[15], (DEPTH, MLA_Q_RANK)),
        'mla_kv_norm_g': gain(ks[16], (DEPTH, MLA_KV_RANK)),
        'mla_w_uq': nrm(ks[17], (DEPTH, MLA_Q_RANK, MLA_HEADS * (MLA_NOPE + MLA_ROPE)), MLA_Q_RANK ** -0.5),
        'mla_w_ukv': nrm(ks[18], (DEPTH, MLA_KV_RANK, MLA_HEADS * (MLA_NOPE + MLA_DV)), MLA_KV_RANK ** -0.5),
        'diff_lambda': nrm(ks[19], (DEPTH, 4, DIFF_DQK), 0.1),
        'diff_norm_g': gain(ks[20], (DEPTH, DIFF_DV)),
        'peer_wq': nrm(ks[21], (DEPTH, D, PEER_HEADS * PEER_DQ), D ** -0.5),
        'peer_keys': nrm(ks[22], (DEPTH, PEER_HEADS, 2, PEER_NKEYS, PEER_DQ // 2), (PEER_DQ // 2) ** -0.5),
        'peer_u': nrm(ks[23], (DEPTH, PEER_N_EXPERTS, D), D ** -0.5),
        'peer_v': nrm(ks[24], (DEPTH, PEER_N_EXPERTS, D), 0.3),
        'final_norm_g': gain(ks[25], (D,)),
    }

def reference(x, c, ctx, c_ctx, ada_w, ada_b, norm_mix_g, norm_ffn_g, w_in, w_out,
              gla_gate_w, gla_gate_b, gla_norm_g, hgrn_lb_raw, hgrn_norm_g,
              mla_q_norm_g, mla_kv_norm_g, mla_w_uq, mla_w_ukv, diff_lambda, diff_norm_g,
              peer_wq, peer_keys, peer_u, peer_v, final_norm_g):
    L = x.shape[1]
    ROWS = L // GRID_W
    rows = jnp.repeat(jnp.arange(ROWS, dtype=jnp.int32), GRID_W)
    cols = jnp.tile(jnp.arange(GRID_W, dtype=jnp.int32), ROWS)
    pos = (rows, cols)

    lb_sm = jax.nn.softmax(hgrn_lb_raw.astype(jnp.float32), axis=0)
    lb_all = jnp.cumsum(lb_sm, axis=0) - lb_sm[0]

    silu_c = jax.nn.silu(c)
    silu_cc = jax.nn.silu(c_ctx)
    xc = ctx
    for l in range(DEPTH):
        need_ctx = l < DEPTH - 1
        lambda_init = 0.8 - 0.6 * math.exp(-0.3 * l)
        mod_l = jnp.split((silu_c @ ada_w[l] + ada_b[l])[:, None, :], 6, axis=-1)
        mod_c = jnp.split(silu_cc @ ada_w[l] + ada_b[l], 6, axis=-1)

        h_l = modulate(rms_norm(x, norm_mix_g[l]), mod_l[0], mod_l[1])
        h_c = modulate(rms_norm(xc, norm_mix_g[l]), mod_c[0], mod_c[1])
        gla_l, hg_l, mla_l, dif_l = split_cols(h_l @ w_in[l], MIXER_COLS)
        gla_c, hg_c, mla_c, dif_c = split_cols(h_c @ w_in[l], MIXER_COLS)

        a_c, a_l = gla_mixer(gla_c, gla_l, gla_gate_w[l], gla_gate_b[l], gla_norm_g[l], need_ctx)
        b_c, b_l = hgrn2_mixer(hg_c, hg_l, lb_all[l], hgrn_norm_g[l], need_ctx)
        m_c, m_l = mla_mixer(mla_c, mla_l, mla_q_norm_g[l], mla_kv_norm_g[l], mla_w_uq[l], mla_w_ukv[l], pos, need_ctx)
        d_c, d_l = diff_mixer(dif_c, dif_l, diff_lambda[l], diff_norm_g[l], lambda_init, pos, need_ctx)

        x = x + mod_l[2] * (jnp.concatenate([a_l, b_l, m_l, d_l], axis=-1) @ w_out[l])
        x = x + mod_l[5] * peer_ffn(modulate(rms_norm(x, norm_ffn_g[l]), mod_l[3], mod_l[4]),
                                    peer_wq[l], peer_keys[l], peer_u[l], peer_v[l])
        if need_ctx:
            xc = xc + mod_c[2] * (jnp.concatenate([a_c, b_c, m_c, d_c], axis=-1) @ w_out[l])
            xc = xc + mod_c[5] * peer_ffn(modulate(rms_norm(xc, norm_ffn_g[l]), mod_c[3], mod_c[4]),
                                          peer_wq[l], peer_keys[l], peer_u[l], peer_v[l])
    return rms_norm(x, final_norm_g)


_drawn_inputs = setup_inputs


def setup_inputs(seed=0):
    import zlib

    import numpy as np

    out = dict(_drawn_inputs(seed))
    spreads = {}
    factors = {'norm_mix_g': 5.883,
     'norm_ffn_g': 27.886,
     'gla_gate_b': 6.512,
     'gla_norm_g': 8.0,
     'hgrn_lb_raw': 8.0,
     'hgrn_norm_g': 8.0,
     'mla_q_norm_g': 8.0,
     'mla_kv_norm_g': 8.0,
     'diff_lambda': 5.209,
     'diff_norm_g': 64.0,
     'final_norm_g': 7.855}
    for name, (base, spread) in spreads.items():
        noise = np.random.default_rng([zlib.crc32(name.encode()), seed]).standard_normal(out[name].shape)
        drawn = base * np.exp(spread * noise) if base else spread * noise
        out[name] = jnp.asarray(drawn.astype(out[name].dtype))
    for name, factor in factors.items():
        out[name] = (out[name] * factor).astype(out[name].dtype)
    return out
```

```python
from contextlib import ExitStack
import math

import numpy as np

import concourse.bass as bass
from concourse import mybir

F32 = mybir.dt.float32
BF16 = mybir.dt.bfloat16
U32 = mybir.dt.uint32
I32 = mybir.dt.int32
ALU = mybir.AluOpType
ACT = mybir.ActivationFunctionType
AX = mybir.AxisListType.X

P = 128
BANK = 512
EPS = 1e-6
D_MODEL = 1024
DC = D_MODEL // P
CTX = 256
SEQ = 256
T = CTX + SEQ
TT = T // P
DEPTH = 2
GRID_W = 64
ROPE_BASE = 10000.0

GLA_HEADS, GLA_DK = 4, 32
GLA_GATE_NORM = 16.0
HG_CHUNKS = 2
LB_FLOOR = 1e-30
DV = 64
HEADS = 4
MLA_Q, MLA_KV, MLA_NOPE, MLA_ROPE = 192, 128, 64, 32
MLA_DQ = MLA_NOPE + MLA_ROPE
DIFF_DQK = 32

GATE0 = 0
HQ = 4
GQ, GK = 6, 7
HZ = 8
CQ0, CQ1, CKV = 12, 13, 14
DQ, DK = 15, 17
FM = 19
SILU_CHUNKS = 6
TMC = 3 * HEADS * DV
KR0, GZ0 = 64, 96

LEVELS = [64, 32, 16, 8, 4, 2, 1]
NL = len(LEVELS)
HALF = P // 2
UNITS = [((0, 0), (0, 1)), ((0, 2), (0, 3)), ((0, 4), (0, 5)), ((0, 6), (1, 6)),
         ((1, 0), (1, 1)), ((1, 2), (1, 3)), ((1, 4), (1, 5)), None]
NU = len(UNITS)
XQ_TILES = [(1, 3, 2, 3), (0, 2, 2, 3)]
XK_TILES = [(0, 2, 0, 1), (1, 3, 0, 1)]

PH = 8
NKEY = 128
TOPK = 16
GE = 4
NG = NKEY // GE
NEG = -3.0e38
SMALL = 2.0 ** -40
UP = 2.0 ** 60


class Chain:

    def __init__(self, sem):
        self.sem, self.n = sem, 0

    def __call__(self, eng, ins):
        self.n += 1
        ins.then_inc(self.sem, 1)
        eng.wait_ge(self.sem, self.n)


def bc(ap, axis, n):
    ap = ap.unsqueeze(axis)
    shape = list(ap.shape)
    shape[axis] = n
    return ap.to_broadcast(shape)


def halves(ap, L, side):
    return ap.rearrange("p a (n two l) -> p a n two l", two=2, l=L)[:, :, :, side, :]


def mids(ap, L):
    return halves(ap, L, 1)[:, :, :, 0:1].to_broadcast([P, TT, HALF // L, L])


def build(nc, d, out):
    ctx = ExitStack()

    layer_sems = []

    def sem(name):
        layer_sems.append(nc.alloc_semaphore(name=name))
        return layer_sems[-1]

    def clear_layer_sems():
        nc.clear_and_free_semaphores(layer_sems)
        layer_sems.clear()
        nc.all_engine_barrier()

    def sb(st, name, shape, dt=F32):
        return st.enter_context(nc.sbuf_tensor(name, shape, dt))

    with ctx:
        ps = ctx.enter_context(nc.psum_tensor("ps", [P, 8, BANK], F32))
        xT = sb(ctx, "xT", [P, DC, T])
        mod = sb(ctx, "mod", [P, 6 * DC, 2])
        ident = sb(ctx, "ident", [P, P])
        ones = sb(ctx, "ones", [P, P])
        meanD = sb(ctx, "meanD", [P, P])
        mean64 = sb(ctx, "mean64", [P, P])
        rotp = sb(ctx, "rotp", [P, P])
        cosT = sb(ctx, "cosT", [P, SEQ])
        sinT = sb(ctx, "sinT", [P, SEQ])
        mask = sb(ctx, "mask", [P, 2 * NL, HALF], I32)
        maskd = sb(ctx, "maskd", [P, P], I32)
        iota = sb(ctx, "iota", [P, P])
        iotab = sb(ctx, "iotab", [P, P], BF16)
        cvec = sb(ctx, "cvec", [P, DC, 2])
        silu_c = sb(ctx, "silu_c", [P, DC, 2])
        onecol = sb(ctx, "onecol", [P, 1])
        epscol = sb(ctx, "epscol", [P, 1])
        dve_chain = Chain(ctx.enter_context(nc.semaphore("dve_chain")))

        def phase_start():
            loaded = sem("consts_loaded")
            c_in = sem("c_in")
            const = [(xT, d["xT"]), (ident, d["ident"]), (mean64, d["mean64"]), (rotp, d["rotp"]),
                     (cosT, d["cosT"]), (sinT, d["sinT"]), (mask, d["mask"]), (maskd, d["maskd"]), (iota, d["iota"])]
            with nc.Block() as block:
                @block.sync
                def _(sp):
                    sp.dma_start(cvec[:], d["cvec"]).then_inc(c_in, 16)
                    for dst, src in const:
                        sp.dma_start(dst[:], src).then_inc(loaded, 16)
                    sp.wait_ge(loaded, 16 * len(const))

                @block.vector
                def _(dve):
                    nc.vector.memset(ones[:], 1.0)
                    nc.vector.memset(meanD[:], 1.0 / D_MODEL)
                    nc.vector.memset(onecol[:], 1.0)
                    nc.vector.memset(epscol[:], EPS)
                    dve.wait_ge(loaded, 16 * len(const))
                    nc.vector.tensor_copy(iotab[:], iota[:])

                @block.scalar
                def _(act):
                    act.wait_ge(c_in, 16)
                    nc.scalar.activation(silu_c[:], cvec[:], ACT.Silu)

        def phase_ada(l):
            slab_in = [sem(f"ada_in{l}_{r}") for r in range(2)]
            slab_used, bias_in = sem(f"ada_used{l}"), sem(f"ada_b_in{l}")
            with ExitStack() as st:
                slab = sb(st, f"ada_slab{l}", [P, 2, DC, D_MODEL])
                bias = sb(st, f"ada_bias{l}", [P, 6 * DC])
                with nc.Block() as block:
                    @block.sync
                    def _(sp):
                        sp.dma_start(bias[:], d["ada_b"][l]).then_inc(bias_in, 16)
                        for m in range(6):
                            if m >= 2:
                                sp.wait_ge(slab_used, m - 1)
                            src = d["ada_w"][l, :, m * D_MODEL:(m + 1) * D_MODEL].rearrange("(k p) n -> p k n", p=P)
                            sp.dma_start(slab[:, m % 2], src).then_inc(slab_in[m % 2], 16)

                    @block.tensor
                    def _(pe):
                        for m in range(6):
                            pe.wait_ge(slab_in[m % 2], 16 * (m // 2 + 1))
                            for j in range(DC):
                                o = 2 * (m * DC + j)
                                for k in range(DC):
                                    mm = nc.tensor.matmul(ps[:, 0, o:o + 2], slab[:, m % 2, k, j * P:(j + 1) * P],
                                                          silu_c[:, k, :], start=(k == 0), stop=(k == DC - 1))
                            mm.then_inc(slab_used, 1)

                    @block.vector
                    def _(dve):
                        dve.wait_ge(bias_in, 16)
                        dve.wait_ge(slab_used, 6)
                        got = ps[:, 0, 0:12 * DC].rearrange("p (n v) -> p n v", v=2)
                        nc.vector.tensor_tensor(mod[:], got, bc(bias[:], 2, 2), ALU.add)

        def phase_norm(name, gain, which, lo, dst):
            n = T - lo
            g_in, sq_done, sum_done, scaled = (sem(f"{name}_{x}") for x in ("g_in", "sq_done", "sum_done", "scaled"))
            a_done, root_done = sem(f"{name}_a_done"), sem(f"{name}_root_done")
            with ExitStack() as st:
                g = sb(st, f"{name}_g", [P, DC])
                amp = sb(st, f"{name}_amp", [P, DC, 2])
                rstd = sb(st, f"{name}_rstd", [P, T])
                with nc.Block() as block:
                    @block.sync
                    def _(sp):
                        sp.dma_start(g[:], gain).then_inc(g_in, 16)

                    @block.scalar
                    def _(act):
                        for k in range(DC):
                            nc.scalar.activation(dst[:, k, lo:T], xT[:, k, lo:T], ACT.Square).then_inc(sq_done, 1)
                        act.wait_ge(sum_done, 1)
                        nc.scalar.activation(rstd[:, lo:T], ps[:, 0, 0:n], ACT.Sqrt, bias=epscol[:]).then_inc(root_done, 1)
                        if which is None:
                            return
                        act.wait_ge(a_done, 1)
                        for k in range(DC):
                            act.wait_ge(scaled, k // 2 + 1)
                            for v, (a, b) in enumerate(((lo, CTX), (max(lo, CTX), T))):
                                if a < b:
                                    w = 1 - v
                                    nc.scalar.activation(dst[:, k, a:b], dst[:, k, a:b], ACT.Identity,
                                                         bias=mod[:, which * DC + k, w:w + 1],
                                                         scale=amp[:, k, w:w + 1])

                    @block.tensor
                    def _(pe):
                        for k in range(DC):
                            pe.wait_ge(sq_done, k + 1)
                            mm = nc.tensor.matmul(ps[:, 0, 0:n], meanD[:], dst[:, k, lo:T],
                                                  start=(k == 0), stop=(k == DC - 1))
                        mm.then_inc(sum_done, 1)

                    @block.vector
                    def _(dve):
                        dve.wait_ge(g_in, 16)
                        if which is not None:
                            dve_chain(dve, nc.vector.tensor_scalar(
                                amp[:], mod[:, (which + 1) * DC:(which + 2) * DC, :], 1.0, None, ALU.add))
                            nc.vector.tensor_tensor(amp[:], amp[:], bc(g[:], 2, 2), ALU.mult).then_inc(a_done, 1)
                        dve.wait_ge(root_done, 1)
                        dve_chain(dve, nc.vector.reciprocal(rstd[:, lo:T], rstd[:, lo:T]))
                        if which is None:
                            for k in range(DC):
                                nc.vector.scalar_tensor_tensor(out=dst[:, k, lo:T], in0=xT[:, k, lo:T], scalar=g[:, k:k + 1],
                                                               in1=rstd[:, lo:T], op0=ALU.mult, op1=ALU.mult)
                            return
                        for k in range(0, DC, 2):
                            nc.vector.tensor_tensor(dst[:, k:k + 2, lo:T], xT[:, k:k + 2, lo:T],
                                                    bc(rstd[:, lo:T], 1, 2), ALU.mult).then_inc(scaled, 1)

        def phase_proj(l, hT, fm, tm):
            RW = 4
            w_in = [sem(f"proj_w_in{l}_{r}") for r in range(RW)]
            mm_done, ev_done = sem(f"proj_mm{l}"), sem(f"proj_ev{l}")
            tw_in, tmm_done, tev_done = sem(f"projt_w_in{l}"), sem(f"projt_mm{l}"), sem(f"projt_ev{l}")
            with ExitStack() as st:
                slab = sb(st, f"proj_slab{l}", [P, RW, DC, P])
                tslab = sb(st, f"proj_tslab{l}", [P, DC, TMC])
                with nc.Block() as block:
                    @block.sync
                    def _(sp):
                        for c in range(FM):
                            if c >= RW:
                                sp.wait_ge(mm_done, c - RW + 1)
                            sp.dma_start(slab[:, c % RW], d["w_fm"][l, c]).then_inc(w_in[c % RW], 16)
                            if c == RW - 1:
                                sp.dma_start(tslab[:], d["w_tm"][l]).then_inc(tw_in, 16)

                    @block.tensor
                    def _(pe):
                        for c in range(FM):
                            pe.wait_ge(w_in[c % RW], 16 * (c // RW + 1))
                            if c >= 4:
                                pe.wait_ge(ev_done, c - 3)
                            for k in range(DC):
                                mm = nc.tensor.matmul(ps[:, c % 4, :], slab[:, c % RW, k, :], hT[:, k, :],
                                                      start=(k == 0), stop=(k == DC - 1))
                            mm.then_inc(mm_done, 1)
                        pe.wait_ge(tw_in, 16)
                        for n in range(2 * TT):
                            if n >= 4:
                                pe.wait_ge(tev_done, n - 3)
                            cols = slice((n % 2) * TMC // 2, (n % 2 + 1) * TMC // 2)
                            for k in range(DC):
                                mm = nc.tensor.matmul(ps[:, 4 + n % 4, 0:TMC // 2], hT[:, k, (n // 2) * P:(n // 2 + 1) * P],
                                                      tslab[:, k, cols], start=(k == 0), stop=(k == DC - 1))
                            mm.then_inc(tmm_done, 1)

                    @block.scalar
                    def _(act):
                        for c in range(FM):
                            act.wait_ge(mm_done, c + 1)
                            nc.scalar.activation(fm[:, c, :], ps[:, c % 4, :], ACT.Silu if c < SILU_CHUNKS else ACT.Copy,
                                                 scale=GLA_DK ** -0.5 if c == GQ else 1.0).then_inc(ev_done, 1)

                    @block.vector
                    def _(dve):
                        for n in range(2 * TT):
                            dve.wait_ge(tmm_done, n + 1)
                            cols = slice((n % 2) * TMC // 2, (n % 2 + 1) * TMC // 2)
                            nc.vector.tensor_copy(tm[:, n // 2, cols], ps[:, 4 + n % 4, 0:TMC // 2]).then_inc(tev_done, 1)

        def phase_gates(l, fm, hk, cum):
            loaded, z_done, e_ready, e_done, f_ready, l_done = (
                sem(f"gates_{x}{l}") for x in ("loaded", "z_done", "e_ready", "e_done", "f_ready", "l_done"))
            with ExitStack() as st:
                lg = sb(st, f"lg{l}", [P, 6, T])
                e = sb(st, f"gate_e{l}", [P, 4, T])
                r = sb(st, f"gate_r{l}", [P, 4, T])
                m = sb(st, f"gate_m{l}", [P, 4, T])
                a = sb(st, f"gate_a{l}", [P, 2, T])
                ea = sb(st, f"gate_ea{l}", [P, 2, T])
                wg = sb(st, f"gate_w{l}", [P, 2, P])
                bg = sb(st, f"gate_b{l}", [P, 2])
                lbr = sb(st, f"lb_raw{l}", [P, DEPTH, HG_CHUNKS])
                lbe = sb(st, f"lb_exp{l}", [P, DEPTH, HG_CHUNKS])
                lbs = sb(st, f"lb_sum{l}", [P, 4, HG_CHUNKS])
                with nc.Block() as block:
                    @block.sync
                    def _(sp):
                        sp.dma_start(wg[GZ0:P], d["gate_w"][l]).then_inc(loaded, 16)
                        sp.dma_start(bg[:], d["gate_b"][l]).then_inc(loaded, 16)
                        sp.dma_start(lbr[:], d["lb_raw"]).then_inc(loaded, 16)

                    @block.tensor
                    def _(pe):
                        pe.wait_ge(loaded, 48)
                        for k in range(2):
                            nc.tensor.matmul(ps[:, k, :], wg[GZ0:P, k, :], fm[GZ0:P, CQ1, :],
                                             start=True, stop=True).then_inc(z_done, 1)

                    @block.scalar
                    def _(act):
                        act.wait_ge(e_ready, 1)
                        nc.scalar.activation(lbe[:], lbe[:], ACT.Exp).then_inc(e_done, 1)
                        act.wait_ge(e_ready, 2)
                        nc.scalar.activation(e[:], e[:], ACT.Exp).then_inc(e_done, 1)
                        act.wait_ge(e_ready, 3)
                        nc.scalar.activation(ea[:], ea[:], ACT.Exp).then_inc(e_done, 1)
                        act.wait_ge(e_done, 3)
                        nc.scalar.activation(ea[:], ea[:], ACT.Ln, bias=onecol[:], scale=1.0).then_inc(l_done, 1)
                        act.wait_ge(f_ready, 1)
                        nc.scalar.activation(r[:], r[:], ACT.Ln).then_inc(l_done, 1)

                    @block.vector
                    def _(dve):
                        def step(ins):
                            dve_chain(dve, ins)
                        dve.wait_ge(loaded, 48)
                        step(nc.vector.tensor_tensor(lbs[:, 0], lbr[:, 0], lbr[:, 1], ALU.max))
                        nc.vector.tensor_tensor(lbe[:], lbr[:], bc(lbs[:, 0], 1, DEPTH), ALU.subtract).then_inc(e_ready, 1)
                        nc.vector.tensor_scalar(e[:], fm[:, HZ:HZ + 4, :], -1.0, 80.0, ALU.mult, ALU.min).then_inc(e_ready, 1)
                        for k in range(2):
                            dve.wait_ge(z_done, k + 1)
                            step(nc.vector.tensor_scalar(a[:, k], ps[:, k, :], bg[:, k:k + 1], None, ALU.add))
                        nc.vector.scalar_tensor_tensor(out=ea[:], in0=a[:], scalar=-1.0, in1=a[:],
                                                       op0=ALU.mult, op1=ALU.min).then_inc(e_ready, 1)
                        dve.wait_ge(e_done, 1)
                        step(nc.vector.tensor_tensor(lbs[:, 0], lbe[:, 0], lbe[:, 1], ALU.add))
                        step(nc.vector.reciprocal(lbs[:, 1], lbs[:, 0]))
                        step(nc.vector.tensor_tensor(lbe[:], lbe[:], bc(lbs[:, 1], 1, DEPTH), ALU.mult))
                        step(nc.vector.tensor_copy(lbs[:, 0], lbe[:, 0]))
                        for i in range(1, l + 1):
                            step(nc.vector.tensor_tensor(lbs[:, 0], lbs[:, 0], lbe[:, i], ALU.add))
                        step(nc.vector.tensor_tensor(lbs[:, 1], lbs[:, 0], lbe[:, 0], ALU.subtract))
                        step(nc.vector.tensor_scalar(lbs[:, 2], lbs[:, 1], -1.0, 1.0, ALU.mult, ALU.add))
                        step(nc.vector.tensor_scalar(lbs[:, 3], lbs[:, 1], LB_FLOOR, None, ALU.max))
                        dve.wait_ge(e_done, 2)
                        step(nc.vector.tensor_scalar(r[:], e[:], 1.0, None, ALU.add))
                        step(nc.vector.reciprocal(r[:], r[:]))
                        for j in range(4):
                            c = j % 2
                            nc.vector.scalar_tensor_tensor(out=hk[:, j], in0=e[:, j], scalar=lbs[:, 2, c:c + 1],
                                                           in1=r[:, j], op0=ALU.mult, op1=ALU.mult)
                        for j in range(4):
                            c = j % 2
                            step(nc.vector.tensor_scalar(r[:, j], r[:, j], lbs[:, 2, c:c + 1], lbs[:, 3, c:c + 1],
                                                         ALU.mult, ALU.add))
                        step(nc.vector.tensor_scalar(m[:], r[:], SMALL, None, ALU.is_lt))
                        step(nc.vector.tensor_scalar(e[:], m[:], UP - 1.0, 1.0, ALU.mult, ALU.add))
                        nc.vector.tensor_tensor(r[:], r[:], e[:], ALU.mult).then_inc(f_ready, 1)
                        dve.wait_ge(l_done, 1)
                        step(nc.vector.scalar_tensor_tensor(out=a[:], in0=a[:], scalar=0.0, in1=ea[:],
                                                            op0=ALU.min, op1=ALU.subtract))
                        for k in range(2):
                            step(nc.vector.tensor_scalar(lg[:, 3 * k], a[:, k], 1.0 / GLA_GATE_NORM, None, ALU.mult))
                        dve.wait_ge(l_done, 2)
                        for k in range(2):
                            step(nc.vector.scalar_tensor_tensor(
                                out=lg[:, 3 * k + 1:3 * k + 3], in0=m[:, 2 * k:2 * k + 2], scalar=-60.0 * math.log(2.0),
                                in1=r[:, 2 * k:2 * k + 2], op0=ALU.mult, op1=ALU.add))
                        nc.vector.memset(cum[:, :, :, 0:1], 0.0)
                        for s in range(6):
                            for t in range(TT):
                                nc.vector.tensor_tensor_scan(cum[:, s, t, 1:P + 1], ones[:], lg[:, s, t * P:(t + 1) * P],
                                                             0.0, ALU.mult, ALU.add)

        def phase_scan(l, fm, tm, hk, cum, mix):
            arg_done, exp_done, xexp_done, fac_done, ready, unit_mm, unit_ev, x_mm, x_ev, o_mm, o_ev = (
                sem(f"scan_{x}{l}") for x in ("arg_done", "exp_done", "xexp_done", "fac_done", "ready", "unit_mm", "unit_ev",
                                              "x_mm", "x_ev", "o_mm", "o_ev"))
            zeroed, tot_done = sem(f"scan_zeroed{l}"), sem(f"scan_tot_done{l}")
            heads = [(0, GLA_DK * h, GLA_DK) for h in range(4)] + [(1 + h // 2, 64 * (h % 2), 64) for h in range(4)]
            first = [0, 4, 6, 8]
            with ExitStack() as st:
                ex = sb(st, f"scan_ex{l}", [P, 2, 2, NL, TT * HALF])
                lk = sb(st, f"scan_lk{l}", [P, 2, NL, TT, P])
                xq = sb(st, f"scan_xq{l}", [P, 2, 4, P])
                xk = sb(st, f"scan_xk{l}", [P, 2, 4, P])
                ksum = sb(st, f"scan_ksum{l}", [P, T])
                tot2 = sb(st, f"scan_tot2{l}", [P, 2, 6])
                sc = sb(st, f"scan_sc{l}", [P, 2, TT, P])
                scx = sb(st, f"scan_scx{l}", [P, 2, 2, BANK])

                def keys(c, dr):
                    return fm[:, GK, :] if c == 0 else hk[:, 2 * dr + c - 1, :]

                def queries(c):
                    return fm[:, GQ if c == 0 else HQ + c - 1, :]

                with nc.Block() as block:
                    @block.vector
                    def _(dve):
                        nc.vector.memset(lk[:], 0.0).then_inc(zeroed, 1)
                        dve.wait_ge(zeroed, 1)
                        for j in range(2):
                            nc.vector.tensor_tensor(tot2[:, j], cum[:, :, 2 * j, P], cum[:, :, 2 * j + 1, P], ALU.add)\
                                .then_inc(tot_done, 1)

                        def factors(c):
                            if c:
                                dve.wait_ge(unit_mm, NU * first[c])
                                dve.wait_ge(x_mm, first[c])
                            for dr in range(2):
                                cb = cum[:, 3 * dr + c]
                                lo, hi = cb[:, :, 0:P], cb[:, :, 1:P + 1]
                                for i, L in enumerate(LEVELS):
                                    mid = mids(lo, L)
                                    qa = ex[:, dr, 0, i].rearrange("p (a n l) -> p a n l", a=TT, l=L)
                                    ka = ex[:, dr, 1, i].rearrange("p (a n l) -> p a n l", a=TT, l=L)
                                    if dr == 0:
                                        nc.vector.tensor_tensor(qa, halves(hi, L, 1), mid, ALU.subtract)
                                        last = nc.vector.tensor_tensor(ka, mid, halves(hi, L, 0), ALU.subtract)
                                    else:
                                        nc.vector.tensor_tensor(qa, mid, halves(lo, L, 0), ALU.subtract)
                                        last = nc.vector.tensor_tensor(ka, halves(lo, L, 1), mid, ALU.subtract)
                                last.then_inc(arg_done, 1)
                            for dr in range(2):
                                q = queries(c).rearrange("p (a t) -> p a t", a=TT)
                                k = keys(c, dr).rearrange("p (a t) -> p a t", a=TT)
                                dve.wait_ge(exp_done, 2 * c + dr + 1)
                                for i, L in enumerate(LEVELS):
                                    qa = ex[:, dr, 0, i].rearrange("p (a n l) -> p a n l", a=TT, l=L)
                                    ka = ex[:, dr, 1, i].rearrange("p (a n l) -> p a n l", a=TT, l=L)
                                    nc.vector.tensor_tensor(qa, qa, halves(q, L, 1 - dr), ALU.mult)
                                    nc.vector.tensor_tensor(halves(lk[:, dr, i], L, dr), ka, halves(k, L, dr), ALU.mult)
                                dve.wait_ge(xexp_done, 2 * c + dr + 1)
                                for j in (0, 1):
                                    a, b = XQ_TILES[dr][j], XK_TILES[dr][j]
                                    nc.vector.tensor_tensor(xq[:, dr, j], xq[:, dr, j], q[:, a], ALU.mult)
                                    nc.vector.tensor_tensor(xk[:, dr, j], xk[:, dr, j], k[:, b], ALU.mult)
                                nc.vector.tensor_tensor(xq[:, dr, 2:4], xq[:, dr, 2:4], q[:, 2:4], ALU.mult)
                                nc.vector.tensor_tensor(xk[:, dr, 2:4], xk[:, dr, 2:4], k[:, 0:2], ALU.mult)
                            nc.vector.tensor_tensor(ksum[:], keys(c, 0), keys(c, 1), ALU.add).then_inc(ready, 1)

                        def gather(h):
                            for u, unit in enumerate(UNITS):
                                n = NU * h + u
                                dve.wait_ge(unit_mm, n + 1)
                                if n:
                                    dve.wait_ge(unit_ev, n)
                                if u == 0 and h >= 2:
                                    dve.wait_ge(o_mm, h - 1)
                                dst = sc[:, h % 2]
                                if unit is None:
                                    nc.vector.copy_predicated(dst, bc(maskd[:], 1, TT),
                                                              ps[:, n % 4, :].rearrange("p (a t) -> p a t", a=TT)).then_inc(unit_ev, 1)
                                    continue
                                for j, (dr, i) in enumerate(unit):
                                    L = LEVELS[i]
                                    got = ps[:, n % 4, j * 256:(j + 1) * 256].rearrange("p (a n l) -> p a n l", a=TT, l=L)
                                    msk = bc(mask[:, NL * dr + i].rearrange("p (n l) -> p n l", l=L), 1, TT)
                                    copied = nc.vector.copy_predicated(halves(dst, L, 1 - dr), msk, got)
                                    if j == 0:
                                        dve_chain(dve, copied)
                                    else:
                                        copied.then_inc(unit_ev, 1)

                        for c in range(3):
                            factors(c)
                            for h in range(first[c], first[c + 1]):
                                gather(h)

                    @block.scalar
                    def _(act):
                        def exps(c):
                            for dr in range(2):
                                act.wait_ge(arg_done, 2 * c + dr + 1)
                                nc.scalar.activation(ex[:, dr], ex[:, dr], ACT.Exp).then_inc(exp_done, 1)
                                s = 3 * dr + c
                                cb = cum[:, s]
                                tot = [cum[:, s, t, P:P + 1] for t in range(TT)]
                                tot01, tot23 = tot2[:, 0, s:s + 1], tot2[:, 1, s:s + 1]
                                if c == 0 and dr == 0:
                                    act.wait_ge(tot_done, 2)
                                if dr == 0:
                                    o = 1
                                    jobs = [(xq, 0, 1, 1.0, None), (xq, 1, 3, 1.0, None), (xq, 2, 2, 1.0, None), (xq, 3, 3, 1.0, tot[2]),
                                            (xk, 0, 0, -1.0, tot[0]), (xk, 1, 2, -1.0, tot[2]),
                                            (xk, 2, 0, -1.0, tot01), (xk, 3, 1, -1.0, tot[1])]
                                else:
                                    o = 0
                                    jobs = [(xq, 0, 0, -1.0, tot[0]), (xq, 1, 2, -1.0, tot[2]),
                                            (xq, 2, 2, -1.0, tot23), (xq, 3, 3, -1.0, tot[3]),
                                            (xk, 0, 1, 1.0, None), (xk, 1, 3, 1.0, None),
                                            (xk, 2, 0, 1.0, None), (xk, 3, 1, 1.0, tot[0])]
                                for buf, j, t, scale, bias in jobs:
                                    src = cb[:, t, o:o + P]
                                    if bias is None:
                                        last = nc.scalar.activation(buf[:, dr, j], src, ACT.Exp, scale=scale)
                                    else:
                                        last = nc.scalar.activation(buf[:, dr, j], src, ACT.Exp, scale=scale, bias=bias)
                                last.then_inc(xexp_done, 1)

                        def evac(h):
                            act.wait_ge(x_mm, h + 1)
                            if h >= 2:
                                act.wait_ge(o_mm, h - 1)
                            nc.scalar.activation(scx[:, h % 2], ps[:, 4:6, :], ACT.Copy).then_inc(x_ev, 1)

                        def out(h):
                            act.wait_ge(o_mm, h + 1)
                            p0 = 64 * (h % 2)
                            nc.scalar.activation(mix[p0:p0 + 64, h // 2, :], ps[p0:p0 + 64, 6 + h % 2, :], ACT.Copy).then_inc(o_ev, 1)

                        for c in range(3):
                            if c:
                                act.wait_ge(x_mm, first[c])
                            exps(c)
                            for h in range(first[c], first[c + 1]):
                                evac(h)
                                if h:
                                    out(h - 1)
                        out(7)

                    @block.tensor
                    def _(pe):
                        def scores(h):
                            c, p0, w = heads[h]
                            if h == first[c]:
                                pe.wait_ge(ready, c + 1)
                            r = slice(p0, p0 + w)
                            q = queries(c)
                            for u, unit in enumerate(UNITS):
                                n = NU * h + u
                                if n >= 4:
                                    pe.wait_ge(unit_ev, n - 3)
                                if unit is None:
                                    for t in range(TT):
                                        mm = nc.tensor.matmul(ps[:, n % 4, t * P:(t + 1) * P], ksum[r, t * P:(t + 1) * P],
                                                              q[r, t * P:(t + 1) * P], start=True, stop=True)
                                else:
                                    for j, (dr, i) in enumerate(unit):
                                        for t in range(TT):
                                            o = j * 256 + t * HALF
                                            mm = nc.tensor.matmul(ps[:, n % 4, o:o + HALF], lk[r, dr, i, t, :],
                                                                  ex[r, dr, 0, i, t * HALF:(t + 1) * HALF], start=True, stop=True)
                                mm.then_inc(unit_mm, 1)
                            if h >= 1:
                                pe.wait_ge(x_ev, h)
                            for dr in range(2):
                                for j in range(2):
                                    o = (2 * dr + j) * P
                                    nc.tensor.matmul(ps[:, 4, o:o + P], xk[r, dr, j, :], xq[r, dr, j, :], start=True, stop=True)
                            for s in range(2):
                                for dr in range(2):
                                    mm = nc.tensor.matmul(ps[:, 5, s * 256:(s + 1) * 256], xk[r, dr, 2 + s, :],
                                                          xq[r, dr, 2:4, :], start=(dr == 0), stop=(dr == 1))
                            mm.then_inc(x_mm, 1)

                        def output(h):
                            pe.wait_ge(unit_ev, NU * (h + 1))
                            pe.wait_ge(x_ev, h + 1)
                            if h >= 2:
                                pe.wait_ge(o_ev, h - 1)
                            p0 = 64 * (h % 2)
                            for t in range(TT):
                                parts = [(t, sc[:, h % 2, t, :])]
                                for dr in range(2):
                                    for j in range(2):
                                        if XQ_TILES[dr][j] == t:
                                            o = (2 * dr + j) * P
                                            parts.append((XK_TILES[dr][j], scx[:, h % 2, 0, o:o + P]))
                                if t >= 2:
                                    for s in range(2):
                                        o = s * 256 + (t - 2) * P
                                        parts.append((s, scx[:, h % 2, 1, o:o + P]))
                                for j, (s, sco) in enumerate(parts):
                                    mm = nc.tensor.matmul(ps[p0:p0 + 64, 6 + h % 2, t * P:(t + 1) * P],
                                                          tm[:, s, h * DV:(h + 1) * DV], sco,
                                                          start=(j == 0), stop=(j == len(parts) - 1))
                            mm.then_inc(o_mm, 1)

                        for h in range(8):
                            scores(h)
                            if h:
                                output(h - 1)
                        output(7)

        def phase_attn(l, fm, tm, mix):
            lam_init = 0.8 - 0.6 * math.exp(-0.3 * l)
            (loaded, sq_done, sum_done, n_done, qk_mm, qk_ev, rot_mm, rot_ev, prep_done, lam_e, lam_x, s_done, nm_done, exp_done,
             diag_done, t_done, ptc_done, pv_done, oev_done, root_done) = (
                sem(f"attn_{x}{l}") for x in ("loaded", "sq_done", "sum_done", "n_done", "qk_mm", "qk_ev", "rot_mm", "rot_ev",
                                              "prep_done", "lam_e", "lam_x", "s_done", "nm_done", "exp_done", "diag_done", "t_done",
                                              "ptc_done", "pv_done", "oev_done", "root_done"))
            NUN = 2 * HEADS * TT
            ncomp = [1 if n < HEADS * TT else 2 for n in range(NUN)]
            c0 = [sum(ncomp[:n]) for n in range(NUN + 1)]
            with ExitStack() as st:
                wq = sb(st, f"mla_wq{l}", [P, 2, HEADS, MLA_DQ])
                wkv = sb(st, f"mla_wkv{l}", [P, HEADS, P])
                gq = sb(st, f"mla_gq{l}", [P, 2])
                gkv = sb(st, f"mla_gkv{l}", [P, 1])
                sq = sb(st, f"mla_sq{l}", [P, 3, T])
                rs = sb(st, f"mla_rs{l}", [P, 2, T])
                qh = sb(st, f"mla_qh{l}", [P, HEADS, T])
                kh = sb(st, f"mla_kh{l}", [P, HEADS, T])
                vm = sb(st, f"mla_v{l}", [P, TT, HEADS * DV])
                rot = sb(st, f"rot{l}", [P, 2, SEQ])
                lamr = sb(st, f"lamr{l}", [P, 4, DIFF_DQK])
                lamp = sb(st, f"lamp{l}", [P, 2, DIFF_DQK])
                lame = sb(st, f"lame{l}", [P, 2])
                nlam = sb(st, f"nlam{l}", [P, 1])
                pr = sb(st, f"probs{l}", [P, 2, 2, T])
                pt = sb(st, f"probsT{l}", [P, 2, T])
                dg = sb(st, f"diag{l}", [P, 2, 2, P])
                mx = sb(st, f"smax{l}", [P, c0[-1]])
                nm = sb(st, f"nsmax{l}", [P, c0[-1]])
                rsum = sb(st, f"rsum{l}", [P, c0[-1]])
                rinv = sb(st, f"rinv{l}", [P, c0[-1]])
                rots = [(slice(0, P), fm[:, DQ + j, CTX:T]) for j in range(4)] + \
                       [(slice(KR0, KR0 + 32), fm[KR0:KR0 + 32, CQ1, CTX:T])] + \
                       [(slice(KR0, KR0 + 32), qh[KR0:KR0 + 32, h, CTX:T]) for h in range(HEADS)]
                with nc.Block() as block:
                    @block.sync
                    def _(sp):
                        sp.dma_start(wq[:, 0], d["w_uq"][l, 0:P]).then_inc(loaded, 16)
                        sp.dma_start(wq[0:64, 1], d["w_uq"][l, P:MLA_Q]).then_inc(loaded, 16)
                        sp.dma_start(wkv[:], d["w_ukv"][l]).then_inc(loaded, 16)
                        sp.dma_start(gq[:, 0:1], d["g_q0"][l]).then_inc(loaded, 16)
                        sp.dma_start(gq[0:64, 1:2], d["g_q1"][l]).then_inc(loaded, 16)
                        sp.dma_start(gkv[:], d["g_kv"][l]).then_inc(loaded, 16)
                        sp.dma_start(lamr[:], d["lam"][l].partition_broadcast(P)).then_inc(loaded, 16)

                    @block.scalar
                    def _(act):
                        nc.scalar.activation(sq[:, 0], fm[:, CQ0, :], ACT.Square)
                        nc.scalar.activation(sq[0:64, 1], fm[0:64, CQ1, :], ACT.Square)
                        nc.scalar.activation(sq[:, 2], fm[:, CKV, :], ACT.Square).then_inc(sq_done, 1)
                        act.wait_ge(lam_e, 1)
                        nc.scalar.activation(lame[:], lame[:], ACT.Exp).then_inc(lam_x, 1)
                        act.wait_ge(sum_done, 1)
                        for j, width in enumerate((MLA_Q, MLA_KV)):
                            nc.scalar.activation(rs[:, j], ps[:, j, :], ACT.Sqrt, scale=1.0 / width,
                                                 bias=epscol[:]).then_inc(root_done, 1)
                        for n in range(3 * HEADS):
                            act.wait_ge(qk_mm, n + 1)
                            bank = n % 4
                            if n < HEADS:
                                nc.scalar.activation(qh[0:MLA_DQ, n], ps[0:MLA_DQ, bank, :], ACT.Copy).then_inc(qk_ev, 1)
                            elif n < 2 * HEADS:
                                nc.scalar.activation(kh[0:64, n - HEADS], ps[0:64, bank, :], ACT.Copy).then_inc(qk_ev, 1)
                            else:
                                nc.scalar.activation(vm[:, n - 2 * HEADS], ps[:, bank, 0:HEADS * DV], ACT.Copy).then_inc(qk_ev, 1)

                        def exps(n):
                            for c in range(ncomp[n]):
                                j = c0[n] + c
                                act.wait_ge(nm_done, j + 1)
                                if n >= 2:
                                    act.wait_ge(t_done, n - 1)
                                ns = T if n % TT >= 2 else CTX
                                scale = (MLA_DQ if n < HEADS * TT else DIFF_DQK) ** -0.5
                                nc.scalar.activation(pr[:, n % 2, c, 0:ns], ps[:, 2 * (n % 2) + c, 0:ns], ACT.Exp, scale=scale,
                                                     bias=nm[:, j:j + 1], accum_out=rsum[:, j:j + 1]).then_inc(exp_done, 1)

                        def turned(n):
                            act.wait_ge(t_done, n + 1)
                            if n >= 2:
                                act.wait_ge(pv_done, n - 1)
                            ns = T if n % TT >= 2 else CTX
                            nc.scalar.activation(pt[:, n % 2, 0:ns], ps[:, 4 + n % 2, 0:ns], ACT.Copy).then_inc(ptc_done, 1)

                        def evac(h):
                            act.wait_ge(pv_done, TT * (h + 1))
                            p0 = 64 * (h % 2)
                            nc.scalar.activation(mix[p0:p0 + 64, 4 + h // 2, :], ps[p0:p0 + 64, 6 + h % 2, :], ACT.Copy).then_inc(oev_done, 1)

                        exps(0)
                        for n in range(NUN):
                            if n + 1 < NUN:
                                exps(n + 1)
                            turned(n)
                            if n % TT == 1 and n > TT:
                                evac(n // TT - 1)
                        evac(2 * HEADS - 1)

                    @block.tensor
                    def _(pe):
                        pe.wait_ge(sq_done, 1)
                        nc.tensor.matmul(ps[:, 0, :], ones[:], sq[:, 0], start=True, stop=False)
                        nc.tensor.matmul(ps[:, 0, :], ones[0:64, :], sq[0:64, 1], start=False, stop=True)
                        nc.tensor.matmul(ps[:, 1, :], ones[:], sq[:, 2], start=True, stop=True).then_inc(sum_done, 1)
                        pe.wait_ge(n_done, 1)
                        for n in range(3 * HEADS):
                            bank = n % 4
                            if n >= 4:
                                pe.wait_ge(qk_ev, n - 3)
                            h = n % HEADS
                            if n < HEADS:
                                nc.tensor.matmul(ps[0:MLA_DQ, bank, :], wq[:, 0, h, :], fm[:, CQ0, :], start=True, stop=False)
                                mm = nc.tensor.matmul(ps[0:MLA_DQ, bank, :], wq[0:64, 1, h, :], fm[0:64, CQ1, :],
                                                      start=False, stop=True)
                            elif n < 2 * HEADS:
                                mm = nc.tensor.matmul(ps[0:64, bank, :], wkv[:, h, 0:MLA_NOPE], fm[:, CKV, :], start=True, stop=True)
                            else:
                                mm = nc.tensor.matmul(ps[:, bank, 0:HEADS * DV], fm[:, CKV, h * P:(h + 1) * P],
                                                      wkv[:, :, MLA_NOPE:P], start=True, stop=True)
                            mm.then_inc(qk_mm, 1)
                        for n, (rows, x) in enumerate(rots):
                            if n == 5:
                                pe.wait_ge(qk_ev, HEADS)
                            if n >= 2:
                                pe.wait_ge(rot_ev, n - 1)
                            nc.tensor.matmul(ps[rows, 4 + n % 2, 0:SEQ], rotp[rows, rows], x, start=True, stop=True).then_inc(rot_mm, 1)
                        pe.wait_ge(prep_done, 1)
                        pe.wait_ge(qk_ev, 3 * HEADS)

                        def scores(n):
                            h, t = n // TT, n % TT
                            ns = T if t >= 2 else CTX
                            for c in range(ncomp[n]):
                                if n >= 2:
                                    pe.wait_ge(exp_done, c0[n - 1])
                                if h < HEADS:
                                    q, k = qh[0:MLA_DQ, h, t * P:(t + 1) * P], kh[0:MLA_DQ, h, 0:ns]
                                else:
                                    j = 2 * (h - HEADS) + c
                                    r = slice(32 * (j % 4), 32 * (j % 4) + 32)
                                    q, k = fm[r, DQ + j // 4, t * P:(t + 1) * P], fm[r, DK + j // 4, 0:ns]
                                nc.tensor.matmul(ps[:, 2 * (n % 2) + c, 0:ns], q, k, start=True, stop=True).then_inc(s_done, 1)

                        def turn(n):
                            pe.wait_ge(diag_done, c0[n + 1])
                            if n >= 2:
                                pe.wait_ge(ptc_done, n - 1)
                            for s in range(4 if n % TT >= 2 else 2):
                                for c in range(ncomp[n]):
                                    mm = nc.tensor.matmul(ps[:, 4 + n % 2, s * P:(s + 1) * P], pr[:, n % 2, c, s * P:(s + 1) * P],
                                                          dg[:, n % 2, c, :], start=(c == 0), stop=(c == ncomp[n] - 1))
                            mm.then_inc(t_done, 1)

                        def values(n):
                            h, t = n // TT, n % TT
                            pe.wait_ge(ptc_done, n + 1)
                            if t == 0 and h >= 2:
                                pe.wait_ge(oev_done, h - 1)
                            p0 = 64 * (h % 2)
                            nst = 4 if t >= 2 else 2
                            for s in range(nst):
                                v = vm[:, s, h * DV:(h + 1) * DV] if h < HEADS else \
                                    tm[:, s, (h + HEADS) * DV:(h + HEADS + 1) * DV]
                                mm = nc.tensor.matmul(ps[p0:p0 + 64, 6 + h % 2, t * P:(t + 1) * P], v, pt[:, n % 2, s * P:(s + 1) * P],
                                                      start=(s == 0), stop=(s == nst - 1))
                            mm.then_inc(pv_done, 1)

                        scores(0)
                        for n in range(NUN):
                            if n + 1 < NUN:
                                scores(n + 1)
                            turn(n)
                            if n:
                                values(n - 1)
                        values(NUN - 1)

                    @block.vector
                    def _(dve):
                        def step(ins):
                            dve_chain(dve, ins)
                        dve.wait_ge(loaded, 7 * 16)
                        step(nc.vector.tensor_tensor(lamp[:], lamr[:, 0:4:2], lamr[:, 1:4:2], ALU.mult))
                        nc.vector.tensor_reduce(lame[:], lamp[:], AX, ALU.add).then_inc(lam_e, 1)
                        dve.wait_ge(lam_x, 1)
                        step(nc.vector.tensor_tensor(nlam[:], lame[:, 1:2], lame[:, 0:1], ALU.subtract))
                        step(nc.vector.tensor_scalar(nlam[:], nlam[:], -lam_init, None, ALU.add))
                        dve.wait_ge(root_done, 2)
                        step(nc.vector.reciprocal(rs[:], rs[:]))
                        for x, g, r in ((fm[:, CQ0, :], gq[:, 0:1], rs[:, 0]), (fm[0:64, CQ1, :], gq[0:64, 1:2], rs[0:64, 0]),
                                        (fm[:, CKV, :], gkv[:], rs[:, 1])):
                            last = nc.vector.scalar_tensor_tensor(out=x, in0=x, scalar=g, in1=r, op0=ALU.mult, op1=ALU.mult)
                        last.then_inc(n_done, 1)
                        for n, (rows, x) in enumerate(rots):
                            dve.wait_ge(rot_mm, n + 1)
                            nc.vector.tensor_tensor(rot[rows, n % 2], ps[rows, 4 + n % 2, 0:SEQ], sinT[rows], ALU.mult).then_inc(rot_ev, 1)
                            step(nc.vector.tensor_tensor(x, x, cosT[rows], ALU.mult))
                            dve.wait_ge(rot_ev, n + 1)
                            last = nc.vector.tensor_tensor(x, x, rot[rows, n % 2], ALU.add)
                            if n == 4:
                                step(last)
                                for h in range(HEADS):
                                    nc.vector.tensor_copy(kh[KR0:KR0 + 32, h], fm[KR0:KR0 + 32, CQ1, :])
                        last.then_inc(prep_done, 1)

                        def maxima(n):
                            ns = T if n % TT >= 2 else CTX
                            scale = (MLA_DQ if n < HEADS * TT else DIFF_DQK) ** -0.5
                            for c in range(ncomp[n]):
                                j = c0[n] + c
                                dve.wait_ge(s_done, j + 1)
                                step(nc.vector.tensor_reduce(mx[:, j:j + 1], ps[:, 2 * (n % 2) + c, 0:ns], AX, ALU.max))
                                nc.vector.tensor_scalar(nm[:, j:j + 1], mx[:, j:j + 1], -scale, None, ALU.mult).then_inc(nm_done, 1)

                        def diagonals(n):
                            for c in range(ncomp[n]):
                                j = c0[n] + c
                                dve.wait_ge(exp_done, j + 1)
                                step(nc.vector.reciprocal(rinv[:, j:j + 1], rsum[:, j:j + 1]))
                                if n >= 2:
                                    dve.wait_ge(t_done, n - 1)
                                if c == 0:
                                    nc.vector.tensor_scalar(dg[:, n % 2, c], ident[:], rinv[:, j:j + 1], None, ALU.mult).then_inc(diag_done, 1)
                                else:
                                    nc.vector.tensor_scalar(dg[:, n % 2, c], ident[:], rinv[:, j:j + 1], nlam[:], ALU.mult, ALU.mult)\
                                        .then_inc(diag_done, 1)

                        maxima(0)
                        for n in range(NUN):
                            if n + 1 < NUN:
                                maxima(n + 1)
                            diagonals(n)

        def phase_post(l, fm, mix):
            lam_init = 0.8 - 0.6 * math.exp(-0.3 * l)
            chunks = [0, 1, 2, 3, 6, 7]
            loaded, sq_done, sum_done, root_done = (sem(f"post_{x}{l}") for x in ("loaded", "sq_done", "sum_done", "root_done"))
            with ExitStack() as st:
                sq = sb(st, f"post_sq{l}", [P, 6, T])
                g = sb(st, f"post_g{l}", [P, 3])
                with nc.Block() as block:
                    @block.sync
                    def _(sp):
                        sp.dma_start(g[:], d["g_head"][l]).then_inc(loaded, 16)

                    @block.scalar
                    def _(act):
                        for j, c in enumerate(chunks):
                            nc.scalar.activation(sq[:, j], mix[:, c, :], ACT.Square).then_inc(sq_done, 1)
                        for j in range(6):
                            act.wait_ge(sum_done, j + 1)
                            nc.scalar.activation(sq[:, j], ps[:, j, :], ACT.Sqrt, bias=epscol[:]).then_inc(root_done, 1)

                    @block.tensor
                    def _(pe):
                        for j in range(6):
                            pe.wait_ge(sq_done, j + 1)
                            nc.tensor.matmul(ps[:, j, :], mean64[:], sq[:, j], start=True, stop=True).then_inc(sum_done, 1)

                    @block.vector
                    def _(dve):
                        def step(ins):
                            dve_chain(dve, ins)
                        dve.wait_ge(loaded, 16)
                        step(nc.vector.tensor_scalar(g[:, 2:3], g[:, 2:3], 1.0 - lam_init, None, ALU.mult))
                        for j, c in enumerate(chunks):
                            dve.wait_ge(root_done, j + 1)
                            step(nc.vector.reciprocal(sq[:, j], sq[:, j]))
                            step(nc.vector.scalar_tensor_tensor(out=mix[:, c], in0=mix[:, c], scalar=g[:, j // 2:j // 2 + 1],
                                                                in1=sq[:, j], op0=ALU.mult, op1=ALU.mult))
                            if c < 4:
                                nc.vector.tensor_tensor(mix[:, c], mix[:, c], fm[:, GATE0 + c, :], ALU.mult)

        def add_gated(k, which, src, lo):
            n = []
            for v, (a, b) in enumerate(((lo, CTX), (max(lo, CTX), T))):
                if a < b:
                    w = 1 - v
                    n.append(nc.vector.scalar_tensor_tensor(out=xT[:, k, a:b], in0=src[:, a - lo:b - lo],
                                                            scalar=mod[:, which * DC + k, w:w + 1], in1=xT[:, k, a:b],
                                                            op0=ALU.mult, op1=ALU.add))
            return n[-1]

        def phase_out(l, lo, mix):
            RW = 4
            w_in = [sem(f"out_w_in{l}_{r}") for r in range(RW)]
            mm_done, ev_done = sem(f"out_mm{l}"), sem(f"out_ev{l}")
            with ExitStack() as st:
                slab = sb(st, f"out_slab{l}", [P, RW, DC, P])
                with nc.Block() as block:
                    @block.sync
                    def _(sp):
                        for c in range(DC):
                            if c >= RW:
                                sp.wait_ge(mm_done, c - RW + 1)
                            sp.dma_start(slab[:, c % RW], d["w_out"][l, c]).then_inc(w_in[c % RW], 16)

                    @block.tensor
                    def _(pe):
                        for c in range(DC):
                            pe.wait_ge(w_in[c % RW], 16 * (c // RW + 1))
                            if c >= 4:
                                pe.wait_ge(ev_done, c - 3)
                            for k in range(DC):
                                mm = nc.tensor.matmul(ps[:, c % 4, 0:T - lo], slab[:, c % RW, k, :], mix[:, k, lo:T],
                                                      start=(k == 0), stop=(k == DC - 1))
                            mm.then_inc(mm_done, 1)

                    @block.vector
                    def _(dve):
                        for c in range(DC):
                            dve.wait_ge(mm_done, c + 1)
                            add_gated(c, 2, ps[:, c % 4, :], lo).then_inc(ev_done, 1)

        def phase_route(l, lo, h2, iT, jT, gp):
            RW = 4
            nt = (T - lo) // P
            n = T - lo
            HP = 2 * PH
            w_in = [sem(f"route_w_in{l}_{r}") for r in range(RW)]
            (k_in, q_mm, q_ev, s_mm, s_ev, s_used, b_done, x_done, tr_in, tr_mm, tr_ev) = (
                sem(f"route_{x}{l}") for x in ("k_in", "q_mm", "q_ev", "s_mm", "s_ev", "s_used", "b_done", "x_done",
                                               "tr_in", "tr_mm", "tr_ev"))
            with ExitStack() as st:
                slab = sb(st, f"route_slab{l}", [P, RW, DC, P])
                kT = sb(st, f"route_keys{l}", [P, HP, NKEY])
                qT = sb(st, f"route_q{l}", [P, 2, n])
                s_sb = sb(st, f"route_s{l}", [P, 2, nt, NKEY])
                s2 = sb(st, f"route_s2{l}", [P, 2 * NKEY])
                top = sb(st, f"route_top{l}", [P, nt, HP, TOPK])
                idx = sb(st, f"route_idx{l}", [P, nt, HP, TOPK], U32)
                idf = sb(st, f"route_idf{l}", [P, nt, HP, TOPK])
                cand = sb(st, f"route_cand{l}", [P, PH, TOPK, TOPK])
                best = sb(st, f"route_best{l}", [P, PH, TOPK])
                sel = sb(st, f"route_sel{l}", [P, PH, TOPK], U32)
                sela = sb(st, f"route_sela{l}", [P, 2, PH * TOPK], U32)
                self_ = sb(st, f"route_self{l}", [P, 2, PH * TOPK])
                eq = sb(st, f"route_eq{l}", [P, PH * TOPK, TOPK])
                ijg = sb(st, f"route_ijg{l}", [P, 2, 3, PH * TOPK])
                esum = sb(st, f"route_esum{l}", [P, PH])
                gT = sb(st, f"route_gT{l}", [P, P])
                with nc.Block() as block:
                    @block.sync
                    def _(sp):
                        for c in range(HP):
                            if c >= RW:
                                sp.wait_ge(q_mm, c - RW + 1)
                            sp.dma_start(slab[:, c % RW], d["w_pq"][l, c]).then_inc(w_in[c % RW], 16)
                            if c == 0:
                                sp.dma_start(kT[:], d["keysT"][l]).then_inc(k_in, 16)

                    @block.tensor
                    def _(pe):
                        def sub_scores(c):
                            pe.wait_ge(q_ev, c + 1)
                            pe.wait_ge(k_in, 16)
                            if c >= 2:
                                pe.wait_ge(s_ev, c - 1)
                            for t in range(nt):
                                mm = nc.tensor.matmul(ps[:, 2 + c % 2, t * P:(t + 1) * P], qT[:, c % 2, t * P:(t + 1) * P], kT[:, c, :],
                                                      start=True, stop=True)
                            mm.then_inc(s_mm, 1)

                        for c in range(HP):
                            pe.wait_ge(w_in[c % RW], 16 * (c // RW + 1))
                            if c >= 2:
                                pe.wait_ge(q_ev, c - 1)
                            for k in range(DC):
                                mm = nc.tensor.matmul(ps[:, c % 2, 0:n], slab[:, c % RW, k, :], h2[:, k, lo:T],
                                                      start=(k == 0), stop=(k == DC - 1))
                            mm.then_inc(q_mm, 1)
                            if c:
                                sub_scores(c - 1)
                        sub_scores(HP - 1)
                        for t in range(nt):
                            pe.wait_ge(tr_in, t + 1)
                            if t >= 1:
                                pe.wait_ge(tr_ev, t)
                            for j in range(3):
                                mm = nc.tensor.transpose(ps[:, 4, j * P:(j + 1) * P], ijg[:, t % 2, j, :], ident[:])
                            mm.then_inc(tr_mm, 1)

                    @block.scalar
                    def _(act):
                        def s_copy(c):
                            act.wait_ge(s_mm, c + 1)
                            if c >= 2:
                                act.wait_ge(s_used, c - 1)
                            nc.scalar.activation(s_sb[:, c % 2], ps[:, 2 + c % 2, 0:n].rearrange("p (a k) -> p a k", a=nt),
                                                 ACT.Copy).then_inc(s_ev, 1)
                        for c in range(HP):
                            act.wait_ge(q_mm, c + 1)
                            if c >= 2:
                                act.wait_ge(s_mm, c - 1)
                            nc.scalar.activation(qT[:, c % 2, :], ps[:, c % 2, 0:n], ACT.Copy).then_inc(q_ev, 1)
                            if c:
                                s_copy(c - 1)
                        s_copy(HP - 1)
                        for t in range(nt):
                            act.wait_ge(b_done, t + 1)
                            nc.scalar.activation(best[:], best[:], ACT.Exp).then_inc(x_done, 1)

                    @block.vector
                    def _(dve):
                        def step(ins):
                            dve_chain(dve, ins)

                        def top16(vals, ids, src, tmp):
                            step(nc.vector.max(vals[:, 0:8], src))
                            nc.vector.max_index(ids[:, 0:8], vals[:, 0:8], src)
                            step(nc.vector.match_replace(tmp, vals[:, 0:8], src, NEG))
                            step(nc.vector.max(vals[:, 8:16], tmp))
                            return nc.vector.max_index(ids[:, 8:16], vals[:, 8:16], tmp)

                        for c in range(HP):
                            dve.wait_ge(s_ev, c + 1)
                            for t in range(nt):
                                last = top16(top[:, t, c], idx[:, t, c], s_sb[:, c % 2, t], s2[:, 0:NKEY])
                            last.then_inc(s_used, 1)
                        dve.wait_ge(s_used, HP)
                        step(nc.vector.tensor_copy(idf[:], idx[:]))
                        for t in range(nt):
                            a = top[:, t].rearrange("p (h two) k -> p h two k", two=2)
                            f = idf[:, t].rearrange("p (h two) k -> p h two k", two=2)
                            step(nc.vector.tensor_tensor(cand[:], bc(a[:, :, 0], 3, TOPK), bc(a[:, :, 1], 2, TOPK), ALU.add))
                            for h in range(PH):
                                last = top16(best[:, h], sel[:, h], cand[:, h].rearrange("p a b -> p (a b)"), s2[:])
                            step(last)
                            nc.vector.tensor_copy(esum[:], best[:, :, 0])
                            step(nc.vector.tensor_copy(s2[:, 0:PH], best[:, :, 0]))
                            nc.vector.tensor_tensor(best[:], best[:], bc(s2[:, 0:PH], 2, TOPK), ALU.subtract).then_inc(b_done, 1)
                            flat = sel[:].rearrange("p h k -> p (h k)")
                            nc.vector.tensor_scalar(sela[:, 0], flat, 4, None, ALU.logical_shift_right)
                            step(nc.vector.tensor_scalar(sela[:, 1], flat, 15, None, ALU.bitwise_and))
                            step(nc.vector.tensor_copy(self_[:], sela[:]))
                            r = t % 2
                            for j in range(2):
                                step(nc.vector.tensor_tensor(eq[:], bc(self_[:, j], 2, TOPK), bc(iota[:, 0:TOPK], 1, PH * TOPK), ALU.is_equal))
                                e4 = eq[:].rearrange("p (h k) a -> p h k a", h=PH)
                                step(nc.vector.tensor_tensor(e4, e4, bc(f[:, :, j], 2, TOPK), ALU.mult))
                                step(nc.vector.tensor_reduce(ijg[:, r, j], eq[:], AX, ALU.add))
                            dve.wait_ge(x_done, t + 1)
                            step(nc.vector.tensor_reduce(esum[:], best[:], AX, ALU.add))
                            step(nc.vector.reciprocal(esum[:], esum[:]))
                            g3 = ijg[:, r, 2].rearrange("p (h k) -> p h k", h=PH)
                            nc.vector.tensor_tensor(g3, best[:], bc(esum[:], 2, TOPK), ALU.mult).then_inc(tr_in, 1)
                            dve.wait_ge(tr_mm, t + 1)
                            cols = slice(t * P, (t + 1) * P)
                            nc.vector.tensor_copy(iT[:, cols], ps[:, 4, 0:P])
                            nc.vector.tensor_copy(jT[:, cols], ps[:, 4, P:2 * P])
                            step(nc.vector.tensor_copy(gT[:], ps[:, 4, 2 * P:3 * P]))
                            step(nc.vector.tensor_copy(gp[:, cols, 0], gT[:]))
                            for j in range(2):
                                step(nc.vector.tensor_tensor(gT[:], gT[:], gp[:, cols, j], ALU.subtract))
                                last = nc.vector.tensor_copy(gp[:, cols, j + 1], gT[:])
                                step(last)
                            nc.vector.tensor_copy(esum[:], ps[:, 4, 0:PH]).then_inc(tr_ev, 1)

        def phase_peer(l, lo, h2, iT, jT, gp):
            n = T - lo
            NI = 16 * T // n
            NPASS = NKEY // NI
            UT = 8 * n // 256 if n == T else 8
            PB = UT // 2
            NUNIT = n // UT
            UPS = NUNIT // NI
            ITE = 2 * GE
            NIT = NKEY // ITE
            IPP = NI // ITE
            u_in = [sem(f"peer_u_in{l}_{r}") for r in range(2)]
            v_in = [sem(f"peer_v_in{l}_{r}") for r in range(2)]
            (act_mm, gelu_done, w_done, out_mm, x_done, hot0_done, hot_done, hotb_done, g_mm, g_ev) = (
                sem(f"peer_{x}{l}") for x in ("act_mm", "gelu_done", "w_done", "out_mm", "x_done", "hot0_done",
                                              "hot_done", "hotb_done", "g_mm", "g_ev"))
            with ExitStack() as st:
                us = sb(st, f"peer_u{l}", [P, 2, DC, GE * P])
                vs = sb(st, f"peer_v{l}", [P, 2, GE, D_MODEL])
                gd = sb(st, f"peer_g{l}", [P, 2 * NI, n])
                wv = sb(st, f"peer_w{l}", [P, 2, GE, n])
                ga = sb(st, f"peer_act{l}", [P, 2, n])
                hot = sb(st, f"peer_hot{l}", [P, 2, UT, NI], BF16)
                hotg = sb(st, f"peer_hotg{l}", [P, 2, UT, 3, NI], BF16)
                hotj = sb(st, f"peer_hotj{l}", [P, 2, UT, P], BF16)

                def unit_hot(dve, u, r, p, t0):
                    it_ = iT[:, bass.ds(t0, UT)]
                    if not (isinstance(u, int) and u < 2):
                        dve.wait_ge(g_mm, u - 1)
                    nc.vector.tensor_tensor(hotj[:, r], bc(jT[:, bass.ds(t0, UT)], 2, P), bc(iotab[:], 1, UT),
                                            ALU.is_equal).then_inc(hotb_done, 1)
                    nc.vector.tensor_tensor(hot[:, r], bc(it_, 2, NI), bc(iotab[:, bass.ds(p * NI, NI)], 1, UT),
                                            ALU.is_equal).then_inc(hot0_done, 1)
                    dve.wait_ge(hot0_done, u + 1)
                    nc.vector.tensor_tensor(hotg[:, r], bc(hot[:, r], 2, 3), bc(gp[:, bass.ds(t0, UT), :], 3, NI),
                                            ALU.mult).then_inc(hot_done, 1)

                def unit_mm(pe, u, r):
                    pe.wait_ge(hot_done, u + 1)
                    pe.wait_ge(hotb_done, u + 1)
                    if not (isinstance(u, int) and u < 2):
                        pe.wait_ge(g_ev, 2 * (u - 1))
                    for t in range(UT):
                        o = (t % PB) * 3 * NI
                        mm = nc.tensor.matmul(ps[:, 4 + 2 * r + t // PB, o:o + 3 * NI], hotj[:, r, t, :],
                                              hotg[:, r, t].rearrange("p a i -> p (a i)"), start=True, stop=True)
                    mm.then_inc(g_mm, 1)

                def unit_ev(dve, u, r, slot, t0):
                    dve.wait_ge(g_mm, u + 1)
                    for b in range(2):
                        got = ps[:, 4 + 2 * r + b, 0:PB * 3 * NI].rearrange("p (t a i) -> p t i a", a=3, i=NI)
                        rows = slice(slot, slot + NI) if isinstance(slot, int) else bass.ds(slot, NI)
                        dst = gd[:, rows, bass.ds(t0 + b * PB, PB)].rearrange("p i t -> p t i")
                        nc.vector.tensor_reduce(dst, got, AX, ALU.add).then_inc(g_ev, 1)

                with nc.Block() as block:
                    @block.sync
                    def _(sp):
                        def load(g, r, first):
                            if not first:
                                sp.wait_ge(act_mm, GE * (g - 1))
                            sp.dma_start(us[:, r], d["uT"][l, bass.ds(g, 1)].rearrange("a p k e -> p (a k) e")).then_inc(u_in[r], 16)
                            if not first:
                                sp.wait_ge(out_mm, DC * (g - 1))
                            sp.dma_start(vs[:, r], d["v"][l, bass.ds(g, 1)].rearrange("a p j n -> p (a j) n")).then_inc(v_in[r], 16)
                        load(0, 0, True)
                        load(1, 1, True)
                        with sp.Fori(1, NG // 2) as i:
                            load(2 * i, 0, False)
                            load(2 * i + 1, 1, False)

                    @block.tensor
                    def _(pe):
                        unit_mm(pe, 0, 0)
                        unit_mm(pe, 1, 1)
                        with pe.Fori(1, NUNIT // 2) as i:
                            unit_mm(pe, 2 * i, 0)
                            unit_mm(pe, 2 * i + 1, 1)

                        def body(it, first, build):
                            for e in range(ITE):
                                g, jj, r = e // GE, e % GE, (e // GE) % 2
                                eg = ITE * it + e
                                if build:
                                    for q in range(UPS):
                                        w = e * UPS + q
                                        unit_mm(pe, NUNIT + ITE * UPS * it + w, w % 2)
                                if jj == 0:
                                    pe.wait_ge(u_in[r], 16 * (it + 1))
                                if not (first and e < 2):
                                    pe.wait_ge(gelu_done, eg - 1)
                                for k in range(DC):
                                    mm = nc.tensor.matmul(ps[:, e % 2, 0:n], us[:, r, k, jj * P:(jj + 1) * P], h2[:, k, lo:T],
                                                          start=(k == 0), stop=(k == DC - 1))
                                mm.then_inc(act_mm, 1)
                                if not (first and g == 0):
                                    out_chunks(2 * it + g - 1, 1 - r, it + g, jj, first and g == 1)

                        def out_chunks(g, r, loads, jj, first):
                            if jj == 0:
                                pe.wait_ge(w_done, GE * (g + 1))
                                pe.wait_ge(v_in[r], 16 * loads)
                            for c in (2 * jj, 2 * jj + 1):
                                if not (first and c < 2):
                                    pe.wait_ge(x_done, DC * g + c - 1)
                                for j in range(GE):
                                    mm = nc.tensor.matmul(ps[:, 2 + c % 2, 0:n], vs[:, r, j, c * P:(c + 1) * P], wv[:, r, j, :],
                                                          start=(j == 0), stop=(j == GE - 1))
                                mm.then_inc(out_mm, 1)

                        body(0, True, True)
                        with pe.Fori(1, NIT - IPP) as it:
                            body(it, False, True)
                        with pe.Fori(NIT - IPP, NIT) as it:
                            body(it, False, False)
                        for jj in range(GE):
                            out_chunks(NG - 1, 1, NG // 2, jj, False)

                    @block.scalar
                    def _(act):
                        def gelu(e, r, first):
                            act.wait_ge(act_mm, e + 1)
                            if not first:
                                act.wait_ge(w_done, e - 1)
                            nc.scalar.activation(ga[:, r], ps[:, r, 0:n], ACT.Gelu_apprx_tanh).then_inc(gelu_done, 1)
                        gelu(0, 0, True)
                        gelu(1, 1, True)
                        with act.Fori(1, NKEY // 2) as i:
                            gelu(2 * i, 0, False)
                            gelu(2 * i + 1, 1, False)

                    @block.vector
                    def _(dve):
                        unit_hot(dve, 0, 0, 0, 0)
                        unit_hot(dve, 1, 1, 0, UT)
                        unit_ev(dve, 0, 0, 0, 0)
                        with dve.Fori(0, NUNIT // 2 - 1) as i:
                            unit_hot(dve, 2 * i + 2, 0, 0, (2 * i + 2) * UT)
                            unit_ev(dve, 2 * i + 1, 1, 0, (2 * i + 1) * UT)
                            unit_hot(dve, 2 * i + 3, 1, 0, (2 * i + 3) * UT)
                            unit_ev(dve, 2 * i + 2, 0, 0, (2 * i + 2) * UT)
                        unit_ev(dve, NUNIT - 1, 1, 0, (NUNIT - 1) * UT)

                        def body(p, s, first, build):
                            it = IPP * p + s
                            own = ((p % 2) * NI)
                            nxt = (((p + 1) % 2) * NI)
                            for e in range(ITE):
                                g, jj, r = e // GE, e % GE, (e // GE) % 2
                                eg = ITE * it + e
                                units = [e * UPS + q for q in range(UPS)] if build else []
                                for w in units:
                                    t0 = (ITE * UPS * s + w) * UT
                                    unit_hot(dve, NUNIT + ITE * UPS * it + w, w % 2, p + 1, t0)
                                if e == 0:
                                    dve.wait_ge(g_ev, 2 * NUNIT * (p + 1))
                                if jj == 0 and not first:
                                    dve.wait_ge(out_mm, DC * (2 * it + g - 1))
                                dve.wait_ge(gelu_done, eg + 1)
                                row = gd[:, bass.ds(own + ITE * s + e, 1), :].rearrange("p a t -> p (a t)")
                                nc.vector.tensor_tensor(wv[:, r, jj], ga[:, e % 2], row, ALU.mult).then_inc(w_done, 1)
                                for w in units:
                                    t0 = (ITE * UPS * s + w) * UT
                                    unit_ev(dve, NUNIT + ITE * UPS * it + w, w % 2, nxt, t0)
                                if not (first and g == 0):
                                    add_out(2 * it + g - 1, jj, first and g == 1)

                        def add_out(g, jj, first):
                            for c in (2 * jj, 2 * jj + 1):
                                dve.wait_ge(out_mm, DC * g + c + 1)
                                if jj == 0 and c == 0 and not first:
                                    dve.wait_ge(x_done, DC * g)
                                add_gated(c, 5, ps[:, 2 + c % 2, :], lo).then_inc(x_done, 1)

                        for s in range(IPP):
                            body(0, s, s == 0, True)
                        with dve.Fori(1, NPASS - 1) as p:
                            for s in range(IPP):
                                body(p, s, False, True)
                        for s in range(IPP):
                            body(NPASS - 1, s, False, False)
                        for jj in range(GE):
                            add_out(NG - 1, jj, False)

        phase_start()
        for l in range(DEPTH):
            last_layer = l == DEPTH - 1
            lo = CTX if last_layer else 0
            phase_ada(l)
            with ExitStack() as st:
                mix = sb(st, f"mix{l}", [P, DC, T])
                with ExitStack() as st1:
                    fm = sb(st1, f"fm{l}", [P, FM, T])
                    tm = sb(st1, f"tm{l}", [P, TT, TMC])
                    phase_norm(f"norm_mix{l}", d["norm_mix_g"][l], 0, 0, mix)
                    phase_proj(l, mix, fm, tm)
                    with ExitStack() as st2:
                        hk = sb(st2, f"hk{l}", [P, 4, T])
                        cum = sb(st2, f"cum{l}", [P, 6, TT, P + 1])
                        phase_gates(l, fm, hk, cum)
                        phase_scan(l, fm, tm, hk, cum, mix)
                    phase_attn(l, fm, tm, mix)
                    phase_post(l, fm, mix)
                phase_out(l, lo, mix)
            with ExitStack() as st:
                h2 = sb(st, f"h2{l}", [P, DC, T])
                iT = sb(st, f"iT{l}", [P, T - lo], BF16)
                jT = sb(st, f"jT{l}", [P, T - lo], BF16)
                gp = sb(st, f"gp{l}", [P, T - lo, 3], BF16)
                phase_norm(f"norm_ffn{l}", d["norm_ffn_g"][l], 3, lo, h2)
                phase_route(l, lo, h2, iT, jT, gp)
                phase_peer(l, lo, h2, iT, jT, gp)
            clear_layer_sems()
        with ExitStack() as st:
            y = sb(st, "y", [P, DC, T])
            phase_norm("norm_final", d["final_norm_g"], None, CTX, y)
            stored = sem("stored")
            with nc.Block() as block:
                @block.sync
                def _(sp):
                    sp.dma_start(out, y[:, :, CTX:T]).then_inc(stored, 16)
                    sp.wait_ge(stored, 16)


def constants():
    c = {}
    c["ident"] = np.eye(P, dtype=np.float32)
    c["iota"] = np.tile(np.arange(P, dtype=np.float32), (P, 1))
    c["mean64"] = np.kron(np.eye(2), np.full((64, 64), 1.0 / 64)).astype(np.float32)
    f = np.arange(P)
    partner = (f // 16) * 16 + (f + 8) % 16
    rotp = np.zeros((P, P), np.float32)
    rotp[partner, f] = 1.0
    c["rotp"] = rotp
    freqs = np.float32(ROPE_BASE) ** (-np.arange(8, dtype=np.float32) / np.float32(8))
    n = np.arange(SEQ)
    pos = np.stack([n // GRID_W, n % GRID_W]).astype(np.float32)
    ang = (pos[(f // 16) % 2] * freqs[f % 8][:, None]).astype(np.float32)
    c["cosT"] = np.cos(ang).astype(np.float32)
    c["sinT"] = (np.sin(ang) * np.where(f % 16 < 8, -1.0, 1.0)[:, None]).astype(np.float32)
    mask = np.zeros((P, 2 * NL, HALF), np.int32)
    s = np.arange(P)[:, None]
    for dr in range(2):
        for i, L in enumerate(LEVELS):
            j = np.arange(HALF)[None, :]
            mask[:, NL * dr + i] = (s // (2 * L) == j // L) & ((s // L) % 2 == dr)
    c["mask"] = mask
    c["maskd"] = np.eye(P, dtype=np.int32)
    return c


def lay_out(x, c, ctx, c_ctx, ada_w, ada_b, norm_mix_g, norm_ffn_g, w_in, w_out,
            gla_gate_w, gla_gate_b, gla_norm_g, hgrn_lb_raw, hgrn_norm_g,
            mla_q_norm_g, mla_kv_norm_g, mla_w_uq, mla_w_ukv, diff_lambda, diff_norm_g,
            peer_wq, peer_keys, peer_u, peer_v, final_norm_g):
    a = constants()
    cols = lambda v: np.swapaxes(v.reshape(*v.shape[:-1], -1, P), -1, -2)
    tokens = np.concatenate([ctx[0], x[0]], axis=0)
    a["xT"] = tokens.T.reshape(DC, P, T).transpose(1, 0, 2)
    a["cvec"] = np.stack([c[0], c_ctx], axis=-1).reshape(DC, P, 2).transpose(1, 0, 2)
    a["ada_w"], a["ada_b"] = ada_w, cols(ada_b)
    a["norm_mix_g"], a["norm_ffn_g"], a["final_norm_g"] = cols(norm_mix_g), cols(norm_ffn_g), cols(final_norm_g)
    g, h, m, f = 0, 800, 2080, 2432
    fm_cols = [(g + 512, 256), (h + 512, 256), (h, 256), (g, 128), (g + 128, 128), (h + 768, 512),
               (m, 192), (m + 320, 32), (g + 768, 32), (m + 192, 128), (f, 512)]
    tm_cols = [(g + 256, 256), (h + 256, 256), (f + 512, 256)]
    w = np.concatenate([w_in[:, :, o:o + n] for o, n in fm_cols], axis=-1)
    a["w_fm"] = w.reshape(DEPTH, DC, P, FM, P).transpose(0, 3, 2, 1, 4)
    w = np.concatenate([w_in[:, :, o:o + n] for o, n in tm_cols], axis=-1)
    a["w_tm"] = w.reshape(DEPTH, DC, P, TMC).transpose(0, 2, 1, 3)
    a["w_out"] = w_out.reshape(DEPTH, DC, P, DC, P).transpose(0, 3, 2, 1, 4)
    zero = np.zeros_like(gla_gate_w[:, 0])
    a["gate_w"] = np.concatenate([np.stack([gla_gate_w[:, 0], zero], axis=2),
                                  np.stack([zero, gla_gate_w[:, 1]], axis=2)], axis=1)
    a["gate_b"] = gla_gate_b.transpose(0, 2, 1)
    a["lb_raw"] = cols(hgrn_lb_raw).transpose(1, 0, 2)
    a["g_head"] = np.stack([np.tile(v, (1, 2)) for v in (gla_norm_g, hgrn_norm_g, diff_norm_g)], axis=-1)
    a["g_q0"], a["g_q1"] = mla_q_norm_g[:, 0:P, None], mla_q_norm_g[:, P:, None]
    a["g_kv"] = mla_kv_norm_g[:, :, None]
    a["w_uq"] = mla_w_uq.reshape(DEPTH, MLA_Q, HEADS, MLA_DQ)
    a["w_ukv"] = mla_w_ukv.reshape(DEPTH, MLA_KV, HEADS, P)
    a["lam"] = diff_lambda
    a["w_pq"] = peer_wq.reshape(DEPTH, DC, P, 2 * PH, P).transpose(0, 3, 2, 1, 4)
    a["keysT"] = peer_keys.reshape(DEPTH, 2 * PH, NKEY, P).transpose(0, 3, 1, 2)
    a["uT"] = peer_u.reshape(DEPTH, NG, GE * P, DC, P).transpose(0, 1, 4, 3, 2)
    a["v"] = peer_v.reshape(DEPTH, NG, GE, P, D_MODEL).transpose(0, 1, 3, 2, 4)
    return a


def kernel(**inputs):
    import concourse.bacc as _bacc
    from concourse.bass_utils import run_bass_kernel_spmd as _run

    nc = _bacc.Bacc("TRN2", target_bir_lowering=False, num_devices=1)
    arrays, d = {}, {}
    for name, a in lay_out(**{k: np.asarray(v) for k, v in inputs.items()}).items():
        a = np.ascontiguousarray(a)
        arrays[f"in_{name}"] = a
        d[name] = nc.dram_tensor(f"in_{name}", a.shape, mybir.dt.from_np(a.dtype), kind="ExternalInput").ap()
    out = nc.dram_tensor("out_yT", (P, DC, SEQ), F32, kind="ExternalOutput").ap()
    build(nc, d, out)
    r = _run(nc, [arrays], core_ids=[0])
    y = r.results[0]["out_yT"]
    return y.transpose(2, 1, 0).reshape(1, SEQ, D_MODEL)
```

```python
from contextlib import ExitStack
import math

import numpy as np

import concourse.bass as bass
from concourse import mybir

F32 = mybir.dt.float32
F32R = mybir.dt.float32r
U32 = mybir.dt.uint32
I32 = mybir.dt.int32
ALU = mybir.AluOpType
ACT = mybir.ActivationFunctionType
AX = mybir.AxisListType.X

P = 128
BANK = 512
EPS = 1e-6
D_MODEL = 1024
DC = D_MODEL // P
CTX = 256
SEQ = 256
T = CTX + SEQ
TT = T // P
DEPTH = 2
GRID_W = 64
ROPE_BASE = 10000.0

GLA_HEADS, GLA_DK = 4, 32
GLA_GATE_NORM = 16.0
HG_CHUNKS = 2
LB_FLOOR = 1e-30
DV = 64
HEADS = 4
MLA_Q, MLA_KV, MLA_NOPE, MLA_ROPE = 192, 128, 64, 32
MLA_DQ = MLA_NOPE + MLA_ROPE
DIFF_DQK = 32

GATE0 = 0
HQ = 4
GQ, GK = 6, 7
HZ = 8
CQ0, CQ1, CKV = 12, 13, 14
DQ, DK = 15, 17
FM = 19
SILU_CHUNKS = 6
TMC = 3 * HEADS * DV
KR0, GZ0 = 64, 96

LEVELS = [64, 32, 16, 8, 4, 2, 1]
NL = len(LEVELS)
HALF = P // 2
UNITS = [((0, 0), (0, 1)), ((0, 2), (0, 3)), ((0, 4), (0, 5)), ((0, 6), (1, 6)),
         ((1, 0), (1, 1)), ((1, 2), (1, 3)), ((1, 4), (1, 5)), None]
NU = len(UNITS)
XQ_TILES = [(1, 3, 2, 3), (0, 2, 2, 3)]
XK_TILES = [(0, 2, 0, 1), (1, 3, 0, 1)]

PH = 8
NKEY = 128
TOPK = 16
GE = 2
NG = NKEY // GE
GROWS = 4
TB = 32
NEG = -3.0e38
SMALL = 2.0 ** -40
UP = 2.0 ** 60


class Chain:

    def __init__(self, sem):
        self.sem, self.n = sem, 0

    def __call__(self, eng, ins):
        self.n += 1
        ins.then_inc(self.sem, 1)
        eng.wait_ge(self.sem, self.n)


def f32(ap):
    return ap.bitcast(F32)


def product(nc, out, w, x, start, stop):
    nc.tensor.matmul(out, w[0], x[0], start=start, stop=False)
    nc.tensor.matmul(out, w[0], x[1], start=False, stop=False)
    return nc.tensor.matmul(out, w[1], x[0], start=False, stop=stop)


def bc(ap, axis, n):
    ap = ap.unsqueeze(axis)
    shape = list(ap.shape)
    shape[axis] = n
    return ap.to_broadcast(shape)


def halves(ap, L, side):
    return ap.rearrange("p a (n two l) -> p a n two l", two=2, l=L)[:, :, :, side, :]


def mids(ap, L):
    ap = halves(ap, L, 1)[:, :, :, 0:1]
    return ap.to_broadcast([P, ap.shape[1], HALF // L, L])


def build(nc, d, out):
    ctx = ExitStack()

    layer_sems = []

    def sem(name):
        layer_sems.append(nc.alloc_semaphore(name=name))
        return layer_sems[-1]

    def clear_layer_sems():
        nc.clear_and_free_semaphores(layer_sems)
        layer_sems.clear()
        nc.all_engine_barrier()

    def sb(st, name, shape, dt=F32):
        return st.enter_context(nc.sbuf_tensor(name, shape, dt))

    with ctx:
        ps = ctx.enter_context(nc.psum_tensor("ps", [P, 8, BANK], F32))
        xT = sb(ctx, "xT", [P, DC, T])
        mod = sb(ctx, "mod", [P, 6 * DC, 2])
        ident = sb(ctx, "ident", [P, P])
        ones = sb(ctx, "ones", [P, P])
        meanD = sb(ctx, "meanD", [P, P])
        mean64 = sb(ctx, "mean64", [P, P])
        rotp = sb(ctx, "rotp", [P, P])
        cosT = sb(ctx, "cosT", [P, SEQ])
        sinT = sb(ctx, "sinT", [P, SEQ])
        mask = sb(ctx, "mask", [P, 2 * NL, HALF], I32)
        maskd = sb(ctx, "maskd", [P, P], I32)
        iota = sb(ctx, "iota", [P, P])
        gates_dram = nc.dram_tensor("peer_gates", (T // TB, P, NKEY, TB), F32, kind="Internal").ap()
        cvec = sb(ctx, "cvec", [P, DC, 2])
        silu_c = sb(ctx, "silu_c", [P, DC, 2])
        onecol = sb(ctx, "onecol", [P, 1])
        epscol = sb(ctx, "epscol", [P, 1])
        dve_chain = Chain(ctx.enter_context(nc.semaphore("dve_chain")))

        def phase_start():
            loaded = sem("consts_loaded")
            c_in = sem("c_in")
            const = [(xT, d["xT"]), (ident, d["ident"]), (mean64, d["mean64"]), (rotp, d["rotp"]),
                     (cosT, d["cosT"]), (sinT, d["sinT"]), (mask, d["mask"]), (maskd, d["maskd"]), (iota, d["iota"])]
            with nc.Block() as block:
                @block.sync
                def _(sp):
                    sp.dma_start(cvec[:], d["cvec"]).then_inc(c_in, 16)
                    for dst, src in const:
                        sp.dma_start(dst[:], src).then_inc(loaded, 16)
                    sp.wait_ge(loaded, 16 * len(const))

                @block.vector
                def _(dve):
                    nc.vector.memset(ones[:], 1.0)
                    nc.vector.memset(meanD[:], 1.0 / D_MODEL)
                    nc.vector.memset(onecol[:], 1.0)
                    nc.vector.memset(epscol[:], EPS)

                @block.scalar
                def _(act):
                    act.wait_ge(c_in, 16)
                    nc.scalar.activation(silu_c[:], cvec[:], ACT.Silu)

        def phase_ada(l):
            slab_in = [sem(f"ada_in{l}_{r}") for r in range(2)]
            bias_in = sem(f"ada_b_in{l}")
            row_mm, row_ev, col_mm = sem(f"ada_row{l}"), sem(f"ada_row_ev{l}"), sem(f"ada_col{l}")
            NR = 6 * D_MODEL // BANK
            with ExitStack() as st:
                slab = sb(st, f"ada_slab{l}", [P, 2, DC, D_MODEL])
                bias = sb(st, f"ada_bias{l}", [P, 6 * DC])
                row = sb(st, f"ada_rowv{l}", [2, NR, BANK])
                with nc.Block() as block:
                    @block.sync
                    def _(sp):
                        sp.dma_start(bias[:], d["ada_b"][l]).then_inc(bias_in, 16)
                        for m in range(6):
                            if m >= 2:
                                sp.wait_ge(row_mm, 2 * (m - 1))
                            src = d["ada_w"][l, :, m * D_MODEL:(m + 1) * D_MODEL].rearrange("(k p) n -> p k n", p=P)
                            sp.dma_start(slab[:, m % 2], src).then_inc(slab_in[m % 2], 16)

                    @block.tensor
                    def _(pe):
                        def columns(n):
                            pe.wait_ge(row_ev, n + 1)
                            for j in range(4):
                                o = 2 * (4 * n + j)
                                mm = nc.tensor.transpose(ps[:, 4, o:o + 2], row[0:2, n, j * P:(j + 1) * P], ident[0:2, 0:2])
                            mm.then_inc(col_mm, 1)

                        for n in range(NR):
                            m, h = n // 2, n % 2
                            pe.wait_ge(slab_in[m % 2], 16 * (m // 2 + 1))
                            if n >= 4:
                                pe.wait_ge(row_ev, n - 3)
                            for k in range(DC):
                                mm = nc.tensor.matmul(ps[0:2, n % 4, :], silu_c[:, k, :], slab[:, m % 2, k, h * BANK:(h + 1) * BANK],
                                                      start=(k == 0), stop=(k == DC - 1))
                            mm.then_inc(row_mm, 1)
                            if n:
                                columns(n - 1)
                        columns(NR - 1)

                    @block.scalar
                    def _(act):
                        for n in range(NR):
                            act.wait_ge(row_mm, n + 1)
                            nc.scalar.activation(row[0:2, n, :], ps[0:2, n % 4, :], ACT.Copy).then_inc(row_ev, 1)

                    @block.vector
                    def _(dve):
                        dve.wait_ge(bias_in, 16)
                        dve.wait_ge(col_mm, NR)
                        got = ps[:, 4, 0:12 * DC].rearrange("p (n v) -> p n v", v=2)
                        nc.vector.tensor_tensor(mod[:], got, bc(bias[:], 2, 2), ALU.add)

        def phase_norm(name, gain, which, lo, dst, parts=None):
            n = T - lo
            g_in, sq_done, sum_done, scaled = (sem(f"{name}_{x}") for x in ("g_in", "sq_done", "sum_done", "scaled"))
            a_done, root_done, full_done = (sem(f"{name}_{x}") for x in ("a_done", "root_done", "full_done"))
            plo = T - parts[0].shape[2] if parts else 0
            with ExitStack() as st:
                g = sb(st, f"{name}_g", [P, DC])
                amp = sb(st, f"{name}_amp", [P, DC, 2])
                rstd = sb(st, f"{name}_rstd", [P, T])
                with nc.Block() as block:
                    @block.sync
                    def _(sp):
                        sp.dma_start(g[:], gain).then_inc(g_in, 16)

                    @block.scalar
                    def _(act):
                        for k in range(DC):
                            nc.scalar.activation(dst[:, k, lo:T], xT[:, k, lo:T], ACT.Square).then_inc(sq_done, 1)
                        act.wait_ge(sum_done, 1)
                        nc.scalar.activation(rstd[:, lo:T], ps[:, 0, 0:n], ACT.Sqrt, bias=epscol[:]).then_inc(root_done, 1)
                        if which is None:
                            return
                        act.wait_ge(a_done, 1)
                        for k in range(DC):
                            act.wait_ge(scaled, k // 2 + 1)
                            for v, (a, b) in enumerate(((lo, CTX), (max(lo, CTX), T))):
                                if a < b:
                                    w = 1 - v
                                    nc.scalar.activation(parts[0][:, k, a - plo:b - plo], dst[:, k, a:b], ACT.Identity,
                                                         bias=mod[:, which * DC + k, w:w + 1], scale=amp[:, k, w:w + 1])
                                    full = nc.scalar.activation(dst[:, k, a:b], dst[:, k, a:b], ACT.Identity,
                                                                bias=mod[:, which * DC + k, w:w + 1], scale=amp[:, k, w:w + 1])
                            full.then_inc(full_done, 1)

                    @block.tensor
                    def _(pe):
                        for k in range(DC):
                            pe.wait_ge(sq_done, k + 1)
                            mm = nc.tensor.matmul(ps[:, 0, 0:n], meanD[:], dst[:, k, lo:T],
                                                  start=(k == 0), stop=(k == DC - 1))
                        mm.then_inc(sum_done, 1)

                    @block.vector
                    def _(dve):
                        dve.wait_ge(g_in, 16)
                        if which is not None:
                            dve_chain(dve, nc.vector.tensor_scalar(
                                amp[:], mod[:, (which + 1) * DC:(which + 2) * DC, :], 1.0, None, ALU.add))
                            nc.vector.tensor_tensor(amp[:], amp[:], bc(g[:], 2, 2), ALU.mult).then_inc(a_done, 1)
                        dve.wait_ge(root_done, 1)
                        dve_chain(dve, nc.vector.reciprocal(rstd[:, lo:T], rstd[:, lo:T]))
                        if which is None:
                            for k in range(DC):
                                nc.vector.scalar_tensor_tensor(out=dst[:, k, lo:T], in0=xT[:, k, lo:T], scalar=g[:, k:k + 1],
                                                               in1=rstd[:, lo:T], op0=ALU.mult, op1=ALU.mult)
                            return
                        for k in range(0, DC, 2):
                            nc.vector.tensor_tensor(dst[:, k:k + 2, lo:T], xT[:, k:k + 2, lo:T],
                                                    bc(rstd[:, lo:T], 1, 2), ALU.mult).then_inc(scaled, 1)
                        for k in range(DC):
                            dve.wait_ge(full_done, k + 1)
                            hi = parts[0][:, k, lo - plo:T - plo]
                            nc.vector.tensor_tensor(parts[1][:, k, lo - plo:T - plo], dst[:, k, lo:T], f32(hi), ALU.subtract)

        def phase_proj(l, lo, hp, fm, tm):
            RW = 4
            NT = 2 * TT
            w_in = [sem(f"proj_w_in{l}_{r}") for r in range(RW)]
            t_in = [sem(f"projt_w_in{l}_{r}") for r in range(2)]
            hi_done, lo_done, mm_done, ev_done, thi_done, tlo_done, tmm_done, tend = (
                sem(f"proj_{x}{l}") for x in ("hi", "lo", "mm", "ev", "thi", "tlo", "tmm", "tend"))
            own = [lo if c in (0, 1, 2, 3, HQ, HQ + 1, GQ, CQ0, DQ, DQ + 1) else 0 for c in range(FM)]
            with ExitStack() as st:
                slab = sb(st, f"proj_slab{l}", [P, RW, DC, P])
                wh = sb(st, f"proj_wh{l}", [P, 2, DC, P], F32R)
                wl = sb(st, f"proj_wl{l}", [P, 2, DC, P], F32R)
                tslab = sb(st, f"proj_tslab{l}", [P, 2, TMC])
                th = sb(st, f"proj_th{l}", [P, 2, TMC], F32R)
                tl = sb(st, f"proj_tl{l}", [P, 2, TMC], F32R)
                with nc.Block() as block:
                    @block.sync
                    def _(sp):
                        for c in range(FM):
                            if c >= RW:
                                sp.wait_ge(lo_done, c - RW + 1)
                            sp.dma_start(slab[:, c % RW], d["w_fm"][l, c]).then_inc(w_in[c % RW], 16)
                        for k in range(DC):
                            if k >= 2:
                                sp.wait_ge(tlo_done, k - 1)
                            sp.dma_start(tslab[:, k % 2], d["w_tm"][l, :, k, :]).then_inc(t_in[k % 2], 16)

                    @block.tensor
                    def _(pe):
                        for c in range(FM):
                            pe.wait_ge(lo_done, c + 1)
                            if c >= 4:
                                pe.wait_ge(ev_done, c - 3)
                            a = own[c]
                            for k in range(DC):
                                mm = product(nc, ps[:, c % 4, 0:T - a], (wh[:, c % 2, k, :], wl[:, c % 2, k, :]),
                                             (hp[0][:, k, a:T], hp[1][:, k, a:T]), k == 0, k == DC - 1)
                            mm.then_inc(mm_done, 1)
                        pe.wait_ge(ev_done, FM)
                        for k in range(DC):
                            pe.wait_ge(tlo_done, k + 1)
                            for n in range(NT):
                                cols = slice((n % 2) * TMC // 2, (n % 2 + 1) * TMC // 2)
                                t = slice((n // 2) * P, (n // 2 + 1) * P)
                                mm = product(nc, ps[:, n, 0:TMC // 2], (hp[0][:, k, t], hp[1][:, k, t]),
                                             (th[:, k % 2, cols], tl[:, k % 2, cols]), k == 0, k == DC - 1)
                                if k == DC - 1:
                                    mm.then_inc(tend, 1)
                            if k < DC - 1:
                                mm.then_inc(tmm_done, 1)

                    @block.scalar
                    def _(act):
                        def evac(c):
                            act.wait_ge(mm_done, c + 1)
                            a = own[c]
                            nc.scalar.activation(fm[:, c, a:T], ps[:, c % 4, 0:T - a], ACT.Silu if c < SILU_CHUNKS else ACT.Copy,
                                                 scale=GLA_DK ** -0.5 if c == GQ else 1.0).then_inc(ev_done, 1)
                        for c in range(FM):
                            act.wait_ge(w_in[c % RW], 16 * (c // RW + 1))
                            if c >= 2:
                                act.wait_ge(mm_done, c - 1)
                            nc.scalar.activation(wh[:, c % 2], slab[:, c % RW], ACT.Copy).then_inc(hi_done, 1)
                            if c:
                                evac(c - 1)
                        evac(FM - 1)
                        for k in range(DC):
                            act.wait_ge(t_in[k % 2], 16 * (k // 2 + 1))
                            if k >= 2:
                                act.wait_ge(tmm_done, k - 1)
                            nc.scalar.activation(th[:, k % 2], tslab[:, k % 2], ACT.Copy).then_inc(thi_done, 1)

                    @block.vector
                    def _(dve):
                        for c in range(FM):
                            dve.wait_ge(hi_done, c + 1)
                            nc.vector.tensor_tensor(wl[:, c % 2], slab[:, c % RW], f32(wh[:, c % 2]), ALU.subtract).then_inc(lo_done, 1)
                        for k in range(DC):
                            dve.wait_ge(thi_done, k + 1)
                            nc.vector.tensor_tensor(tl[:, k % 2], tslab[:, k % 2], f32(th[:, k % 2]), ALU.subtract).then_inc(tlo_done, 1)
                        for n in range(NT):
                            dve.wait_ge(tend, n + 1)
                            cols = slice((n % 2) * TMC // 2, (n % 2 + 1) * TMC // 2)
                            nc.vector.tensor_copy(tm[:, n // 2, cols], ps[:, n, 0:TMC // 2])

        def phase_gates(l, fm, hk, cum):
            loaded, z_done, e_ready, e_done, f_ready, l_done = (
                sem(f"gates_{x}{l}") for x in ("loaded", "z_done", "e_ready", "e_done", "f_ready", "l_done"))
            with ExitStack() as st:
                lg = sb(st, f"lg{l}", [P, 6, T])
                e = sb(st, f"gate_e{l}", [P, 4, T])
                r = sb(st, f"gate_r{l}", [P, 4, T])
                m = sb(st, f"gate_m{l}", [P, 4, T])
                a = sb(st, f"gate_a{l}", [P, 2, T])
                ea = sb(st, f"gate_ea{l}", [P, 2, T])
                wg = sb(st, f"gate_w{l}", [P, 2, P])
                bg = sb(st, f"gate_b{l}", [P, 2])
                lbr = sb(st, f"lb_raw{l}", [P, DEPTH, HG_CHUNKS])
                lbe = sb(st, f"lb_exp{l}", [P, DEPTH, HG_CHUNKS])
                lbs = sb(st, f"lb_sum{l}", [P, 4, HG_CHUNKS])
                with nc.Block() as block:
                    @block.sync
                    def _(sp):
                        sp.dma_start(wg[GZ0:P], d["gate_w"][l]).then_inc(loaded, 16)
                        sp.dma_start(bg[:], d["gate_b"][l]).then_inc(loaded, 16)
                        sp.dma_start(lbr[:], d["lb_raw"]).then_inc(loaded, 16)

                    @block.tensor
                    def _(pe):
                        pe.wait_ge(loaded, 48)
                        for k in range(2):
                            nc.tensor.matmul(ps[:, k, :], wg[GZ0:P, k, :], fm[GZ0:P, CQ1, :],
                                             start=True, stop=True).then_inc(z_done, 1)

                    @block.scalar
                    def _(act):
                        act.wait_ge(e_ready, 1)
                        nc.scalar.activation(lbe[:], lbe[:], ACT.Exp).then_inc(e_done, 1)
                        act.wait_ge(e_ready, 2)
                        nc.scalar.activation(e[:], e[:], ACT.Exp).then_inc(e_done, 1)
                        act.wait_ge(e_ready, 3)
                        nc.scalar.activation(ea[:], ea[:], ACT.Exp).then_inc(e_done, 1)
                        act.wait_ge(e_done, 3)
                        nc.scalar.activation(ea[:], ea[:], ACT.Ln, bias=onecol[:], scale=1.0).then_inc(l_done, 1)
                        act.wait_ge(f_ready, 1)
                        nc.scalar.activation(r[:], r[:], ACT.Ln).then_inc(l_done, 1)

                    @block.vector
                    def _(dve):
                        def step(ins):
                            dve_chain(dve, ins)
                        dve.wait_ge(loaded, 48)
                        step(nc.vector.tensor_tensor(lbs[:, 0], lbr[:, 0], lbr[:, 1], ALU.max))
                        nc.vector.tensor_tensor(lbe[:], lbr[:], bc(lbs[:, 0], 1, DEPTH), ALU.subtract).then_inc(e_ready, 1)
                        nc.vector.tensor_scalar(e[:], fm[:, HZ:HZ + 4, :], -1.0, 80.0, ALU.mult, ALU.min).then_inc(e_ready, 1)
                        for k in range(2):
                            dve.wait_ge(z_done, k + 1)
                            step(nc.vector.tensor_scalar(a[:, k], ps[:, k, :], bg[:, k:k + 1], None, ALU.add))
                        nc.vector.scalar_tensor_tensor(out=ea[:], in0=a[:], scalar=-1.0, in1=a[:],
                                                       op0=ALU.mult, op1=ALU.min).then_inc(e_ready, 1)
                        dve.wait_ge(e_done, 1)
                        step(nc.vector.tensor_tensor(lbs[:, 0], lbe[:, 0], lbe[:, 1], ALU.add))
                        step(nc.vector.reciprocal(lbs[:, 1], lbs[:, 0]))
                        step(nc.vector.tensor_tensor(lbe[:], lbe[:], bc(lbs[:, 1], 1, DEPTH), ALU.mult))
                        step(nc.vector.tensor_copy(lbs[:, 0], lbe[:, 0]))
                        for i in range(1, l + 1):
                            step(nc.vector.tensor_tensor(lbs[:, 0], lbs[:, 0], lbe[:, i], ALU.add))
                        step(nc.vector.tensor_tensor(lbs[:, 1], lbs[:, 0], lbe[:, 0], ALU.subtract))
                        step(nc.vector.tensor_scalar(lbs[:, 2], lbs[:, 1], -1.0, 1.0, ALU.mult, ALU.add))
                        step(nc.vector.tensor_scalar(lbs[:, 3], lbs[:, 1], LB_FLOOR, None, ALU.max))
                        dve.wait_ge(e_done, 2)
                        step(nc.vector.tensor_scalar(r[:], e[:], 1.0, None, ALU.add))
                        step(nc.vector.reciprocal(r[:], r[:]))
                        for j in range(4):
                            c = j % 2
                            nc.vector.scalar_tensor_tensor(out=hk[:, j], in0=e[:, j], scalar=lbs[:, 2, c:c + 1],
                                                           in1=r[:, j], op0=ALU.mult, op1=ALU.mult)
                        for j in range(4):
                            c = j % 2
                            step(nc.vector.tensor_scalar(r[:, j], r[:, j], lbs[:, 2, c:c + 1], lbs[:, 3, c:c + 1],
                                                         ALU.mult, ALU.add))
                        step(nc.vector.tensor_scalar(m[:], r[:], SMALL, None, ALU.is_lt))
                        step(nc.vector.tensor_scalar(e[:], m[:], UP - 1.0, 1.0, ALU.mult, ALU.add))
                        nc.vector.tensor_tensor(r[:], r[:], e[:], ALU.mult).then_inc(f_ready, 1)
                        dve.wait_ge(l_done, 1)
                        step(nc.vector.scalar_tensor_tensor(out=a[:], in0=a[:], scalar=0.0, in1=ea[:],
                                                            op0=ALU.min, op1=ALU.subtract))
                        for k in range(2):
                            step(nc.vector.tensor_scalar(lg[:, 3 * k], a[:, k], 1.0 / GLA_GATE_NORM, None, ALU.mult))
                        dve.wait_ge(l_done, 2)
                        for k in range(2):
                            step(nc.vector.scalar_tensor_tensor(
                                out=lg[:, 3 * k + 1:3 * k + 3], in0=m[:, 2 * k:2 * k + 2], scalar=-60.0 * math.log(2.0),
                                in1=r[:, 2 * k:2 * k + 2], op0=ALU.mult, op1=ALU.add))
                        nc.vector.memset(cum[:, :, :, 0:1], 0.0)
                        for s in range(6):
                            for t in range(TT):
                                nc.vector.tensor_tensor_scan(cum[:, s, t, 1:P + 1], ones[:], lg[:, s, t * P:(t + 1) * P],
                                                             0.0, ALU.mult, ALU.add)

        def phase_scan(l, lo, fm, tm, hk, cum, mix):
            t0 = lo // P
            nt = TT - t0
            xj = range(1 if t0 else 0, 2)
            arg_done, exp_done, xexp_done, fac_done, ready, unit_mm, unit_ev, x_mm, x_ev, o_mm, o_ev = (
                sem(f"scan_{x}{l}") for x in ("arg_done", "exp_done", "xexp_done", "fac_done", "ready", "unit_mm", "unit_ev",
                                              "x_mm", "x_ev", "o_mm", "o_ev"))
            zeroed, tot_done = sem(f"scan_zeroed{l}"), sem(f"scan_tot_done{l}")
            heads = [(0, GLA_DK * h, GLA_DK) for h in range(4)] + [(1 + h // 2, 64 * (h % 2), 64) for h in range(4)]
            first = [0, 4, 6, 8]
            with ExitStack() as st:
                ex = sb(st, f"scan_ex{l}", [P, 2, 2, NL, TT * HALF])
                lk = sb(st, f"scan_lk{l}", [P, 2, NL, TT, P])
                xq = sb(st, f"scan_xq{l}", [P, 2, 4, P])
                xk = sb(st, f"scan_xk{l}", [P, 2, 4, P])
                ksum = sb(st, f"scan_ksum{l}", [P, T])
                tot2 = sb(st, f"scan_tot2{l}", [P, 2, 6])
                sc = sb(st, f"scan_sc{l}", [P, 2, TT, P])
                scx = sb(st, f"scan_scx{l}", [P, 2, 2, BANK])

                def keys(c, dr):
                    return fm[:, GK, :] if c == 0 else hk[:, 2 * dr + c - 1, :]

                def queries(c):
                    return fm[:, GQ if c == 0 else HQ + c - 1, :]

                with nc.Block() as block:
                    @block.vector
                    def _(dve):
                        nc.vector.memset(lk[:], 0.0).then_inc(zeroed, 1)
                        dve.wait_ge(zeroed, 1)
                        for j in range(2):
                            nc.vector.tensor_tensor(tot2[:, j], cum[:, :, 2 * j, P], cum[:, :, 2 * j + 1, P], ALU.add)\
                                .then_inc(tot_done, 1)

                        def factors(c):
                            if c:
                                dve.wait_ge(unit_mm, NU * first[c])
                                dve.wait_ge(x_mm, first[c])
                            for dr in range(2):
                                cb = cum[:, 3 * dr + c, t0:TT]
                                before, upto = cb[:, :, 0:P], cb[:, :, 1:P + 1]
                                for i, L in enumerate(LEVELS):
                                    mid = mids(before, L)
                                    qa = ex[:, dr, 0, i, t0 * HALF:].rearrange("p (a n l) -> p a n l", a=nt, l=L)
                                    ka = ex[:, dr, 1, i, t0 * HALF:].rearrange("p (a n l) -> p a n l", a=nt, l=L)
                                    if dr == 0:
                                        nc.vector.tensor_tensor(qa, halves(upto, L, 1), mid, ALU.subtract)
                                        last = nc.vector.tensor_tensor(ka, mid, halves(upto, L, 0), ALU.subtract)
                                    else:
                                        nc.vector.tensor_tensor(qa, mid, halves(before, L, 0), ALU.subtract)
                                        last = nc.vector.tensor_tensor(ka, halves(before, L, 1), mid, ALU.subtract)
                                last.then_inc(arg_done, 1)
                            for dr in range(2):
                                q = queries(c).rearrange("p (a t) -> p a t", a=TT)
                                k = keys(c, dr).rearrange("p (a t) -> p a t", a=TT)
                                dve.wait_ge(exp_done, 2 * c + dr + 1)
                                for i, L in enumerate(LEVELS):
                                    qa = ex[:, dr, 0, i, t0 * HALF:].rearrange("p (a n l) -> p a n l", a=nt, l=L)
                                    ka = ex[:, dr, 1, i, t0 * HALF:].rearrange("p (a n l) -> p a n l", a=nt, l=L)
                                    nc.vector.tensor_tensor(qa, qa, halves(q[:, t0:], L, 1 - dr), ALU.mult)
                                    nc.vector.tensor_tensor(halves(lk[:, dr, i, t0:], L, dr), ka, halves(k[:, t0:], L, dr), ALU.mult)
                                dve.wait_ge(xexp_done, 2 * c + dr + 1)
                                for j in xj:
                                    a, b = XQ_TILES[dr][j], XK_TILES[dr][j]
                                    nc.vector.tensor_tensor(xq[:, dr, j], xq[:, dr, j], q[:, a], ALU.mult)
                                    nc.vector.tensor_tensor(xk[:, dr, j], xk[:, dr, j], k[:, b], ALU.mult)
                                nc.vector.tensor_tensor(xq[:, dr, 2:4], xq[:, dr, 2:4], q[:, 2:4], ALU.mult)
                                nc.vector.tensor_tensor(xk[:, dr, 2:4], xk[:, dr, 2:4], k[:, 0:2], ALU.mult)
                            nc.vector.tensor_tensor(ksum[:, lo:], keys(c, 0)[:, lo:], keys(c, 1)[:, lo:], ALU.add).then_inc(ready, 1)

                        def gather(h):
                            for u, unit in enumerate(UNITS):
                                n = NU * h + u
                                dve.wait_ge(unit_mm, n + 1)
                                if n:
                                    dve.wait_ge(unit_ev, n)
                                if u == 0 and h >= 2:
                                    dve.wait_ge(o_mm, h - 1)
                                dst = sc[:, h % 2]
                                if unit is None:
                                    nc.vector.copy_predicated(dst[:, t0:], bc(maskd[:], 1, nt),
                                                              ps[:, n % 4, lo:].rearrange("p (a t) -> p a t", a=nt)).then_inc(unit_ev, 1)
                                    continue
                                for j, (dr, i) in enumerate(unit):
                                    L = LEVELS[i]
                                    got = ps[:, n % 4, j * 256 + t0 * HALF:(j + 1) * 256].rearrange("p (a n l) -> p a n l", a=nt, l=L)
                                    msk = bc(mask[:, NL * dr + i].rearrange("p (n l) -> p n l", l=L), 1, nt)
                                    copied = nc.vector.copy_predicated(halves(dst[:, t0:], L, 1 - dr), msk, got)
                                    if j == 0:
                                        dve_chain(dve, copied)
                                    else:
                                        copied.then_inc(unit_ev, 1)

                        for c in range(3):
                            factors(c)
                            for h in range(first[c], first[c + 1]):
                                gather(h)

                    @block.scalar
                    def _(act):
                        def exps(c):
                            for dr in range(2):
                                act.wait_ge(arg_done, 2 * c + dr + 1)
                                e = ex[:, dr, :, :, t0 * HALF:].rearrange("p a i t -> p (a i) t")
                                nc.scalar.activation(e, e, ACT.Exp).then_inc(exp_done, 1)
                                s = 3 * dr + c
                                cb = cum[:, s]
                                tot = [cum[:, s, t, P:P + 1] for t in range(TT)]
                                tot01, tot23 = tot2[:, 0, s:s + 1], tot2[:, 1, s:s + 1]
                                if c == 0 and dr == 0:
                                    act.wait_ge(tot_done, 2)
                                if dr == 0:
                                    o = 1
                                    jobs = [(xq, 0, 1, 1.0, None), (xq, 1, 3, 1.0, None), (xq, 2, 2, 1.0, None), (xq, 3, 3, 1.0, tot[2]),
                                            (xk, 0, 0, -1.0, tot[0]), (xk, 1, 2, -1.0, tot[2]),
                                            (xk, 2, 0, -1.0, tot01), (xk, 3, 1, -1.0, tot[1])]
                                else:
                                    o = 0
                                    jobs = [(xq, 0, 0, -1.0, tot[0]), (xq, 1, 2, -1.0, tot[2]),
                                            (xq, 2, 2, -1.0, tot23), (xq, 3, 3, -1.0, tot[3]),
                                            (xk, 0, 1, 1.0, None), (xk, 1, 3, 1.0, None),
                                            (xk, 2, 0, 1.0, None), (xk, 3, 1, 1.0, tot[0])]
                                for buf, j, t, scale, bias in jobs:
                                    if j < 2 and j not in xj:
                                        continue
                                    src = cb[:, t, o:o + P]
                                    if bias is None:
                                        last = nc.scalar.activation(buf[:, dr, j], src, ACT.Exp, scale=scale)
                                    else:
                                        last = nc.scalar.activation(buf[:, dr, j], src, ACT.Exp, scale=scale, bias=bias)
                                last.then_inc(xexp_done, 1)

                        def evac(h):
                            act.wait_ge(x_mm, h + 1)
                            if h >= 2:
                                act.wait_ge(o_mm, h - 1)
                            if t0:
                                two = ps[:, 4, :].rearrange("p (dr j t) -> p dr j t", dr=2, j=2)[:, :, 1, :]
                                nc.scalar.activation(scx[:, h % 2, 0, :].rearrange("p (dr j t) -> p dr j t", dr=2, j=2)[:, :, 1, :],
                                                     two, ACT.Copy)
                                nc.scalar.activation(scx[:, h % 2, 1], ps[:, 5, :], ACT.Copy).then_inc(x_ev, 1)
                            else:
                                nc.scalar.activation(scx[:, h % 2], ps[:, 4:6, :], ACT.Copy).then_inc(x_ev, 1)

                        def out(h):
                            act.wait_ge(o_mm, h + 1)
                            p0 = 64 * (h % 2)
                            nc.scalar.activation(mix[p0:p0 + 64, h // 2, lo:], ps[p0:p0 + 64, 6 + h % 2, lo:], ACT.Copy).then_inc(o_ev, 1)

                        for c in range(3):
                            if c:
                                act.wait_ge(x_mm, first[c])
                            exps(c)
                            for h in range(first[c], first[c + 1]):
                                evac(h)
                                if h:
                                    out(h - 1)
                        out(7)

                    @block.tensor
                    def _(pe):
                        def scores(h):
                            c, p0, w = heads[h]
                            if h == first[c]:
                                pe.wait_ge(ready, c + 1)
                            r = slice(p0, p0 + w)
                            q = queries(c)
                            for u, unit in enumerate(UNITS):
                                n = NU * h + u
                                if n >= 4:
                                    pe.wait_ge(unit_ev, n - 3)
                                if unit is None:
                                    for t in range(t0, TT):
                                        mm = nc.tensor.matmul(ps[:, n % 4, t * P:(t + 1) * P], ksum[r, t * P:(t + 1) * P],
                                                              q[r, t * P:(t + 1) * P], start=True, stop=True)
                                else:
                                    for j, (dr, i) in enumerate(unit):
                                        for t in range(t0, TT):
                                            o = j * 256 + t * HALF
                                            mm = nc.tensor.matmul(ps[:, n % 4, o:o + HALF], lk[r, dr, i, t, :],
                                                                  ex[r, dr, 0, i, t * HALF:(t + 1) * HALF], start=True, stop=True)
                                mm.then_inc(unit_mm, 1)
                            if h >= 1:
                                pe.wait_ge(x_ev, h)
                            for dr in range(2):
                                for j in xj:
                                    o = (2 * dr + j) * P
                                    nc.tensor.matmul(ps[:, 4, o:o + P], xk[r, dr, j, :], xq[r, dr, j, :], start=True, stop=True)
                            for s in range(2):
                                for dr in range(2):
                                    mm = nc.tensor.matmul(ps[:, 5, s * 256:(s + 1) * 256], xk[r, dr, 2 + s, :],
                                                          xq[r, dr, 2:4, :], start=(dr == 0), stop=(dr == 1))
                            mm.then_inc(x_mm, 1)

                        def output(h):
                            pe.wait_ge(unit_ev, NU * (h + 1))
                            pe.wait_ge(x_ev, h + 1)
                            if h >= 2:
                                pe.wait_ge(o_ev, h - 1)
                            p0 = 64 * (h % 2)
                            for t in range(t0, TT):
                                parts = [(t, sc[:, h % 2, t, :])]
                                for dr in range(2):
                                    for j in range(2):
                                        if XQ_TILES[dr][j] == t:
                                            o = (2 * dr + j) * P
                                            parts.append((XK_TILES[dr][j], scx[:, h % 2, 0, o:o + P]))
                                if t >= 2:
                                    for s in range(2):
                                        o = s * 256 + (t - 2) * P
                                        parts.append((s, scx[:, h % 2, 1, o:o + P]))
                                for j, (s, sco) in enumerate(parts):
                                    mm = nc.tensor.matmul(ps[p0:p0 + 64, 6 + h % 2, t * P:(t + 1) * P],
                                                          tm[:, s, h * DV:(h + 1) * DV], sco,
                                                          start=(j == 0), stop=(j == len(parts) - 1))
                            mm.then_inc(o_mm, 1)

                        for h in range(8):
                            scores(h)
                            if h:
                                output(h - 1)
                        output(7)

        def phase_attn(l, lo, fm, tm, mix):
            t0 = lo // P
            nt = TT - t0
            lam_init = 0.8 - 0.6 * math.exp(-0.3 * l)
            (loaded, sq_done, sum_done, n_done, qk_mm, qk_ev, rot_mm, rot_ev, prep_done, lam_e, lam_x, s_done, nm_done, exp_done,
             diag_done, t_done, ptc_done, pv_done, oev_done, root_done) = (
                sem(f"attn_{x}{l}") for x in ("loaded", "sq_done", "sum_done", "n_done", "qk_mm", "qk_ev", "rot_mm", "rot_ev",
                                              "prep_done", "lam_e", "lam_x", "s_done", "nm_done", "exp_done", "diag_done", "t_done",
                                              "ptc_done", "pv_done", "oev_done", "root_done"))
            NUN = 2 * HEADS * nt
            ncomp = [1 if n < HEADS * nt else 2 for n in range(NUN)]
            keys_of = [T if t0 + n % nt >= CTX // P else CTX for n in range(NUN)]
            c0 = [sum(ncomp[:n]) for n in range(NUN + 1)]
            with ExitStack() as st:
                wq = sb(st, f"mla_wq{l}", [P, 2, HEADS, MLA_DQ])
                wkv = sb(st, f"mla_wkv{l}", [P, HEADS, P])
                gq = sb(st, f"mla_gq{l}", [P, 2])
                gkv = sb(st, f"mla_gkv{l}", [P, 1])
                sq = sb(st, f"mla_sq{l}", [P, 3, T])
                rs = sb(st, f"mla_rs{l}", [P, 2, T])
                qh = sb(st, f"mla_qh{l}", [P, HEADS, T])
                kh = sb(st, f"mla_kh{l}", [P, HEADS, T])
                vm = sb(st, f"mla_v{l}", [P, TT, HEADS * DV])
                rot = sb(st, f"rot{l}", [P, 2, SEQ])
                lamr = sb(st, f"lamr{l}", [P, 4, DIFF_DQK])
                lamp = sb(st, f"lamp{l}", [P, 2, DIFF_DQK])
                lame = sb(st, f"lame{l}", [P, 2])
                nlam = sb(st, f"nlam{l}", [P, 1])
                pr = sb(st, f"probs{l}", [P, 2, 2, T])
                pt = sb(st, f"probsT{l}", [P, 2, T])
                dg = sb(st, f"diag{l}", [P, 2, 2, P])
                mx = sb(st, f"smax{l}", [P, c0[-1]])
                nm = sb(st, f"nsmax{l}", [P, c0[-1]])
                rsum = sb(st, f"rsum{l}", [P, c0[-1]])
                rinv = sb(st, f"rinv{l}", [P, c0[-1]])
                rots = [(slice(0, P), fm[:, DQ + j, CTX:T]) for j in range(4)] + \
                       [(slice(KR0, KR0 + 32), fm[KR0:KR0 + 32, CQ1, CTX:T])] + \
                       [(slice(KR0, KR0 + 32), qh[KR0:KR0 + 32, h, CTX:T]) for h in range(HEADS)]
                with nc.Block() as block:
                    @block.sync
                    def _(sp):
                        sp.dma_start(wq[:, 0], d["w_uq"][l, 0:P]).then_inc(loaded, 16)
                        sp.dma_start(wq[0:64, 1], d["w_uq"][l, P:MLA_Q]).then_inc(loaded, 16)
                        sp.dma_start(wkv[:], d["w_ukv"][l]).then_inc(loaded, 16)
                        sp.dma_start(gq[:, 0:1], d["g_q0"][l]).then_inc(loaded, 16)
                        sp.dma_start(gq[0:64, 1:2], d["g_q1"][l]).then_inc(loaded, 16)
                        sp.dma_start(gkv[:], d["g_kv"][l]).then_inc(loaded, 16)
                        sp.dma_start(lamr[:], d["lam"][l].partition_broadcast(P)).then_inc(loaded, 16)

                    @block.scalar
                    def _(act):
                        nc.scalar.activation(sq[:, 0, lo:], fm[:, CQ0, lo:], ACT.Square)
                        nc.scalar.activation(sq[0:64, 1, lo:], fm[0:64, CQ1, lo:], ACT.Square)
                        nc.scalar.activation(sq[:, 2], fm[:, CKV, :], ACT.Square).then_inc(sq_done, 1)
                        act.wait_ge(lam_e, 1)
                        nc.scalar.activation(lame[:], lame[:], ACT.Exp).then_inc(lam_x, 1)
                        act.wait_ge(sum_done, 1)
                        for j, (width, a) in enumerate(((MLA_Q, lo), (MLA_KV, 0))):
                            nc.scalar.activation(rs[:, j, a:], ps[:, j, a:], ACT.Sqrt, scale=1.0 / width,
                                                 bias=epscol[:]).then_inc(root_done, 1)
                        for n in range(3 * HEADS):
                            act.wait_ge(qk_mm, n + 1)
                            bank = n % 4
                            if n < HEADS:
                                nc.scalar.activation(qh[0:MLA_DQ, n, lo:], ps[0:MLA_DQ, bank, lo:], ACT.Copy).then_inc(qk_ev, 1)
                            elif n < 2 * HEADS:
                                nc.scalar.activation(kh[0:64, n - HEADS], ps[0:64, bank, :], ACT.Copy).then_inc(qk_ev, 1)
                            else:
                                nc.scalar.activation(vm[:, n - 2 * HEADS], ps[:, bank, 0:HEADS * DV], ACT.Copy).then_inc(qk_ev, 1)

                        def exps(n):
                            for c in range(ncomp[n]):
                                j = c0[n] + c
                                act.wait_ge(nm_done, j + 1)
                                if n >= 2:
                                    act.wait_ge(t_done, n - 1)
                                ns = keys_of[n]
                                scale = (MLA_DQ if n < HEADS * nt else DIFF_DQK) ** -0.5
                                nc.scalar.activation(pr[:, n % 2, c, 0:ns], ps[:, 2 * (n % 2) + c, 0:ns], ACT.Exp, scale=scale,
                                                     bias=nm[:, j:j + 1], accum_out=rsum[:, j:j + 1]).then_inc(exp_done, 1)

                        def turned(n):
                            act.wait_ge(t_done, n + 1)
                            if n >= 2:
                                act.wait_ge(pv_done, n - 1)
                            ns = keys_of[n]
                            nc.scalar.activation(pt[:, n % 2, 0:ns], ps[:, 4 + n % 2, 0:ns], ACT.Copy).then_inc(ptc_done, 1)

                        def evac(h):
                            act.wait_ge(pv_done, nt * (h + 1))
                            p0 = 64 * (h % 2)
                            nc.scalar.activation(mix[p0:p0 + 64, 4 + h // 2, lo:], ps[p0:p0 + 64, 6 + h % 2, lo:], ACT.Copy).then_inc(oev_done, 1)

                        exps(0)
                        for n in range(NUN):
                            if n + 1 < NUN:
                                exps(n + 1)
                            turned(n)
                            if n % nt == 1 and n > nt:
                                evac(n // nt - 1)
                        evac(2 * HEADS - 1)

                    @block.tensor
                    def _(pe):
                        pe.wait_ge(sq_done, 1)
                        nc.tensor.matmul(ps[:, 0, lo:], ones[:], sq[:, 0, lo:], start=True, stop=False)
                        nc.tensor.matmul(ps[:, 0, lo:], ones[0:64, :], sq[0:64, 1, lo:], start=False, stop=True)
                        nc.tensor.matmul(ps[:, 1, :], ones[:], sq[:, 2], start=True, stop=True).then_inc(sum_done, 1)
                        pe.wait_ge(n_done, 1)
                        for n in range(3 * HEADS):
                            bank = n % 4
                            if n >= 4:
                                pe.wait_ge(qk_ev, n - 3)
                            h = n % HEADS
                            if n < HEADS:
                                nc.tensor.matmul(ps[0:MLA_DQ, bank, lo:], wq[:, 0, h, :], fm[:, CQ0, lo:], start=True, stop=False)
                                mm = nc.tensor.matmul(ps[0:MLA_DQ, bank, lo:], wq[0:64, 1, h, :], fm[0:64, CQ1, lo:],
                                                      start=False, stop=True)
                            elif n < 2 * HEADS:
                                mm = nc.tensor.matmul(ps[0:64, bank, :], wkv[:, h, 0:MLA_NOPE], fm[:, CKV, :], start=True, stop=True)
                            else:
                                mm = nc.tensor.matmul(ps[:, bank, 0:HEADS * DV], fm[:, CKV, h * P:(h + 1) * P],
                                                      wkv[:, :, MLA_NOPE:P], start=True, stop=True)
                            mm.then_inc(qk_mm, 1)
                        for n, (rows, x) in enumerate(rots):
                            if n == 5:
                                pe.wait_ge(qk_ev, HEADS)
                            if n >= 2:
                                pe.wait_ge(rot_ev, n - 1)
                            nc.tensor.matmul(ps[rows, 4 + n % 2, 0:SEQ], rotp[rows, rows], x, start=True, stop=True).then_inc(rot_mm, 1)
                        pe.wait_ge(prep_done, 1)
                        pe.wait_ge(qk_ev, 3 * HEADS)

                        def scores(n):
                            h, t = n // nt, t0 + n % nt
                            ns = T if t >= 2 else CTX
                            for c in range(ncomp[n]):
                                if n >= 2:
                                    pe.wait_ge(exp_done, c0[n - 1])
                                if h < HEADS:
                                    q, k = qh[0:MLA_DQ, h, t * P:(t + 1) * P], kh[0:MLA_DQ, h, 0:ns]
                                else:
                                    j = 2 * (h - HEADS) + c
                                    r = slice(32 * (j % 4), 32 * (j % 4) + 32)
                                    q, k = fm[r, DQ + j // 4, t * P:(t + 1) * P], fm[r, DK + j // 4, 0:ns]
                                nc.tensor.matmul(ps[:, 2 * (n % 2) + c, 0:ns], q, k, start=True, stop=True).then_inc(s_done, 1)

                        def turn(n):
                            pe.wait_ge(diag_done, c0[n + 1])
                            if n >= 2:
                                pe.wait_ge(ptc_done, n - 1)
                            for s in range(keys_of[n] // P):
                                for c in range(ncomp[n]):
                                    mm = nc.tensor.matmul(ps[:, 4 + n % 2, s * P:(s + 1) * P], pr[:, n % 2, c, s * P:(s + 1) * P],
                                                          dg[:, n % 2, c, :], start=(c == 0), stop=(c == ncomp[n] - 1))
                            mm.then_inc(t_done, 1)

                        def values(n):
                            h, t = n // nt, t0 + n % nt
                            pe.wait_ge(ptc_done, n + 1)
                            if t == t0 and h >= 2:
                                pe.wait_ge(oev_done, h - 1)
                            p0 = 64 * (h % 2)
                            nst = keys_of[n] // P
                            for s in range(nst):
                                v = vm[:, s, h * DV:(h + 1) * DV] if h < HEADS else \
                                    tm[:, s, (h + HEADS) * DV:(h + HEADS + 1) * DV]
                                mm = nc.tensor.matmul(ps[p0:p0 + 64, 6 + h % 2, t * P:(t + 1) * P], v, pt[:, n % 2, s * P:(s + 1) * P],
                                                      start=(s == 0), stop=(s == nst - 1))
                            mm.then_inc(pv_done, 1)

                        scores(0)
                        for n in range(NUN):
                            if n + 1 < NUN:
                                scores(n + 1)
                            turn(n)
                            if n:
                                values(n - 1)
                        values(NUN - 1)

                    @block.vector
                    def _(dve):
                        def step(ins):
                            dve_chain(dve, ins)
                        dve.wait_ge(loaded, 7 * 16)
                        step(nc.vector.tensor_tensor(lamp[:], lamr[:, 0:4:2], lamr[:, 1:4:2], ALU.mult))
                        nc.vector.tensor_reduce(lame[:], lamp[:], AX, ALU.add).then_inc(lam_e, 1)
                        dve.wait_ge(lam_x, 1)
                        step(nc.vector.tensor_tensor(nlam[:], lame[:, 1:2], lame[:, 0:1], ALU.subtract))
                        step(nc.vector.tensor_scalar(nlam[:], nlam[:], -lam_init, None, ALU.add))
                        dve.wait_ge(root_done, 2)
                        nc.vector.reciprocal(rs[:, 0, lo:], rs[:, 0, lo:])
                        step(nc.vector.reciprocal(rs[:, 1], rs[:, 1]))
                        for x, g, r in ((fm[:, CQ0, lo:], gq[:, 0:1], rs[:, 0, lo:]), (fm[0:64, CQ1, lo:], gq[0:64, 1:2], rs[0:64, 0, lo:]),
                                        (fm[:, CKV, :], gkv[:], rs[:, 1])):
                            last = nc.vector.scalar_tensor_tensor(out=x, in0=x, scalar=g, in1=r, op0=ALU.mult, op1=ALU.mult)
                        last.then_inc(n_done, 1)
                        for n, (rows, x) in enumerate(rots):
                            dve.wait_ge(rot_mm, n + 1)
                            nc.vector.tensor_tensor(rot[rows, n % 2], ps[rows, 4 + n % 2, 0:SEQ], sinT[rows], ALU.mult).then_inc(rot_ev, 1)
                            step(nc.vector.tensor_tensor(x, x, cosT[rows], ALU.mult))
                            dve.wait_ge(rot_ev, n + 1)
                            last = nc.vector.tensor_tensor(x, x, rot[rows, n % 2], ALU.add)
                            if n == 4:
                                step(last)
                                for h in range(HEADS):
                                    nc.vector.tensor_copy(kh[KR0:KR0 + 32, h], fm[KR0:KR0 + 32, CQ1, :])
                        last.then_inc(prep_done, 1)

                        def maxima(n):
                            ns = keys_of[n]
                            scale = (MLA_DQ if n < HEADS * nt else DIFF_DQK) ** -0.5
                            for c in range(ncomp[n]):
                                j = c0[n] + c
                                dve.wait_ge(s_done, j + 1)
                                step(nc.vector.tensor_reduce(mx[:, j:j + 1], ps[:, 2 * (n % 2) + c, 0:ns], AX, ALU.max))
                                nc.vector.tensor_scalar(nm[:, j:j + 1], mx[:, j:j + 1], -scale, None, ALU.mult).then_inc(nm_done, 1)

                        def diagonals(n):
                            for c in range(ncomp[n]):
                                j = c0[n] + c
                                dve.wait_ge(exp_done, j + 1)
                                step(nc.vector.reciprocal(rinv[:, j:j + 1], rsum[:, j:j + 1]))
                                if n >= 2:
                                    dve.wait_ge(t_done, n - 1)
                                if c == 0:
                                    nc.vector.tensor_scalar(dg[:, n % 2, c], ident[:], rinv[:, j:j + 1], None, ALU.mult).then_inc(diag_done, 1)
                                else:
                                    nc.vector.tensor_scalar(dg[:, n % 2, c], ident[:], rinv[:, j:j + 1], nlam[:], ALU.mult, ALU.mult)\
                                        .then_inc(diag_done, 1)

                        maxima(0)
                        for n in range(NUN):
                            if n + 1 < NUN:
                                maxima(n + 1)
                            diagonals(n)

        def phase_post(l, lo, fm, mix):
            lam_init = 0.8 - 0.6 * math.exp(-0.3 * l)
            chunks = [0, 1, 2, 3, 6, 7]
            loaded, sq_done, sum_done, root_done = (sem(f"post_{x}{l}") for x in ("loaded", "sq_done", "sum_done", "root_done"))
            with ExitStack() as st:
                sq = sb(st, f"post_sq{l}", [P, 6, T])
                g = sb(st, f"post_g{l}", [P, 3])
                with nc.Block() as block:
                    @block.sync
                    def _(sp):
                        sp.dma_start(g[:], d["g_head"][l]).then_inc(loaded, 16)

                    @block.scalar
                    def _(act):
                        for j, c in enumerate(chunks):
                            nc.scalar.activation(sq[:, j, lo:], mix[:, c, lo:], ACT.Square).then_inc(sq_done, 1)
                        for j in range(6):
                            act.wait_ge(sum_done, j + 1)
                            nc.scalar.activation(sq[:, j, lo:], ps[:, j, lo:], ACT.Sqrt, bias=epscol[:]).then_inc(root_done, 1)

                    @block.tensor
                    def _(pe):
                        for j in range(6):
                            pe.wait_ge(sq_done, j + 1)
                            nc.tensor.matmul(ps[:, j, lo:], mean64[:], sq[:, j, lo:], start=True, stop=True).then_inc(sum_done, 1)

                    @block.vector
                    def _(dve):
                        def step(ins):
                            dve_chain(dve, ins)
                        dve.wait_ge(loaded, 16)
                        step(nc.vector.tensor_scalar(g[:, 2:3], g[:, 2:3], 1.0 - lam_init, None, ALU.mult))
                        for j, c in enumerate(chunks):
                            dve.wait_ge(root_done, j + 1)
                            step(nc.vector.reciprocal(sq[:, j, lo:], sq[:, j, lo:]))
                            step(nc.vector.scalar_tensor_tensor(out=mix[:, c, lo:], in0=mix[:, c, lo:], scalar=g[:, j // 2:j // 2 + 1],
                                                                in1=sq[:, j, lo:], op0=ALU.mult, op1=ALU.mult))
                            if c < 4:
                                nc.vector.tensor_tensor(mix[:, c, lo:], mix[:, c, lo:], fm[:, GATE0 + c, lo:], ALU.mult)

        def add_gated(k, which, src, lo):
            n = []
            for v, (a, b) in enumerate(((lo, CTX), (max(lo, CTX), T))):
                if a < b:
                    w = 1 - v
                    n.append(nc.vector.scalar_tensor_tensor(out=xT[:, k, a:b], in0=src[:, a - lo:b - lo],
                                                            scalar=mod[:, which * DC + k, w:w + 1], in1=xT[:, k, a:b],
                                                            op0=ALU.mult, op1=ALU.add))
            return n[-1]

        def phase_out(l, lo, mix):
            RW = 4
            w_in = [sem(f"out_w_in{l}_{r}") for r in range(RW)]
            xhi_done, xlo_done, hi_done, lo_done, mm_done, ev_done = (
                sem(f"out_{x}{l}") for x in ("xhi", "xlo", "hi", "lo", "mm", "ev"))
            with ExitStack() as st:
                slab = sb(st, f"out_slab{l}", [P, RW, DC, P])
                wh = sb(st, f"out_wh{l}", [P, 2, DC, P], F32R)
                wl = sb(st, f"out_wl{l}", [P, 2, DC, P], F32R)
                xh = sb(st, f"out_xh{l}", [P, DC, T - lo], F32R)
                xl = sb(st, f"out_xl{l}", [P, DC, T - lo], F32R)
                with nc.Block() as block:
                    @block.sync
                    def _(sp):
                        for c in range(DC):
                            if c >= RW:
                                sp.wait_ge(lo_done, c - RW + 1)
                            sp.dma_start(slab[:, c % RW], d["w_out"][l, c]).then_inc(w_in[c % RW], 16)

                    @block.tensor
                    def _(pe):
                        for c in range(DC):
                            pe.wait_ge(lo_done, c + 1)
                            if c >= 4:
                                pe.wait_ge(ev_done, c - 3)
                            for k in range(DC):
                                if c == 0:
                                    pe.wait_ge(xlo_done, k + 1)
                                mm = product(nc, ps[:, c % 4, 0:T - lo], (wh[:, c % 2, k, :], wl[:, c % 2, k, :]),
                                             (xh[:, k, :], xl[:, k, :]), k == 0, k == DC - 1)
                            mm.then_inc(mm_done, 1)

                    @block.scalar
                    def _(act):
                        for k in range(DC):
                            nc.scalar.activation(xh[:, k, :], mix[:, k, lo:], ACT.Copy).then_inc(xhi_done, 1)
                        for c in range(DC):
                            act.wait_ge(w_in[c % RW], 16 * (c // RW + 1))
                            if c >= 2:
                                act.wait_ge(mm_done, c - 1)
                            nc.scalar.activation(wh[:, c % 2], slab[:, c % RW], ACT.Copy).then_inc(hi_done, 1)

                    @block.gpsimd
                    def _(pool):
                        for c in range(DC):
                            pool.wait_ge(hi_done, c + 1)
                            nc.gpsimd.tensor_tensor(wl[:, c % 2], slab[:, c % RW], f32(wh[:, c % 2]), ALU.subtract).then_inc(lo_done, 1)

                    @block.vector
                    def _(dve):
                        for k in range(DC):
                            dve.wait_ge(xhi_done, k + 1)
                            nc.vector.tensor_tensor(xl[:, k, :], mix[:, k, lo:], f32(xh[:, k, :]), ALU.subtract).then_inc(xlo_done, 1)
                        for c in range(DC):
                            dve.wait_ge(mm_done, c + 1)
                            add_gated(c, 2, ps[:, c % 4, :], lo).then_inc(ev_done, 1)

        def phase_route(l, lo, hp, iT, jT, gT):
            RW = 4
            nt = (T - lo) // P
            n = T - lo
            HP = 2 * PH
            w_in = [sem(f"route_w_in{l}_{r}") for r in range(RW)]
            (k_in, hi_done, lo_done, q_mm, q_ev, s_mm, s_ev, s_used, b_done, x_done, tr_in, tr_mm, tr_ev) = (
                sem(f"route_{x}{l}") for x in ("k_in", "hi", "lo", "q_mm", "q_ev", "s_mm", "s_ev", "s_used", "b_done", "x_done",
                                               "tr_in", "tr_mm", "tr_ev"))
            with ExitStack() as st:
                slab = sb(st, f"route_slab{l}", [P, RW, DC, P])
                wh = sb(st, f"route_wh{l}", [P, 2, DC, P], F32R)
                wl = sb(st, f"route_wl{l}", [P, 2, DC, P], F32R)
                kT = sb(st, f"route_keys{l}", [P, HP, NKEY])
                qT = sb(st, f"route_q{l}", [P, 2, n])
                s_sb = sb(st, f"route_s{l}", [P, 2, nt, NKEY])
                s2 = sb(st, f"route_s2{l}", [P, 2 * NKEY])
                top = sb(st, f"route_top{l}", [P, nt, HP, TOPK])
                idx = sb(st, f"route_idx{l}", [P, nt, HP, TOPK], U32)
                idf = sb(st, f"route_idf{l}", [P, nt, HP, TOPK])
                cand = sb(st, f"route_cand{l}", [P, PH, TOPK, TOPK])
                best = sb(st, f"route_best{l}", [P, PH, TOPK])
                sel = sb(st, f"route_sel{l}", [P, PH, TOPK], U32)
                sela = sb(st, f"route_sela{l}", [P, 2, PH * TOPK], U32)
                self_ = sb(st, f"route_self{l}", [P, 2, PH * TOPK])
                eq = sb(st, f"route_eq{l}", [P, PH * TOPK, TOPK])
                ijg = sb(st, f"route_ijg{l}", [P, 2, 3, PH * TOPK])
                esum = sb(st, f"route_esum{l}", [P, PH])
                with nc.Block() as block:
                    @block.sync
                    def _(sp):
                        for c in range(HP):
                            if c >= RW:
                                sp.wait_ge(lo_done, c - RW + 1)
                            sp.dma_start(slab[:, c % RW], d["w_pq"][l, c]).then_inc(w_in[c % RW], 16)
                            if c == 0:
                                sp.dma_start(kT[:], d["keysT"][l]).then_inc(k_in, 16)

                    @block.tensor
                    def _(pe):
                        def sub_scores(c):
                            pe.wait_ge(q_ev, c + 1)
                            pe.wait_ge(k_in, 16)
                            if c >= 2:
                                pe.wait_ge(s_ev, c - 1)
                            for t in range(nt):
                                mm = nc.tensor.matmul(ps[:, 2 + c % 2, t * P:(t + 1) * P], qT[:, c % 2, t * P:(t + 1) * P], kT[:, c, :],
                                                      start=True, stop=True)
                            mm.then_inc(s_mm, 1)

                        for c in range(HP):
                            pe.wait_ge(lo_done, c + 1)
                            if c >= 2:
                                pe.wait_ge(q_ev, c - 1)
                            for k in range(DC):
                                mm = product(nc, ps[:, c % 2, 0:n], (wh[:, c % 2, k, :], wl[:, c % 2, k, :]),
                                             (hp[0][:, k, :], hp[1][:, k, :]), k == 0, k == DC - 1)
                            mm.then_inc(q_mm, 1)
                            if c:
                                sub_scores(c - 1)
                        sub_scores(HP - 1)
                        for t in range(nt):
                            pe.wait_ge(tr_in, t + 1)
                            if t >= 1:
                                pe.wait_ge(tr_ev, t)
                            for j in range(3):
                                mm = nc.tensor.transpose(ps[:, 4, j * P:(j + 1) * P], ijg[:, t % 2, j, :], ident[:])
                            mm.then_inc(tr_mm, 1)

                    @block.scalar
                    def _(act):
                        def s_copy(c):
                            act.wait_ge(s_mm, c + 1)
                            if c >= 2:
                                act.wait_ge(s_used, c - 1)
                            nc.scalar.activation(s_sb[:, c % 2], ps[:, 2 + c % 2, 0:n].rearrange("p (a k) -> p a k", a=nt),
                                                 ACT.Copy).then_inc(s_ev, 1)
                        def w_hi(c):
                            act.wait_ge(w_in[c % RW], 16 * (c // RW + 1))
                            if c >= 2:
                                act.wait_ge(q_mm, c - 1)
                            nc.scalar.activation(wh[:, c % 2], slab[:, c % RW], ACT.Copy).then_inc(hi_done, 1)

                        w_hi(0)
                        w_hi(1)
                        for c in range(HP):
                            act.wait_ge(q_mm, c + 1)
                            if c + 2 < HP:
                                w_hi(c + 2)
                            if c >= 2:
                                act.wait_ge(s_mm, c - 1)
                            nc.scalar.activation(qT[:, c % 2, :], ps[:, c % 2, 0:n], ACT.Copy).then_inc(q_ev, 1)
                            if c:
                                s_copy(c - 1)
                        s_copy(HP - 1)
                        for t in range(nt):
                            act.wait_ge(b_done, t + 1)
                            nc.scalar.activation(best[:], best[:], ACT.Exp).then_inc(x_done, 1)

                    @block.gpsimd
                    def _(pool):
                        for c in range(HP):
                            pool.wait_ge(hi_done, c + 1)
                            nc.gpsimd.tensor_tensor(wl[:, c % 2], slab[:, c % RW], f32(wh[:, c % 2]), ALU.subtract).then_inc(lo_done, 1)

                    @block.vector
                    def _(dve):
                        def step(ins):
                            dve_chain(dve, ins)

                        def top16(vals, ids, src, tmp):
                            step(nc.vector.max(vals[:, 0:8], src))
                            nc.vector.max_index(ids[:, 0:8], vals[:, 0:8], src)
                            step(nc.vector.match_replace(tmp, vals[:, 0:8], src, NEG))
                            step(nc.vector.max(vals[:, 8:16], tmp))
                            return nc.vector.max_index(ids[:, 8:16], vals[:, 8:16], tmp)

                        for c in range(HP):
                            dve.wait_ge(s_ev, c + 1)
                            for t in range(nt):
                                last = top16(top[:, t, c], idx[:, t, c], s_sb[:, c % 2, t], s2[:, 0:NKEY])
                            last.then_inc(s_used, 1)
                        dve.wait_ge(s_used, HP)
                        step(nc.vector.tensor_copy(idf[:], idx[:]))
                        for t in range(nt):
                            a = top[:, t].rearrange("p (h two) k -> p h two k", two=2)
                            f = idf[:, t].rearrange("p (h two) k -> p h two k", two=2)
                            step(nc.vector.tensor_tensor(cand[:], bc(a[:, :, 0], 3, TOPK), bc(a[:, :, 1], 2, TOPK), ALU.add))
                            for h in range(PH):
                                last = top16(best[:, h], sel[:, h], cand[:, h].rearrange("p a b -> p (a b)"), s2[:])
                            step(last)
                            nc.vector.tensor_copy(esum[:], best[:, :, 0])
                            step(nc.vector.tensor_copy(s2[:, 0:PH], best[:, :, 0]))
                            nc.vector.tensor_tensor(best[:], best[:], bc(s2[:, 0:PH], 2, TOPK), ALU.subtract).then_inc(b_done, 1)
                            flat = sel[:].rearrange("p h k -> p (h k)")
                            nc.vector.tensor_scalar(sela[:, 0], flat, 4, None, ALU.logical_shift_right)
                            step(nc.vector.tensor_scalar(sela[:, 1], flat, 15, None, ALU.bitwise_and))
                            step(nc.vector.tensor_copy(self_[:], sela[:]))
                            r = t % 2
                            for j in range(2):
                                step(nc.vector.tensor_tensor(eq[:], bc(self_[:, j], 2, TOPK), bc(iota[:, 0:TOPK], 1, PH * TOPK), ALU.is_equal))
                                e4 = eq[:].rearrange("p (h k) a -> p h k a", h=PH)
                                step(nc.vector.tensor_tensor(e4, e4, bc(f[:, :, j], 2, TOPK), ALU.mult))
                                step(nc.vector.tensor_reduce(ijg[:, r, j], eq[:], AX, ALU.add))
                            dve.wait_ge(x_done, t + 1)
                            step(nc.vector.tensor_reduce(esum[:], best[:], AX, ALU.add))
                            step(nc.vector.reciprocal(esum[:], esum[:]))
                            g3 = ijg[:, r, 2].rearrange("p (h k) -> p h k", h=PH)
                            nc.vector.tensor_tensor(g3, best[:], bc(esum[:], 2, TOPK), ALU.mult).then_inc(tr_in, 1)
                            dve.wait_ge(tr_mm, t + 1)
                            cols = slice(t * P, (t + 1) * P)
                            nc.vector.tensor_copy(iT[:, cols], ps[:, 4, 0:P])
                            nc.vector.tensor_copy(jT[:, cols], ps[:, 4, P:2 * P])
                            nc.vector.tensor_copy(gT[:, cols], ps[:, 4, 2 * P:3 * P]).then_inc(tr_ev, 1)

        def phase_dense(l, lo, iT, jT, gT):
            n = T - lo
            U = 16
            UB = 4
            a_done, b_done, g_mm, g_ev = (sem(f"dense_{x}{l}") for x in ("a", "b", "mm", "ev"))
            stored = [sem(f"dense_stored{l}_{r}") for r in range(2)]
            with ExitStack() as st:
                hot_i = sb(st, f"hot_i{l}", [P, 2, U, NKEY])
                hot_j = sb(st, f"hot_j{l}", [P, 2, U, NKEY])
                stage = sb(st, f"dense_stage{l}", [P, 2, NKEY, TB])
                with nc.Block() as block:
                    @block.vector
                    def _(dve):
                        def body(it, first):
                            for q in range(UB):
                                u = UB * it + q
                                r = q % 2
                                if not (first and q < 2):
                                    dve.wait_ge(g_mm, u - 1)
                                nc.vector.tensor_tensor(hot_j[:, r], bc(jT[:, bass.ds(u * U, U)], 2, NKEY),
                                                        bc(iota[:], 1, U), ALU.is_equal).then_inc(b_done, 1)
                                for t in range(U):
                                    at = bass.ds(u * U + t, 1)
                                    last = nc.vector.tensor_scalar(hot_i[:, r, t], iota[:], iT[:, at], gT[:, at],
                                                                   ALU.is_equal, ALU.mult)
                                last.then_inc(a_done, 1)
                        body(0, True)
                        with dve.Fori(1, n // (U * UB)) as it:
                            body(it, False)

                    @block.tensor
                    def _(pe):
                        def body(it, first):
                            for q in range(UB):
                                u = UB * it + q
                                r = q % 2
                                pe.wait_ge(b_done, u + 1)
                                pe.wait_ge(a_done, u + 1)
                                if not (first and q < 2):
                                    pe.wait_ge(g_ev, u - 1)
                                for t in range(U):
                                    mm = nc.tensor.matmul(ps[:, 4 * r + t // 4, (t % 4) * P:(t % 4 + 1) * P],
                                                          hot_j[:, r, t], hot_i[:, r, t], start=True, stop=True)
                                mm.then_inc(g_mm, 1)
                        body(0, True)
                        with pe.Fori(1, n // (U * UB)) as it:
                            body(it, False)

                    @block.scalar
                    def _(act):
                        def body(it, first):
                            for q in range(UB):
                                u = UB * it + q
                                act.wait_ge(g_mm, u + 1)
                                if q % 2 == 0 and not first:
                                    act.wait_ge(stored[q // 2], 16 * it)
                                got = ps[:, 4 * (q % 2):4 * (q % 2) + 4, :].rearrange("p b (t i) -> p i (b t)", i=NKEY)
                                o = (q % 2) * U
                                nc.scalar.activation(stage[:, q // 2, :, o:o + U], got, ACT.Copy).then_inc(g_ev, 1)
                        body(0, True)
                        with act.Fori(1, n // (U * UB)) as it:
                            body(it, False)

                    @block.sync
                    def _(sp):
                        with sp.Fori(0, n // (U * UB)) as it:
                            for r in range(2):
                                sp.wait_ge(g_ev, UB * it + 2 * r + 2)
                                sp.dma_start(gates_dram[bass.ds(2 * it + r, 1)].rearrange("a p i t -> p (a i) t"),
                                             stage[:, r]).then_inc(stored[r], 16)
                        for r in range(2):
                            sp.wait_ge(stored[r], 16 * (n // (U * UB)))

        def phase_peer(l, lo, hp, gates_dram):
            n = T - lo
            ntb = n // TB
            ITE = 8
            NIT = NKEY // ITE
            CPS = DC * 1 // GE
            OB = 4
            u_in = [sem(f"peer_u_in{l}_{r}") for r in range(2)]
            v_in = [sem(f"peer_v_in{l}_{r}") for r in range(2)]
            g_in = [sem(f"peer_g_in{l}_{r}") for r in range(2)]
            (uhi, ulo, vhi, vlo, whi, wlo, act_mm, gelu_done, w_done, out_mm, x_done) = (
                sem(f"peer_{x}{l}") for x in ("uhi", "ulo", "vhi", "vlo", "whi", "wlo", "act_mm", "gelu", "w", "out_mm", "x"))
            with ExitStack() as st:
                us = sb(st, f"peer_u{l}", [P, 2, DC, GE * P])
                uh = sb(st, f"peer_uh{l}", [P, 2, DC, P], F32R)
                ul = sb(st, f"peer_ul{l}", [P, 2, DC, P], F32R)
                vs = sb(st, f"peer_v{l}", [P, 2, GE, D_MODEL])
                vh = sb(st, f"peer_vh{l}", [P, 2, GE, D_MODEL], F32R)
                vl = sb(st, f"peer_vl{l}", [P, 2, GE, D_MODEL], F32R)
                gs = sb(st, f"peer_gates{l}", [P, 2, ntb, GROWS, TB])
                ga = sb(st, f"peer_act{l}", [P, 2, n])
                wt = sb(st, f"peer_wt{l}", [P, 2, n])
                wh = sb(st, f"peer_wh{l}", [P, 2, GE, n], F32R)
                wl = sb(st, f"peer_wl{l}", [P, 2, GE, n], F32R)

                with nc.Block() as block:
                    @block.sync
                    def _(sp):
                        def body(it, first):
                            for g in range(ITE // GE):
                                gg = (ITE // GE) * it + g
                                if g % 2 == 0:
                                    r = g // 2
                                    if not first:
                                        sp.wait_ge(w_done, GROWS * (2 * it + r - 1))
                                    src = gates_dram[0:ntb, :, bass.ds(GROWS * (2 * it + r), GROWS), :].rearrange("b p i t -> p b (i t)")
                                    sp.dma_start(gs[:, r].rearrange("p b i t -> p b (i t)"), src).then_inc(g_in[r], 16)
                                if not (first and g < 2):
                                    sp.wait_ge(ulo, GE * (gg - 1))
                                sp.dma_start(us[:, g % 2], d["uT"][l, bass.ds(gg, 1)].rearrange("a p k e -> p (a k) e")).then_inc(u_in[g % 2], 16)
                                if not (first and g < 2):
                                    sp.wait_ge(vlo, GE * (gg - 1))
                                sp.dma_start(vs[:, g % 2], d["v"][l, bass.ds(gg, 1)].rearrange("a p j n -> p (a j) n")).then_inc(v_in[g % 2], 16)
                        body(0, True)
                        with sp.Fori(1, NIT) as it:
                            body(it, False)

                    @block.gpsimd
                    def _(pool):
                        def body(it):
                            for e in range(ITE):
                                pool.wait_ge(uhi, ITE * it + e + 1)
                                src = us[:, (e // GE) % 2, :, (e % GE) * P:(e % GE + 1) * P]
                                nc.gpsimd.tensor_tensor(ul[:, e % 2], src, f32(uh[:, e % 2]), ALU.subtract).then_inc(ulo, 1)
                        with pool.Fori(0, NIT) as it:
                            body(it)

                    @block.tensor
                    def _(pe):
                        def outputs(g, r, j, first):
                            if j == 0:
                                pe.wait_ge(vlo, GE * (g + 1))
                                pe.wait_ge(wlo, GE * (g + 1))
                            for c in range(CPS * j, CPS * (j + 1)):
                                if not (first and c < OB):
                                    pe.wait_ge(x_done, DC * g + c - OB + 1)
                                for q in range(GE):
                                    mm = product(nc, ps[:, 2 + c % OB, 0:n], (vh[:, r, q, c * P:(c + 1) * P], vl[:, r, q, c * P:(c + 1) * P]),
                                                 (wh[:, r, q, :], wl[:, r, q, :]), q == 0, q == GE - 1)
                                mm.then_inc(out_mm, 1)

                        def body(it, first):
                            for e in range(ITE):
                                eg = ITE * it + e
                                pe.wait_ge(ulo, eg + 1)
                                if not (first and e < 2):
                                    pe.wait_ge(gelu_done, eg - 1)
                                for k in range(DC):
                                    mm = product(nc, ps[:, e % 2, 0:n], (uh[:, e % 2, k, :], ul[:, e % 2, k, :]),
                                                 (hp[0][:, k, :], hp[1][:, k, :]), k == 0, k == DC - 1)
                                mm.then_inc(act_mm, 1)
                                g = e // GE
                                if not (first and g == 0):
                                    outputs((ITE // GE) * it + g - 1, (g + 1) % 2, e % GE, first and g == 1)
                        body(0, True)
                        with pe.Fori(1, NIT) as it:
                            body(it, False)
                        for j in range(GE):
                            outputs(NG - 1, (NG - 1) % 2, j, False)

                    @block.scalar
                    def _(act):
                        def finish(eg, e, first):
                            act.wait_ge(act_mm, eg + 1)
                            if not (first and e < 2):
                                act.wait_ge(w_done, eg - 1)
                            nc.scalar.activation(ga[:, e % 2], ps[:, e % 2, 0:n], ACT.Gelu_apprx_tanh).then_inc(gelu_done, 1)
                            act.wait_ge(w_done, eg + 1)
                            nc.scalar.activation(wh[:, (e // GE) % 2, e % GE], wt[:, e % 2], ACT.Copy).then_inc(whi, 1)

                        def body(it, first):
                            for e in range(ITE):
                                eg = ITE * it + e
                                g = e // GE
                                loads = 2 * it + g // 2 + 1
                                if e % GE == 0:
                                    act.wait_ge(u_in[g % 2], 16 * loads)
                                if not (first and e < 2):
                                    act.wait_ge(act_mm, eg - 1)
                                nc.scalar.activation(uh[:, e % 2], us[:, g % 2, :, (e % GE) * P:(e % GE + 1) * P], ACT.Copy).then_inc(uhi, 1)
                                if not (first and e == 0):
                                    finish(eg - 1, (e - 1) % ITE, first)
                                if e % GE == 0:
                                    act.wait_ge(v_in[g % 2], 16 * loads)
                                    if not (first and g < 2):
                                        act.wait_ge(out_mm, DC * ((ITE // GE) * it + g - 1))
                                nc.scalar.activation(vh[:, g % 2, e % GE], vs[:, g % 2, e % GE], ACT.Copy).then_inc(vhi, 1)
                        body(0, True)
                        with act.Fori(1, NIT) as it:
                            body(it, False)
                        finish(NKEY - 1, ITE - 1, False)

                    @block.vector
                    def _(dve):
                        def add_outputs(g, j, first):
                            for c in range(CPS * j, CPS * (j + 1)):
                                dve.wait_ge(out_mm, DC * g + c + 1)
                                if c == 0 and not first:
                                    dve.wait_ge(x_done, DC * g)
                                add_gated(c, 5, ps[:, 2 + c % OB, :], lo).then_inc(x_done, 1)

                        def finish(it, eg, e, first):
                            g = e // GE
                            if e % GROWS == 0:
                                dve.wait_ge(g_in[e // GROWS], 16 * (it + 1))
                            dve.wait_ge(gelu_done, eg + 1)
                            if not (first and e < 2):
                                dve.wait_ge(wlo, eg - 1)
                            nc.vector.tensor_tensor(wt[:, e % 2].rearrange("p (b t) -> p b t", t=TB), ga[:, e % 2].rearrange("p (b t) -> p b t", t=TB),
                                                    gs[:, e // GROWS, :, e % GROWS, :], ALU.mult).then_inc(w_done, 1)
                            dve.wait_ge(whi, eg + 1)
                            nc.vector.tensor_tensor(wl[:, g % 2, e % GE], wt[:, e % 2], f32(wh[:, g % 2, e % GE]), ALU.subtract).then_inc(wlo, 1)
                            if not (first and g == 0):
                                add_outputs((ITE // GE) * it + g - 1, e % GE, first and g == 1)

                        def body(it, first):
                            for e in range(ITE):
                                eg = ITE * it + e
                                if not (first and e == 0):
                                    if e == 0:
                                        finish(it - 1, eg - 1, ITE - 1, False)
                                    else:
                                        finish(it, eg - 1, e - 1, first)
                                dve.wait_ge(vhi, eg + 1)
                                g = e // GE
                                nc.vector.tensor_tensor(vl[:, g % 2, e % GE], vs[:, g % 2, e % GE], f32(vh[:, g % 2, e % GE]), ALU.subtract).then_inc(vlo, 1)
                        body(0, True)
                        with dve.Fori(1, NIT) as it:
                            body(it, False)
                        finish(NIT - 1, NKEY - 1, ITE - 1, False)
                        for j in range(GE):
                            add_outputs(NG - 1, j, False)

        phase_start()
        for l in range(DEPTH):
            last_layer = l == DEPTH - 1
            lo = CTX if last_layer else 0
            phase_ada(l)
            with ExitStack() as st:
                mix = sb(st, f"mix{l}", [P, DC, T])
                with ExitStack() as st1:
                    fm = sb(st1, f"fm{l}", [P, FM, T])
                    tm = sb(st1, f"tm{l}", [P, TT, TMC])
                    with ExitStack() as st2:
                        hp = [sb(st2, f"h_{x}{l}", [P, DC, T], F32R) for x in ("hi", "lo")]
                        phase_norm(f"norm_mix{l}", d["norm_mix_g"][l], 0, 0, mix, hp)
                        phase_proj(l, lo, hp, fm, tm)
                    with ExitStack() as st2:
                        hk = sb(st2, f"hk{l}", [P, 4, T])
                        cum = sb(st2, f"cum{l}", [P, 6, TT, P + 1])
                        phase_gates(l, fm, hk, cum)
                        phase_scan(l, lo, fm, tm, hk, cum, mix)
                    phase_attn(l, lo, fm, tm, mix)
                    phase_post(l, lo, fm, mix)
                phase_out(l, lo, mix)
            with ExitStack() as st:
                hp = [sb(st, f"h2_{x}{l}", [P, DC, T - lo], F32R) for x in ("hi", "lo")]
                with ExitStack() as st1:
                    h2 = sb(st1, f"h2{l}", [P, DC, T])
                    phase_norm(f"norm_ffn{l}", d["norm_ffn_g"][l], 3, lo, h2, hp)
                with ExitStack() as st1:
                    iT, jT, gT = (sb(st1, f"{x}T{l}", [P, T - lo]) for x in "ijg")
                    phase_route(l, lo, hp, iT, jT, gT)
                    phase_dense(l, lo, iT, jT, gT)
                phase_peer(l, lo, hp, gates_dram)
            clear_layer_sems()
        with ExitStack() as st:
            y = sb(st, "y", [P, DC, T])
            phase_norm("norm_final", d["final_norm_g"], None, CTX, y)
            stored = sem("stored")
            with nc.Block() as block:
                @block.sync
                def _(sp):
                    sp.dma_start(out, y[:, :, CTX:T]).then_inc(stored, 16)
                    sp.wait_ge(stored, 16)


def constants():
    c = {}
    c["ident"] = np.eye(P, dtype=np.float32)
    c["iota"] = np.tile(np.arange(P, dtype=np.float32), (P, 1))
    c["mean64"] = np.kron(np.eye(2), np.full((64, 64), 1.0 / 64)).astype(np.float32)
    f = np.arange(P)
    partner = (f // 16) * 16 + (f + 8) % 16
    rotp = np.zeros((P, P), np.float32)
    rotp[partner, f] = 1.0
    c["rotp"] = rotp
    freqs = np.float32(ROPE_BASE) ** (-np.arange(8, dtype=np.float32) / np.float32(8))
    n = np.arange(SEQ)
    pos = np.stack([n // GRID_W, n % GRID_W]).astype(np.float32)
    ang = (pos[(f // 16) % 2] * freqs[f % 8][:, None]).astype(np.float32)
    c["cosT"] = np.cos(ang).astype(np.float32)
    c["sinT"] = (np.sin(ang) * np.where(f % 16 < 8, -1.0, 1.0)[:, None]).astype(np.float32)
    mask = np.zeros((P, 2 * NL, HALF), np.int32)
    s = np.arange(P)[:, None]
    for dr in range(2):
        for i, L in enumerate(LEVELS):
            j = np.arange(HALF)[None, :]
            mask[:, NL * dr + i] = (s // (2 * L) == j // L) & ((s // L) % 2 == dr)
    c["mask"] = mask
    c["maskd"] = np.eye(P, dtype=np.int32)
    return c


def lay_out(x, c, ctx, c_ctx, ada_w, ada_b, norm_mix_g, norm_ffn_g, w_in, w_out,
            gla_gate_w, gla_gate_b, gla_norm_g, hgrn_lb_raw, hgrn_norm_g,
            mla_q_norm_g, mla_kv_norm_g, mla_w_uq, mla_w_ukv, diff_lambda, diff_norm_g,
            peer_wq, peer_keys, peer_u, peer_v, final_norm_g):
    a = constants()
    cols = lambda v: np.swapaxes(v.reshape(*v.shape[:-1], -1, P), -1, -2)
    tokens = np.concatenate([ctx[0], x[0]], axis=0)
    a["xT"] = tokens.T.reshape(DC, P, T).transpose(1, 0, 2)
    a["cvec"] = np.stack([c[0], c_ctx], axis=-1).reshape(DC, P, 2).transpose(1, 0, 2)
    a["ada_w"], a["ada_b"] = ada_w, cols(ada_b)
    a["norm_mix_g"], a["norm_ffn_g"], a["final_norm_g"] = cols(norm_mix_g), cols(norm_ffn_g), cols(final_norm_g)
    g, h, m, f = 0, 800, 2080, 2432
    fm_cols = [(g + 512, 256), (h + 512, 256), (h, 256), (g, 128), (g + 128, 128), (h + 768, 512),
               (m, 192), (m + 320, 32), (g + 768, 32), (m + 192, 128), (f, 512)]
    tm_cols = [(g + 256, 256), (h + 256, 256), (f + 512, 256)]
    w = np.concatenate([w_in[:, :, o:o + n] for o, n in fm_cols], axis=-1)
    a["w_fm"] = w.reshape(DEPTH, DC, P, FM, P).transpose(0, 3, 2, 1, 4)
    w = np.concatenate([w_in[:, :, o:o + n] for o, n in tm_cols], axis=-1)
    a["w_tm"] = w.reshape(DEPTH, DC, P, TMC).transpose(0, 2, 1, 3)
    a["w_out"] = w_out.reshape(DEPTH, DC, P, DC, P).transpose(0, 3, 2, 1, 4)
    zero = np.zeros_like(gla_gate_w[:, 0])
    a["gate_w"] = np.concatenate([np.stack([gla_gate_w[:, 0], zero], axis=2),
                                  np.stack([zero, gla_gate_w[:, 1]], axis=2)], axis=1)
    a["gate_b"] = gla_gate_b.transpose(0, 2, 1)
    a["lb_raw"] = cols(hgrn_lb_raw).transpose(1, 0, 2)
    a["g_head"] = np.stack([np.tile(v, (1, 2)) for v in (gla_norm_g, hgrn_norm_g, diff_norm_g)], axis=-1)
    a["g_q0"], a["g_q1"] = mla_q_norm_g[:, 0:P, None], mla_q_norm_g[:, P:, None]
    a["g_kv"] = mla_kv_norm_g[:, :, None]
    a["w_uq"] = mla_w_uq.reshape(DEPTH, MLA_Q, HEADS, MLA_DQ)
    a["w_ukv"] = mla_w_ukv.reshape(DEPTH, MLA_KV, HEADS, P)
    a["lam"] = diff_lambda
    a["w_pq"] = peer_wq.reshape(DEPTH, DC, P, 2 * PH, P).transpose(0, 3, 2, 1, 4)
    a["keysT"] = peer_keys.reshape(DEPTH, 2 * PH, NKEY, P).transpose(0, 3, 1, 2)
    a["uT"] = peer_u.reshape(DEPTH, NG, GE * P, DC, P).transpose(0, 1, 4, 3, 2)
    a["v"] = peer_v.reshape(DEPTH, NG, GE, P, D_MODEL).transpose(0, 1, 3, 2, 4)
    return a


def kernel(**inputs):
    import concourse.bacc as _bacc
    from concourse.bass_utils import run_bass_kernel_spmd as _run

    nc = _bacc.Bacc("TRN2", target_bir_lowering=False, num_devices=1)
    arrays, d = {}, {}
    for name, a in lay_out(**{k: np.asarray(v) for k, v in inputs.items()}).items():
        a = np.ascontiguousarray(a)
        arrays[f"in_{name}"] = a
        d[name] = nc.dram_tensor(f"in_{name}", a.shape, mybir.dt.from_np(a.dtype), kind="ExternalInput").ap()
    out = nc.dram_tensor("out_yT", (P, DC, SEQ), F32, kind="ExternalOutput").ap()
    build(nc, d, out)
    r = _run(nc, [arrays], core_ids=[0])
    y = r.results[0]["out_yT"]
    return y.transpose(2, 1, 0).reshape(1, SEQ, D_MODEL)
```

```python
from contextlib import ExitStack
import math

import numpy as np

import concourse.bass as bass
from concourse import mybir

F32 = mybir.dt.float32
F32R = mybir.dt.float32r
U32 = mybir.dt.uint32
I32 = mybir.dt.int32
ALU = mybir.AluOpType
ACT = mybir.ActivationFunctionType
AX = mybir.AxisListType.X

P = 128
BANK = 512
EPS = 1e-6
D_MODEL = 1024
DC = D_MODEL // P
CTX = 256
SEQ = 256
T = CTX + SEQ
TT = T // P
DEPTH = 2
GRID_W = 64
ROPE_BASE = 10000.0

GLA_DK = 32
GLA_GATE_NORM = 16.0
HG_CHUNKS = 2
LB_FLOOR = 1e-30
DV = 64
HEADS = 4
MLA_Q, MLA_KV, MLA_NOPE, MLA_ROPE = 192, 128, 64, 32
MLA_DQ = MLA_NOPE + MLA_ROPE
DIFF_DQK = 32

GATE0 = 0
HQ = 4
GQ, GK = 6, 7
HZ = 8
CQ0, CQ1, CKV = 12, 13, 14
DQ, DK = 15, 17
FM = 19
SILU_CHUNKS = 6
TMC = 3 * HEADS * DV
KR0, GZ0 = 64, 96

LEVELS = [64, 32, 16, 8, 4, 2, 1]
NL = len(LEVELS)
HALF = P // 2
UNITS = [((0, 0), (0, 1)), ((0, 2), (0, 3)), ((0, 4), (0, 5)), ((0, 6), (1, 6)),
         ((1, 0), (1, 1)), ((1, 2), (1, 3)), ((1, 4), (1, 5)), None]
NU = len(UNITS)
XQ_TILES = [(1, 3, 2, 3), (0, 2, 2, 3)]
XK_TILES = [(0, 2, 0, 1), (1, 3, 0, 1)]

PH = 8
NKEY = 128
TOPK = 16
GE = 2
NG = NKEY // GE
GROWS = 4
TB = 32
NEG = -3.0e38
SMALL = 2.0 ** -40
UP = 2.0 ** 60


class Chain:

    def __init__(self, sem):
        self.sem, self.n = sem, 0

    def mark(self, ins):
        self.n += 1
        ins.then_inc(self.sem, 1)
        return self.n

    def __call__(self, eng, ins):
        eng.wait_ge(self.sem, self.mark(ins))


def f32(ap):
    return ap.bitcast(F32)


def product(nc, out, w, x, start, stop):
    nc.tensor.matmul(out, w[0], x[0], start=start, stop=False)
    nc.tensor.matmul(out, w[0], x[1], start=False, stop=False)
    return nc.tensor.matmul(out, w[1], x[0], start=False, stop=stop)


def bc(ap, axis, n):
    ap = ap.unsqueeze(axis)
    shape = list(ap.shape)
    shape[axis] = n
    return ap.to_broadcast(shape)


def halves(ap, L, side):
    return ap.rearrange("p a (n two l) -> p a n two l", two=2, l=L)[:, :, :, side, :]


def mids(ap, L):
    ap = halves(ap, L, 1)[:, :, :, 0:1]
    return ap.to_broadcast([P, ap.shape[1], HALF // L, L])


def build(nc, d, out):
    ctx = ExitStack()

    layer_sems = []

    def sem(name):
        layer_sems.append(nc.alloc_semaphore(name=name))
        return layer_sems[-1]

    def clear_layer_sems():
        nc.clear_and_free_semaphores(layer_sems)
        layer_sems.clear()
        nc.all_engine_barrier()

    def sb(st, name, shape, dt=F32):
        return st.enter_context(nc.sbuf_tensor(name, shape, dt))

    with ctx:
        ps = ctx.enter_context(nc.psum_tensor("ps", [P, 8, BANK], F32))
        xT = sb(ctx, "xT", [P, DC, T])
        mods = [sb(ctx, f"mod{l}", [P, 6 * DC, 2]) for l in range(DEPTH)]
        ident = sb(ctx, "ident", [P, P])
        ones = sb(ctx, "ones", [P, P])
        meanD = sb(ctx, "meanD", [P, P])
        mean64 = sb(ctx, "mean64", [P, P])
        rotp = sb(ctx, "rotp", [P, P])
        cosT = sb(ctx, "cosT", [P, SEQ])
        sinT = sb(ctx, "sinT", [P, SEQ])
        mask = sb(ctx, "mask", [P, 2 * NL, HALF], I32)
        maskd = sb(ctx, "maskd", [P, P], I32)
        iota = sb(ctx, "iota", [P, P])
        gates_dram = nc.dram_tensor("peer_gates", (T // TB, P, NKEY, TB), F32, kind="Internal").ap()
        cvec = sb(ctx, "cvec", [P, DC, 2])
        silu_c = sb(ctx, "silu_c", [P, DC, 2])
        onecol = sb(ctx, "onecol", [P, 1])
        epscol = sb(ctx, "epscol", [P, 1])
        dve_chain = Chain(ctx.enter_context(nc.semaphore("dve_chain")))

        def phase_start():
            loaded = sem("consts_loaded")
            c_in = sem("c_in")
            const = [(xT, d["xT"]), (ident, d["ident"]), (mean64, d["mean64"]), (rotp, d["rotp"]),
                     (cosT, d["cosT"]), (sinT, d["sinT"]), (mask, d["mask"]), (maskd, d["maskd"]), (iota, d["iota"])]
            with nc.Block() as block:
                @block.sync
                def _(sp):
                    sp.dma_start(cvec[:], d["cvec"]).then_inc(c_in, 16)
                    for dst, src in const:
                        sp.dma_start(dst[:], src).then_inc(loaded, 16)
                    sp.wait_ge(loaded, 16 * len(const))

                @block.vector
                def _(dve):
                    nc.vector.memset(ones[:], 1.0)
                    nc.vector.memset(meanD[:], 1.0 / D_MODEL)
                    nc.vector.memset(onecol[:], 1.0)
                    nc.vector.memset(epscol[:], EPS)

                @block.scalar
                def _(act):
                    act.wait_ge(c_in, 16)
                    nc.scalar.activation(silu_c[:], cvec[:], ACT.Silu)

        class AdaPart:

            def __init__(self, st, l, first, n, banks):
                self.l, self.first, self.n, self.banks = l, first, n, banks
                tag = f"ada{l}_{first}"
                self.slab_in = [sem(f"{tag}_slab_in{r}") for r in range(2)]
                self.bias_in, self.row_mm, self.row_ev, self.col_mm = (
                    sem(f"{tag}_{x}") for x in ("bias_in", "row_mm", "row_ev", "col_mm"))
                self.slab = sb(st, f"{tag}_slab", [P, 2, DC, BANK])
                self.bias = sb(st, f"{tag}_bias", [P, 4 * n])
                self.row = sb(st, f"{tag}_row", [2, n, BANK])

            def load(self, sp, i):
                c = self.first + i
                if i == 0:
                    sp.dma_start(self.bias[:], d["ada_b"][self.l, :, 4 * c:4 * (c + self.n)]).then_inc(self.bias_in, 16)
                if i >= 2:
                    sp.wait_ge(self.row_mm, i - 1)
                src = d["ada_w"][self.l, :, c * BANK:(c + 1) * BANK].rearrange("(k p) n -> p k n", p=P)
                sp.dma_start(self.slab[:, i % 2], src).then_inc(self.slab_in[i % 2], 16)

            def rows(self, pe, i):
                pe.wait_ge(self.slab_in[i % 2], 16 * (i // 2 + 1))
                if i >= 2:
                    pe.wait_ge(self.row_ev, i - 1)
                for k in range(DC):
                    mm = nc.tensor.matmul(ps[0:2, self.banks[i % 2], :], silu_c[:, k, :], self.slab[:, i % 2, k, :],
                                          start=(k == 0), stop=(k == DC - 1))
                mm.then_inc(self.row_mm, 1)
                if i:
                    self.columns(pe, i - 1)

            def columns(self, pe, i):
                pe.wait_ge(self.row_ev, i + 1)
                for j in range(4):
                    o = 2 * (4 * i + j)
                    mm = nc.tensor.transpose(ps[:, self.banks[2], o:o + 2], self.row[0:2, i, j * P:(j + 1) * P], ident[0:2, 0:2])
                mm.then_inc(self.col_mm, 1)

            def evac(self, act, i):
                act.wait_ge(self.row_mm, i + 1)
                nc.scalar.activation(self.row[0:2, i, :], ps[0:2, self.banks[i % 2], :], ACT.Copy).then_inc(self.row_ev, 1)

            def add_bias(self, dve):
                dve.wait_ge(self.bias_in, 16)
                dve.wait_ge(self.col_mm, self.n)
                got = ps[:, self.banks[2], 0:8 * self.n].rearrange("p (n v) -> p n v", v=2)
                nc.vector.tensor_tensor(mods[self.l][:, 4 * self.first:4 * (self.first + self.n)], got, bc(self.bias[:], 2, 2), ALU.add)

        def phase_ada(l, first, n):
            with ExitStack() as st:
                ada = AdaPart(st, l, first, n, (0, 1, 2))
                with nc.Block() as block:
                    @block.sync
                    def _(sp):
                        for i in range(n):
                            ada.load(sp, i)

                    @block.tensor
                    def _(pe):
                        for i in range(n):
                            ada.rows(pe, i)
                        ada.columns(pe, n - 1)

                    @block.scalar
                    def _(act):
                        for i in range(n):
                            ada.evac(act, i)

                    @block.vector
                    def _(dve):
                        ada.add_bias(dve)

        def phase_norm(name, gain, mod, which, lo, dst, parts=None):
            n = T - lo
            g_in, sq_done, sum_done, scaled = (sem(f"{name}_{x}") for x in ("g_in", "sq_done", "sum_done", "scaled"))
            a_done, root_done, full_done, hi_done = (sem(f"{name}_{x}") for x in ("a_done", "root_done", "full_done", "hi_done"))
            plo = T - parts[0].shape[2] if parts else 0
            with ExitStack() as st:
                g = sb(st, f"{name}_g", [P, DC])
                amp = sb(st, f"{name}_amp", [P, DC, 2])
                rstd = sb(st, f"{name}_rstd", [P, T])

                def part(i, k):
                    return parts[i][:, k, lo - plo:T - plo]

                with nc.Block() as block:
                    @block.sync
                    def _(sp):
                        sp.dma_start(g[:], gain).then_inc(g_in, 16)

                    @block.scalar
                    def _(act):
                        for k in range(DC):
                            nc.scalar.activation(dst[:, k, lo:T], xT[:, k, lo:T], ACT.Square).then_inc(sq_done, 1)
                        act.wait_ge(sum_done, 1)
                        nc.scalar.activation(rstd[:, lo:T], ps[:, 0, 0:n], ACT.Sqrt, bias=epscol[:]).then_inc(root_done, 1)
                        if which is None:
                            return
                        act.wait_ge(a_done, 1)
                        for k in range(DC):
                            act.wait_ge(scaled, k // 2 + 1)
                            for v, (a, b) in enumerate(((lo, CTX), (max(lo, CTX), T))):
                                if a < b:
                                    w = 1 - v
                                    full = nc.scalar.activation(dst[:, k, a:b], dst[:, k, a:b], ACT.Identity,
                                                                bias=mod[:, which * DC + k, w:w + 1], scale=amp[:, k, w:w + 1])
                            full.then_inc(full_done, 1)

                    @block.tensor
                    def _(pe):
                        for k in range(DC):
                            pe.wait_ge(sq_done, k + 1)
                            mm = nc.tensor.matmul(ps[:, 0, 0:n], meanD[:], dst[:, k, lo:T],
                                                  start=(k == 0), stop=(k == DC - 1))
                        mm.then_inc(sum_done, 1)

                    @block.vector
                    def _(dve):
                        dve.wait_ge(g_in, 16)
                        if which is not None:
                            dve_chain(dve, nc.vector.tensor_scalar(
                                amp[:], mod[:, (which + 1) * DC:(which + 2) * DC, :], 1.0, None, ALU.add))
                            nc.vector.tensor_tensor(amp[:], amp[:], bc(g[:], 2, 2), ALU.mult).then_inc(a_done, 1)
                        dve.wait_ge(root_done, 1)
                        dve_chain(dve, nc.vector.reciprocal(rstd[:, lo:T], rstd[:, lo:T]))
                        if which is None:
                            for k in range(DC):
                                nc.vector.scalar_tensor_tensor(out=dst[:, k, lo:T], in0=xT[:, k, lo:T], scalar=g[:, k:k + 1],
                                                               in1=rstd[:, lo:T], op0=ALU.mult, op1=ALU.mult)
                            return
                        for k in range(0, DC, 2):
                            nc.vector.tensor_tensor(dst[:, k:k + 2, lo:T], xT[:, k:k + 2, lo:T],
                                                    bc(rstd[:, lo:T], 1, 2), ALU.mult).then_inc(scaled, 1)
                        for k in range(DC):
                            dve.wait_ge(full_done, k + 1)
                            nc.vector.tensor_copy(part(0, k), dst[:, k, lo:T]).then_inc(hi_done, 1)
                            if k % 2:
                                dve.wait_ge(hi_done, k + 1)
                                nc.vector.tensor_tensor(part(1, k), dst[:, k, lo:T], f32(part(0, k)), ALU.subtract)

                    @block.gpsimd
                    def _(pool):
                        if which is None:
                            return
                        for k in range(0, DC, 2):
                            pool.wait_ge(hi_done, k + 1)
                            nc.gpsimd.tensor_tensor(part(1, k), dst[:, k, lo:T], f32(part(0, k)), ALU.subtract)

        def phase_proj(l, lo, hp, fm, tm):
            RW = 4
            NT = 2 * TT
            w_in = [sem(f"proj_w_in{l}_{r}") for r in range(RW)]
            t_in = [sem(f"projt_w_in{l}_{r}") for r in range(2)]
            hi_done, lo_done, mm_done, ev_done, thi_done, tlo_done, tmm_done, tend = (
                sem(f"proj_{x}{l}") for x in ("hi", "lo", "mm", "ev", "thi", "tlo", "tmm", "tend"))
            own = [lo if c in (0, 1, 2, 3, HQ, HQ + 1, GQ, CQ0, DQ, DQ + 1) else 0 for c in range(FM)]
            with ExitStack() as st:
                slab = sb(st, f"proj_slab{l}", [P, RW, DC, P])
                wh = sb(st, f"proj_wh{l}", [P, 2, DC, P], F32R)
                wl = sb(st, f"proj_wl{l}", [P, 2, DC, P], F32R)
                tslab = sb(st, f"proj_tslab{l}", [P, 2, TMC])
                th = sb(st, f"proj_th{l}", [P, 2, TMC], F32R)
                tl = sb(st, f"proj_tl{l}", [P, 2, TMC], F32R)
                with nc.Block() as block:
                    @block.sync
                    def _(sp):
                        for c in range(FM):
                            if c >= RW:
                                sp.wait_ge(lo_done, c - RW + 1)
                            sp.dma_start(slab[:, c % RW], d["w_fm"][l, c]).then_inc(w_in[c % RW], 16)
                        for k in range(DC):
                            if k >= 2:
                                sp.wait_ge(tlo_done, k - 1)
                            sp.dma_start(tslab[:, k % 2], d["w_tm"][l, :, k, :]).then_inc(t_in[k % 2], 16)

                    @block.tensor
                    def _(pe):
                        for c in range(FM):
                            pe.wait_ge(lo_done, c + 1)
                            if c >= 4:
                                pe.wait_ge(ev_done, c - 3)
                            a = own[c]
                            for k in range(DC):
                                mm = product(nc, ps[:, c % 4, 0:T - a], (wh[:, c % 2, k, :], wl[:, c % 2, k, :]),
                                             (hp[0][:, k, a:T], hp[1][:, k, a:T]), k == 0, k == DC - 1)
                            mm.then_inc(mm_done, 1)
                        pe.wait_ge(ev_done, FM)
                        for k in range(DC):
                            pe.wait_ge(tlo_done, k + 1)
                            for n in range(NT):
                                cols = slice((n % 2) * TMC // 2, (n % 2 + 1) * TMC // 2)
                                t = slice((n // 2) * P, (n // 2 + 1) * P)
                                mm = product(nc, ps[:, n, 0:TMC // 2], (hp[0][:, k, t], hp[1][:, k, t]),
                                             (th[:, k % 2, cols], tl[:, k % 2, cols]), k == 0, k == DC - 1)
                                if k == DC - 1:
                                    mm.then_inc(tend, 1)
                            if k < DC - 1:
                                mm.then_inc(tmm_done, 1)

                    @block.scalar
                    def _(act):
                        def evac(c):
                            act.wait_ge(mm_done, c + 1)
                            a = own[c]
                            nc.scalar.activation(fm[:, c, a:T], ps[:, c % 4, 0:T - a], ACT.Silu if c < SILU_CHUNKS else ACT.Copy,
                                                 scale=GLA_DK ** -0.5 if c == GQ else 1.0).then_inc(ev_done, 1)
                        for c in range(FM):
                            act.wait_ge(w_in[c % RW], 16 * (c // RW + 1))
                            if c >= 2:
                                act.wait_ge(mm_done, c - 1)
                            nc.scalar.activation(wh[:, c % 2], slab[:, c % RW], ACT.Copy).then_inc(hi_done, 1)
                            if c:
                                evac(c - 1)
                        evac(FM - 1)
                        for k in range(DC):
                            act.wait_ge(t_in[k % 2], 16 * (k // 2 + 1))
                            if k >= 2:
                                act.wait_ge(tmm_done, k - 1)
                            nc.scalar.activation(th[:, k % 2], tslab[:, k % 2], ACT.Copy).then_inc(thi_done, 1)

                    @block.vector
                    def _(dve):
                        for c in range(FM):
                            dve.wait_ge(hi_done, c + 1)
                            nc.vector.tensor_tensor(wl[:, c % 2], slab[:, c % RW], f32(wh[:, c % 2]), ALU.subtract).then_inc(lo_done, 1)
                        for k in range(DC):
                            dve.wait_ge(thi_done, k + 1)
                            nc.vector.tensor_tensor(tl[:, k % 2], tslab[:, k % 2], f32(th[:, k % 2]), ALU.subtract).then_inc(tlo_done, 1)
                        for n in range(NT):
                            dve.wait_ge(tend, n + 1)
                            cols = slice((n % 2) * TMC // 2, (n % 2 + 1) * TMC // 2)
                            nc.vector.tensor_copy(tm[:, n // 2, cols], ps[:, n, 0:TMC // 2])

        def phase_gates(l, fm, hk, cum, ada_part):
            loaded, z_done, e_ready, e_done, f_ready, l_done = (
                sem(f"gates_{x}{l}") for x in ("loaded", "z_done", "e_ready", "e_done", "f_ready", "l_done"))
            with ExitStack() as st:
                lg = sb(st, f"lg{l}", [P, 6, T])
                e = sb(st, f"gate_e{l}", [P, 4, T])
                r = sb(st, f"gate_r{l}", [P, 4, T])
                m = sb(st, f"gate_m{l}", [P, 4, T])
                a = sb(st, f"gate_a{l}", [P, 2, T])
                ea = sb(st, f"gate_ea{l}", [P, 2, T])
                wg = sb(st, f"gate_w{l}", [P, 2, P])
                bg = sb(st, f"gate_b{l}", [P, 2])
                lbr = sb(st, f"lb_raw{l}", [P, DEPTH, HG_CHUNKS])
                lbe = sb(st, f"lb_exp{l}", [P, DEPTH, HG_CHUNKS])
                lbs = sb(st, f"lb_sum{l}", [P, 4, HG_CHUNKS])
                ada = AdaPart(st, *ada_part, (2, 3, 4)) if ada_part else None
                with nc.Block() as block:
                    @block.sync
                    def _(sp):
                        sp.dma_start(wg[GZ0:P], d["gate_w"][l]).then_inc(loaded, 16)
                        sp.dma_start(bg[:], d["gate_b"][l]).then_inc(loaded, 16)
                        sp.dma_start(lbr[:], d["lb_raw"]).then_inc(loaded, 16)
                        if ada:
                            for i in range(ada.n):
                                ada.load(sp, i)

                    @block.tensor
                    def _(pe):
                        pe.wait_ge(loaded, 48)
                        for k in range(2):
                            nc.tensor.matmul(ps[:, k, :], wg[GZ0:P, k, :], fm[GZ0:P, CQ1, :],
                                             start=True, stop=True).then_inc(z_done, 1)
                        if ada:
                            for i in range(ada.n):
                                ada.rows(pe, i)
                            ada.columns(pe, ada.n - 1)

                    @block.scalar
                    def _(act):
                        act.wait_ge(e_ready, 1)
                        nc.scalar.activation(lbe[:], lbe[:], ACT.Exp).then_inc(e_done, 1)
                        act.wait_ge(e_ready, 2)
                        nc.scalar.activation(e[:], e[:], ACT.Exp).then_inc(e_done, 1)
                        act.wait_ge(e_ready, 3)
                        nc.scalar.activation(ea[:], ea[:], ACT.Exp).then_inc(e_done, 1)
                        act.wait_ge(e_done, 3)
                        nc.scalar.activation(ea[:], ea[:], ACT.Ln, bias=onecol[:], scale=1.0).then_inc(l_done, 1)
                        if ada:
                            ada.evac(act, 0)
                        act.wait_ge(f_ready, 1)
                        nc.scalar.activation(r[:], r[:], ACT.Ln).then_inc(l_done, 1)
                        if ada:
                            for i in range(1, ada.n):
                                ada.evac(act, i)

                    @block.vector
                    def _(dve):
                        def step(ins):
                            dve_chain(dve, ins)
                        dve.wait_ge(loaded, 48)
                        step(nc.vector.tensor_tensor(lbs[:, 0], lbr[:, 0], lbr[:, 1], ALU.max))
                        nc.vector.tensor_tensor(lbe[:], lbr[:], bc(lbs[:, 0], 1, DEPTH), ALU.subtract).then_inc(e_ready, 1)
                        nc.vector.tensor_scalar(e[:], fm[:, HZ:HZ + 4, :], -1.0, 80.0, ALU.mult, ALU.min).then_inc(e_ready, 1)
                        for k in range(2):
                            dve.wait_ge(z_done, k + 1)
                            step(nc.vector.tensor_scalar(a[:, k], ps[:, k, :], bg[:, k:k + 1], None, ALU.add))
                        nc.vector.scalar_tensor_tensor(out=ea[:], in0=a[:], scalar=-1.0, in1=a[:],
                                                       op0=ALU.mult, op1=ALU.min).then_inc(e_ready, 1)
                        dve.wait_ge(e_done, 1)
                        step(nc.vector.tensor_tensor(lbs[:, 0], lbe[:, 0], lbe[:, 1], ALU.add))
                        step(nc.vector.reciprocal(lbs[:, 1], lbs[:, 0]))
                        step(nc.vector.tensor_tensor(lbe[:], lbe[:], bc(lbs[:, 1], 1, DEPTH), ALU.mult))
                        step(nc.vector.tensor_copy(lbs[:, 0], lbe[:, 0]))
                        for i in range(1, l + 1):
                            step(nc.vector.tensor_tensor(lbs[:, 0], lbs[:, 0], lbe[:, i], ALU.add))
                        step(nc.vector.tensor_tensor(lbs[:, 1], lbs[:, 0], lbe[:, 0], ALU.subtract))
                        step(nc.vector.tensor_scalar(lbs[:, 2], lbs[:, 1], -1.0, 1.0, ALU.mult, ALU.add))
                        step(nc.vector.tensor_scalar(lbs[:, 3], lbs[:, 1], LB_FLOOR, None, ALU.max))
                        dve.wait_ge(e_done, 2)
                        step(nc.vector.tensor_scalar(r[:], e[:], 1.0, None, ALU.add))
                        step(nc.vector.reciprocal(r[:], r[:]))
                        for j in range(4):
                            c = j % 2
                            nc.vector.scalar_tensor_tensor(out=hk[:, j], in0=e[:, j], scalar=lbs[:, 2, c:c + 1],
                                                           in1=r[:, j], op0=ALU.mult, op1=ALU.mult)
                        for j in range(4):
                            c = j % 2
                            step(nc.vector.tensor_scalar(r[:, j], r[:, j], lbs[:, 2, c:c + 1], lbs[:, 3, c:c + 1],
                                                         ALU.mult, ALU.add))
                        step(nc.vector.tensor_scalar(m[:], r[:], SMALL, None, ALU.is_lt))
                        step(nc.vector.tensor_scalar(e[:], m[:], UP - 1.0, 1.0, ALU.mult, ALU.add))
                        nc.vector.tensor_tensor(r[:], r[:], e[:], ALU.mult).then_inc(f_ready, 1)
                        dve.wait_ge(l_done, 1)
                        step(nc.vector.scalar_tensor_tensor(out=a[:], in0=a[:], scalar=0.0, in1=ea[:],
                                                            op0=ALU.min, op1=ALU.subtract))
                        for k in range(2):
                            step(nc.vector.tensor_scalar(lg[:, 3 * k], a[:, k], 1.0 / GLA_GATE_NORM, None, ALU.mult))
                        dve.wait_ge(l_done, 2)
                        for k in range(2):
                            step(nc.vector.scalar_tensor_tensor(
                                out=lg[:, 3 * k + 1:3 * k + 3], in0=m[:, 2 * k:2 * k + 2], scalar=-60.0 * math.log(2.0),
                                in1=r[:, 2 * k:2 * k + 2], op0=ALU.mult, op1=ALU.add))
                        nc.vector.memset(cum[:, :, :, 0:1], 0.0)
                        for s in range(6):
                            for t in range(TT):
                                nc.vector.tensor_tensor_scan(cum[:, s, t, 1:P + 1], ones[:], lg[:, s, t * P:(t + 1) * P],
                                                             0.0, ALU.mult, ALU.add)
                        if ada:
                            ada.add_bias(dve)

        def phase_scan(l, lo, fm, tm, hk, cum, mix):
            t0 = lo // P
            nt = TT - t0
            xj = range(1 if t0 else 0, 2)
            arg_done, exp_done, xexp_done, ready, unit_mm, unit_ev, x_mm, x_ev, o_mm, o_ev = (
                sem(f"scan_{x}{l}") for x in ("arg_done", "exp_done", "xexp_done", "ready", "unit_mm", "unit_ev",
                                              "x_mm", "x_ev", "o_mm", "o_ev"))
            zeroed, tot_done, pool_arg, pool_q, x_ready = (
                sem(f"scan_{x}{l}") for x in ("zeroed", "tot_done", "pool_arg", "pool_q", "x_ready"))
            heads = [(0, GLA_DK * h, GLA_DK) for h in range(4)] + [(1 + h // 2, 64 * (h % 2), 64) for h in range(4)]
            first = [0, 4, 6, 8]
            with ExitStack() as st:
                exq = sb(st, f"scan_exq{l}", [P, 2, 2, NL, TT * HALF])
                exk = sb(st, f"scan_exk{l}", [P, 2, NL, TT * HALF])
                lk = sb(st, f"scan_lk{l}", [P, 2, NL, TT, P])
                xq = sb(st, f"scan_xq{l}", [P, 2, 4, P])
                xk = sb(st, f"scan_xk{l}", [P, 2, 4, P])
                ksum = sb(st, f"scan_ksum{l}", [P, T])
                tot2 = sb(st, f"scan_tot2{l}", [P, 2, 6])
                sc = sb(st, f"scan_sc{l}", [P, 2, TT, P])
                scx = sb(st, f"scan_scx{l}", [P, 2, 2, BANK])

                def keys(c, dr):
                    return fm[:, GK, :] if c == 0 else hk[:, 2 * dr + c - 1, :]

                def queries(c):
                    return fm[:, GQ if c == 0 else HQ + c - 1, :]

                def tiles(ap, L):
                    return ap[:, t0 * HALF:].rearrange("p (a n l) -> p a n l", a=nt, l=L)

                def arguments(eng, c, dr):
                    cb = cum[:, 3 * dr + c, t0:TT]
                    before, upto = cb[:, :, 0:P], cb[:, :, 1:P + 1]
                    for i, L in enumerate(LEVELS):
                        mid = mids(before, L)
                        qa, ka = tiles(exq[:, c % 2, dr, i], L), tiles(exk[:, dr, i], L)
                        if dr == 0:
                            eng.tensor_tensor(qa, halves(upto, L, 1), mid, ALU.subtract)
                            last = eng.tensor_tensor(ka, mid, halves(upto, L, 0), ALU.subtract)
                        else:
                            eng.tensor_tensor(qa, mid, halves(before, L, 0), ALU.subtract)
                            last = eng.tensor_tensor(ka, halves(before, L, 1), mid, ALU.subtract)
                    return last

                def scale_queries(eng, c, dr):
                    q = queries(c).rearrange("p (a t) -> p a t", a=TT)
                    for i, L in enumerate(LEVELS):
                        qa = tiles(exq[:, c % 2, dr, i], L)
                        last = eng.tensor_tensor(qa, qa, halves(q[:, t0:], L, 1 - dr), ALU.mult)
                    return last

                with nc.Block() as block:
                    @block.gpsimd
                    def _(pool):
                        nc.gpsimd.memset(lk[:], 0.0).then_inc(zeroed, 1)
                        for c in (1, 2):
                            pool.wait_ge(ready, 2 * c)
                            if c == 2:
                                pool.wait_ge(unit_mm, NU * first[1])
                            for dr in range(2):
                                arguments(nc.gpsimd, c, dr).then_inc(pool_arg, 1)
                            for dr in range(2):
                                pool.wait_ge(exp_done, 2 * c + dr + 1)
                                scale_queries(nc.gpsimd, c, dr).then_inc(pool_q, 1)

                    @block.vector
                    def _(dve):
                        for j in range(2):
                            nc.vector.tensor_tensor(tot2[:, j], cum[:, :, 2 * j, P], cum[:, :, 2 * j + 1, P], ALU.add)\
                                .then_inc(tot_done, 1)

                        def factors(c):
                            if c == 0:
                                for dr in range(2):
                                    arguments(nc.vector, 0, dr).then_inc(arg_done, 1)
                                dve.wait_ge(zeroed, 1)
                            else:
                                dve.wait_ge(unit_mm, NU * first[c])
                            for dr in range(2):
                                k = keys(c, dr).rearrange("p (a t) -> p a t", a=TT)
                                dve.wait_ge(exp_done, 2 * c + dr + 1)
                                if c == 0:
                                    scale_queries(nc.vector, 0, dr)
                                for i, L in enumerate(LEVELS):
                                    last = nc.vector.tensor_tensor(halves(lk[:, dr, i, t0:], L, dr), tiles(exk[:, dr, i], L),
                                                                   halves(k[:, t0:], L, dr), ALU.mult)
                                last.then_inc(ready, 1)
                            q = queries(c).rearrange("p (a t) -> p a t", a=TT)
                            for dr in range(2):
                                k = keys(c, dr).rearrange("p (a t) -> p a t", a=TT)
                                dve.wait_ge(xexp_done, 2 * c + dr + 1)
                                for j in xj:
                                    a, b = XQ_TILES[dr][j], XK_TILES[dr][j]
                                    nc.vector.tensor_tensor(xq[:, dr, j], xq[:, dr, j], q[:, a], ALU.mult)
                                    nc.vector.tensor_tensor(xk[:, dr, j], xk[:, dr, j], k[:, b], ALU.mult)
                                nc.vector.tensor_tensor(xq[:, dr, 2:4], xq[:, dr, 2:4], q[:, 2:4], ALU.mult)
                                nc.vector.tensor_tensor(xk[:, dr, 2:4], xk[:, dr, 2:4], k[:, 0:2], ALU.mult)
                            nc.vector.tensor_tensor(ksum[:, lo:], keys(c, 0)[:, lo:], keys(c, 1)[:, lo:], ALU.add).then_inc(x_ready, 1)

                        def gather(h):
                            for u, unit in enumerate(UNITS):
                                n = NU * h + u
                                dve.wait_ge(unit_mm, n + 1)
                                if n:
                                    dve.wait_ge(unit_ev, n)
                                if u == 0 and h >= 2:
                                    dve.wait_ge(o_mm, h - 1)
                                dst = sc[:, h % 2]
                                if unit is None:
                                    nc.vector.copy_predicated(dst[:, t0:], bc(maskd[:], 1, nt),
                                                              ps[:, n % 4, lo:].rearrange("p (a t) -> p a t", a=nt)).then_inc(unit_ev, 1)
                                    continue
                                for j, (dr, i) in enumerate(unit):
                                    L = LEVELS[i]
                                    got = ps[:, n % 4, j * 256 + t0 * HALF:(j + 1) * 256].rearrange("p (a n l) -> p a n l", a=nt, l=L)
                                    msk = bc(mask[:, NL * dr + i].rearrange("p (n l) -> p n l", l=L), 1, nt)
                                    copied = nc.vector.copy_predicated(halves(dst[:, t0:], L, 1 - dr), msk, got)
                                    if j == 0:
                                        dve_chain(dve, copied)
                                    else:
                                        copied.then_inc(unit_ev, 1)

                        for c in range(3):
                            factors(c)
                            for h in range(first[c], first[c + 1]):
                                gather(h)

                    @block.scalar
                    def _(act):
                        def exps(c):
                            for dr in range(2):
                                if c:
                                    act.wait_ge(pool_arg, 2 * (c - 1) + dr + 1)
                                else:
                                    act.wait_ge(arg_done, dr + 1)
                                e = exq[:, c % 2, dr, :, t0 * HALF:]
                                nc.scalar.activation(e, e, ACT.Exp)
                                e = exk[:, dr, :, t0 * HALF:]
                                nc.scalar.activation(e, e, ACT.Exp).then_inc(exp_done, 1)

                        def joining_exps(c):
                            if c:
                                act.wait_ge(x_mm, first[c])
                            for dr in range(2):
                                s = 3 * dr + c
                                cb = cum[:, s]
                                tot = [cum[:, s, t, P:P + 1] for t in range(TT)]
                                tot01, tot23 = tot2[:, 0, s:s + 1], tot2[:, 1, s:s + 1]
                                if c == 0 and dr == 0:
                                    act.wait_ge(tot_done, 2)
                                if dr == 0:
                                    o = 1
                                    jobs = [(xq, 0, 1, 1.0, None), (xq, 1, 3, 1.0, None), (xq, 2, 2, 1.0, None), (xq, 3, 3, 1.0, tot[2]),
                                            (xk, 0, 0, -1.0, tot[0]), (xk, 1, 2, -1.0, tot[2]),
                                            (xk, 2, 0, -1.0, tot01), (xk, 3, 1, -1.0, tot[1])]
                                else:
                                    o = 0
                                    jobs = [(xq, 0, 0, -1.0, tot[0]), (xq, 1, 2, -1.0, tot[2]),
                                            (xq, 2, 2, -1.0, tot23), (xq, 3, 3, -1.0, tot[3]),
                                            (xk, 0, 1, 1.0, None), (xk, 1, 3, 1.0, None),
                                            (xk, 2, 0, 1.0, None), (xk, 3, 1, 1.0, tot[0])]
                                for buf, j, t, scale, bias in jobs:
                                    if j < 2 and j not in xj:
                                        continue
                                    src = cb[:, t, o:o + P]
                                    if bias is None:
                                        last = nc.scalar.activation(buf[:, dr, j], src, ACT.Exp, scale=scale)
                                    else:
                                        last = nc.scalar.activation(buf[:, dr, j], src, ACT.Exp, scale=scale, bias=bias)
                                last.then_inc(xexp_done, 1)

                        def evac(h):
                            act.wait_ge(x_mm, h + 1)
                            if h >= 2:
                                act.wait_ge(o_mm, h - 1)
                            if t0:
                                two = ps[:, 4, :].rearrange("p (dr j t) -> p dr j t", dr=2, j=2)[:, :, 1, :]
                                nc.scalar.activation(scx[:, h % 2, 0, :].rearrange("p (dr j t) -> p dr j t", dr=2, j=2)[:, :, 1, :],
                                                     two, ACT.Copy)
                                nc.scalar.activation(scx[:, h % 2, 1], ps[:, 5, :], ACT.Copy).then_inc(x_ev, 1)
                            else:
                                nc.scalar.activation(scx[:, h % 2], ps[:, 4:6, :], ACT.Copy).then_inc(x_ev, 1)

                        def out(h):
                            act.wait_ge(o_mm, h + 1)
                            p0 = 64 * (h % 2)
                            nc.scalar.activation(mix[p0:p0 + 64, h // 2, lo:], ps[p0:p0 + 64, 6 + h % 2, lo:], ACT.Copy).then_inc(o_ev, 1)

                        exps(0)
                        for c in range(3):
                            joining_exps(c)
                            for h in range(first[c], first[c + 1]):
                                evac(h)
                                if h:
                                    out(h - 1)
                                if h == first[c] and c < 2:
                                    exps(c + 1)
                        out(7)

                    @block.tensor
                    def _(pe):
                        def scores(h):
                            c, p0, w = heads[h]
                            r = slice(p0, p0 + w)
                            q = queries(c)
                            for u, unit in enumerate(UNITS):
                                n = NU * h + u
                                if n >= 4:
                                    pe.wait_ge(unit_ev, n - 3)
                                if h == first[c] and u in (0, 3):
                                    dr = u // 3
                                    pe.wait_ge(ready, 2 * c + dr + 1)
                                    if c:
                                        pe.wait_ge(pool_q, 2 * (c - 1) + dr + 1)
                                if unit is None:
                                    if h == first[c]:
                                        pe.wait_ge(x_ready, c + 1)
                                    for t in range(t0, TT):
                                        mm = nc.tensor.matmul(ps[:, n % 4, t * P:(t + 1) * P], ksum[r, t * P:(t + 1) * P],
                                                              q[r, t * P:(t + 1) * P], start=True, stop=True)
                                else:
                                    for j, (dr, i) in enumerate(unit):
                                        for t in range(t0, TT):
                                            o = j * 256 + t * HALF
                                            mm = nc.tensor.matmul(ps[:, n % 4, o:o + HALF], lk[r, dr, i, t, :],
                                                                  exq[r, c % 2, dr, i, t * HALF:(t + 1) * HALF], start=True, stop=True)
                                mm.then_inc(unit_mm, 1)
                            if h >= 1:
                                pe.wait_ge(x_ev, h)
                            for dr in range(2):
                                for j in xj:
                                    o = (2 * dr + j) * P
                                    nc.tensor.matmul(ps[:, 4, o:o + P], xk[r, dr, j, :], xq[r, dr, j, :], start=True, stop=True)
                            for s in range(2):
                                for dr in range(2):
                                    mm = nc.tensor.matmul(ps[:, 5, s * 256:(s + 1) * 256], xk[r, dr, 2 + s, :],
                                                          xq[r, dr, 2:4, :], start=(dr == 0), stop=(dr == 1))
                            mm.then_inc(x_mm, 1)

                        def output(h):
                            pe.wait_ge(unit_ev, NU * (h + 1))
                            pe.wait_ge(x_ev, h + 1)
                            if h >= 2:
                                pe.wait_ge(o_ev, h - 1)
                            p0 = 64 * (h % 2)
                            for t in range(t0, TT):
                                parts = [(t, sc[:, h % 2, t, :])]
                                for dr in range(2):
                                    for j in range(2):
                                        if XQ_TILES[dr][j] == t:
                                            o = (2 * dr + j) * P
                                            parts.append((XK_TILES[dr][j], scx[:, h % 2, 0, o:o + P]))
                                if t >= 2:
                                    for s in range(2):
                                        o = s * 256 + (t - 2) * P
                                        parts.append((s, scx[:, h % 2, 1, o:o + P]))
                                for j, (s, sco) in enumerate(parts):
                                    mm = nc.tensor.matmul(ps[p0:p0 + 64, 6 + h % 2, t * P:(t + 1) * P],
                                                          tm[:, s, h * DV:(h + 1) * DV], sco,
                                                          start=(j == 0), stop=(j == len(parts) - 1))
                            mm.then_inc(o_mm, 1)

                        for h in range(8):
                            scores(h)
                            if h:
                                output(h - 1)
                        output(7)

        def phase_attn(l, lo, fm, tm, mix):
            t0 = lo // P
            nt = TT - t0
            lam_init = 0.8 - 0.6 * math.exp(-0.3 * l)
            (loaded, sq_done, sum_done, n_done, qk_mm, qk_ev, rot_mm, rot_ev, prep_done, lam_e, lam_x, s_done, nm_done, exp_done,
             diag_done, t_done, ptc_done, pv_done, oev_done, root_done) = (
                sem(f"attn_{x}{l}") for x in ("loaded", "sq_done", "sum_done", "n_done", "qk_mm", "qk_ev", "rot_mm", "rot_ev",
                                              "prep_done", "lam_e", "lam_x", "s_done", "nm_done", "exp_done", "diag_done", "t_done",
                                              "ptc_done", "pv_done", "oev_done", "root_done"))
            NUN = 2 * HEADS * nt
            ncomp = [1 if n < HEADS * nt else 2 for n in range(NUN)]
            keys_of = [T if t0 + n % nt >= CTX // P else CTX for n in range(NUN)]
            c0 = [sum(ncomp[:n]) for n in range(NUN + 1)]
            with ExitStack() as st:
                wq = sb(st, f"mla_wq{l}", [P, 2, HEADS, MLA_DQ])
                wkv = sb(st, f"mla_wkv{l}", [P, HEADS, P])
                gq = sb(st, f"mla_gq{l}", [P, 2])
                gkv = sb(st, f"mla_gkv{l}", [P, 1])
                sq = sb(st, f"mla_sq{l}", [P, 3, T])
                rs = sb(st, f"mla_rs{l}", [P, 2, T])
                qh = sb(st, f"mla_qh{l}", [P, HEADS, T])
                kh = sb(st, f"mla_kh{l}", [P, HEADS, T])
                vm = sb(st, f"mla_v{l}", [P, TT, HEADS * DV])
                rot = sb(st, f"rot{l}", [P, 2, SEQ])
                lamr = sb(st, f"lamr{l}", [P, 4, DIFF_DQK])
                lamp = sb(st, f"lamp{l}", [P, 2, DIFF_DQK])
                lame = sb(st, f"lame{l}", [P, 2])
                nlam = sb(st, f"nlam{l}", [P, 1])
                pr = sb(st, f"probs{l}", [P, 2, 2, T])
                pt = sb(st, f"probsT{l}", [P, 2, T])
                dg = sb(st, f"diag{l}", [P, 2, 2, P])
                mx = sb(st, f"smax{l}", [P, c0[-1]])
                nm = sb(st, f"nsmax{l}", [P, c0[-1]])
                rsum = sb(st, f"rsum{l}", [P, c0[-1]])
                rinv = sb(st, f"rinv{l}", [P, c0[-1]])
                rots = [(slice(0, P), fm[:, DQ + j, CTX:T]) for j in range(4)] + \
                       [(slice(KR0, KR0 + 32), fm[KR0:KR0 + 32, CQ1, CTX:T])] + \
                       [(slice(KR0, KR0 + 32), qh[KR0:KR0 + 32, h, CTX:T]) for h in range(HEADS)]
                with nc.Block() as block:
                    @block.sync
                    def _(sp):
                        sp.dma_start(wq[:, 0], d["w_uq"][l, 0:P]).then_inc(loaded, 16)
                        sp.dma_start(wq[0:64, 1], d["w_uq"][l, P:MLA_Q]).then_inc(loaded, 16)
                        sp.dma_start(wkv[:], d["w_ukv"][l]).then_inc(loaded, 16)
                        sp.dma_start(gq[:, 0:1], d["g_q0"][l]).then_inc(loaded, 16)
                        sp.dma_start(gq[0:64, 1:2], d["g_q1"][l]).then_inc(loaded, 16)
                        sp.dma_start(gkv[:], d["g_kv"][l]).then_inc(loaded, 16)
                        sp.dma_start(lamr[:], d["lam"][l].partition_broadcast(P)).then_inc(loaded, 16)

                    @block.scalar
                    def _(act):
                        nc.scalar.activation(sq[:, 0, lo:], fm[:, CQ0, lo:], ACT.Square)
                        nc.scalar.activation(sq[0:64, 1, lo:], fm[0:64, CQ1, lo:], ACT.Square)
                        nc.scalar.activation(sq[:, 2], fm[:, CKV, :], ACT.Square).then_inc(sq_done, 1)
                        act.wait_ge(lam_e, 1)
                        nc.scalar.activation(lame[:], lame[:], ACT.Exp).then_inc(lam_x, 1)
                        act.wait_ge(sum_done, 1)
                        for j, (width, a) in enumerate(((MLA_Q, lo), (MLA_KV, 0))):
                            nc.scalar.activation(rs[:, j, a:], ps[:, j, a:], ACT.Sqrt, scale=1.0 / width,
                                                 bias=epscol[:]).then_inc(root_done, 1)
                        for n in range(3 * HEADS):
                            act.wait_ge(qk_mm, n + 1)
                            bank = n % 4
                            if n < HEADS:
                                nc.scalar.activation(qh[0:MLA_DQ, n, lo:], ps[0:MLA_DQ, bank, lo:], ACT.Copy).then_inc(qk_ev, 1)
                            elif n < 2 * HEADS:
                                nc.scalar.activation(kh[0:64, n - HEADS], ps[0:64, bank, :], ACT.Copy).then_inc(qk_ev, 1)
                            else:
                                nc.scalar.activation(vm[:, n - 2 * HEADS], ps[:, bank, 0:HEADS * DV], ACT.Copy).then_inc(qk_ev, 1)

                        def exps(n):
                            for c in range(ncomp[n]):
                                j = c0[n] + c
                                act.wait_ge(nm_done, j + 1)
                                if n >= 2:
                                    act.wait_ge(t_done, n - 1)
                                ns = keys_of[n]
                                scale = (MLA_DQ if n < HEADS * nt else DIFF_DQK) ** -0.5
                                nc.scalar.activation(pr[:, n % 2, c, 0:ns], ps[:, 2 * (n % 2) + c, 0:ns], ACT.Exp, scale=scale,
                                                     bias=nm[:, j:j + 1], accum_out=rsum[:, j:j + 1]).then_inc(exp_done, 1)

                        def turned(n):
                            act.wait_ge(t_done, n + 1)
                            if n >= 2:
                                act.wait_ge(pv_done, n - 1)
                            ns = keys_of[n]
                            nc.scalar.activation(pt[:, n % 2, 0:ns], ps[:, 4 + n % 2, 0:ns], ACT.Copy).then_inc(ptc_done, 1)

                        def evac(h):
                            act.wait_ge(pv_done, nt * (h + 1))
                            p0 = 64 * (h % 2)
                            nc.scalar.activation(mix[p0:p0 + 64, 4 + h // 2, lo:], ps[p0:p0 + 64, 6 + h % 2, lo:], ACT.Copy).then_inc(oev_done, 1)

                        exps(0)
                        exps(1)
                        for n in range(NUN):
                            turned(n)
                            if n + 2 < NUN:
                                exps(n + 2)
                            if n % nt == 1 and n > nt:
                                evac(n // nt - 1)
                        evac(2 * HEADS - 1)

                    @block.tensor
                    def _(pe):
                        pe.wait_ge(sq_done, 1)
                        nc.tensor.matmul(ps[:, 0, lo:], ones[:], sq[:, 0, lo:], start=True, stop=False)
                        nc.tensor.matmul(ps[:, 0, lo:], ones[0:64, :], sq[0:64, 1, lo:], start=False, stop=True)
                        nc.tensor.matmul(ps[:, 1, :], ones[:], sq[:, 2], start=True, stop=True).then_inc(sum_done, 1)
                        pe.wait_ge(n_done, 1)
                        for n in range(3 * HEADS):
                            bank = n % 4
                            if n >= 4:
                                pe.wait_ge(qk_ev, n - 3)
                            h = n % HEADS
                            if n < HEADS:
                                nc.tensor.matmul(ps[0:MLA_DQ, bank, lo:], wq[:, 0, h, :], fm[:, CQ0, lo:], start=True, stop=False)
                                mm = nc.tensor.matmul(ps[0:MLA_DQ, bank, lo:], wq[0:64, 1, h, :], fm[0:64, CQ1, lo:],
                                                      start=False, stop=True)
                            elif n < 2 * HEADS:
                                mm = nc.tensor.matmul(ps[0:64, bank, :], wkv[:, h, 0:MLA_NOPE], fm[:, CKV, :], start=True, stop=True)
                            else:
                                mm = nc.tensor.matmul(ps[:, bank, 0:HEADS * DV], fm[:, CKV, h * P:(h + 1) * P],
                                                      wkv[:, :, MLA_NOPE:P], start=True, stop=True)
                            mm.then_inc(qk_mm, 1)
                        for n, (rows, x) in enumerate(rots):
                            if n == 5:
                                pe.wait_ge(qk_ev, HEADS)
                            if n >= 2:
                                pe.wait_ge(rot_ev, n - 1)
                            nc.tensor.matmul(ps[rows, 4 + n % 2, 0:SEQ], rotp[rows, rows], x, start=True, stop=True).then_inc(rot_mm, 1)
                        pe.wait_ge(prep_done, 1)
                        pe.wait_ge(qk_ev, 3 * HEADS)

                        def scores(n):
                            h, t = n // nt, t0 + n % nt
                            ns = T if t >= 2 else CTX
                            for c in range(ncomp[n]):
                                if n >= 2:
                                    pe.wait_ge(exp_done, c0[n - 1])
                                if h < HEADS:
                                    q, k = qh[0:MLA_DQ, h, t * P:(t + 1) * P], kh[0:MLA_DQ, h, 0:ns]
                                else:
                                    j = 2 * (h - HEADS) + c
                                    r = slice(32 * (j % 4), 32 * (j % 4) + 32)
                                    q, k = fm[r, DQ + j // 4, t * P:(t + 1) * P], fm[r, DK + j // 4, 0:ns]
                                nc.tensor.matmul(ps[:, 2 * (n % 2) + c, 0:ns], q, k, start=True, stop=True).then_inc(s_done, 1)

                        def turn(n):
                            pe.wait_ge(diag_done, c0[n + 1])
                            if n >= 2:
                                pe.wait_ge(ptc_done, n - 1)
                            for s in range(keys_of[n] // P):
                                for c in range(ncomp[n]):
                                    mm = nc.tensor.matmul(ps[:, 4 + n % 2, s * P:(s + 1) * P], pr[:, n % 2, c, s * P:(s + 1) * P],
                                                          dg[:, n % 2, c, :], start=(c == 0), stop=(c == ncomp[n] - 1))
                            mm.then_inc(t_done, 1)

                        def values(n):
                            h, t = n // nt, t0 + n % nt
                            pe.wait_ge(ptc_done, n + 1)
                            if t == t0 and h >= 2:
                                pe.wait_ge(oev_done, h - 1)
                            p0 = 64 * (h % 2)
                            nst = keys_of[n] // P
                            for s in range(nst):
                                v = vm[:, s, h * DV:(h + 1) * DV] if h < HEADS else \
                                    tm[:, s, (h + HEADS) * DV:(h + HEADS + 1) * DV]
                                mm = nc.tensor.matmul(ps[p0:p0 + 64, 6 + h % 2, t * P:(t + 1) * P], v, pt[:, n % 2, s * P:(s + 1) * P],
                                                      start=(s == 0), stop=(s == nst - 1))
                            mm.then_inc(pv_done, 1)

                        scores(0)
                        scores(1)
                        for n in range(NUN):
                            turn(n)
                            if n + 2 < NUN:
                                scores(n + 2)
                            if n:
                                values(n - 1)
                        values(NUN - 1)

                    @block.vector
                    def _(dve):
                        def step(ins):
                            dve_chain(dve, ins)
                        dve.wait_ge(loaded, 7 * 16)
                        step(nc.vector.tensor_tensor(lamp[:], lamr[:, 0:4:2], lamr[:, 1:4:2], ALU.mult))
                        nc.vector.tensor_reduce(lame[:], lamp[:], AX, ALU.add).then_inc(lam_e, 1)
                        dve.wait_ge(lam_x, 1)
                        step(nc.vector.tensor_tensor(nlam[:], lame[:, 1:2], lame[:, 0:1], ALU.subtract))
                        step(nc.vector.tensor_scalar(nlam[:], nlam[:], -lam_init, None, ALU.add))
                        dve.wait_ge(root_done, 2)
                        nc.vector.reciprocal(rs[:, 0, lo:], rs[:, 0, lo:])
                        step(nc.vector.reciprocal(rs[:, 1], rs[:, 1]))
                        for x, g, r in ((fm[:, CQ0, lo:], gq[:, 0:1], rs[:, 0, lo:]), (fm[0:64, CQ1, lo:], gq[0:64, 1:2], rs[0:64, 0, lo:]),
                                        (fm[:, CKV, :], gkv[:], rs[:, 1])):
                            last = nc.vector.scalar_tensor_tensor(out=x, in0=x, scalar=g, in1=r, op0=ALU.mult, op1=ALU.mult)
                        last.then_inc(n_done, 1)
                        for n, (rows, x) in enumerate(rots):
                            dve.wait_ge(rot_mm, n + 1)
                            nc.vector.tensor_tensor(rot[rows, n % 2], ps[rows, 4 + n % 2, 0:SEQ], sinT[rows], ALU.mult).then_inc(rot_ev, 1)
                            step(nc.vector.tensor_tensor(x, x, cosT[rows], ALU.mult))
                            dve.wait_ge(rot_ev, n + 1)
                            last = nc.vector.tensor_tensor(x, x, rot[rows, n % 2], ALU.add)
                            if n == 4:
                                step(last)
                                for h in range(HEADS):
                                    nc.vector.tensor_copy(kh[KR0:KR0 + 32, h], fm[KR0:KR0 + 32, CQ1, :])
                        last.then_inc(prep_done, 1)

                        def maxima(n):
                            ns = keys_of[n]
                            scale = (MLA_DQ if n < HEADS * nt else DIFF_DQK) ** -0.5
                            for c in range(ncomp[n]):
                                j = c0[n] + c
                                dve.wait_ge(s_done, j + 1)
                                step(nc.vector.tensor_reduce(mx[:, j:j + 1], ps[:, 2 * (n % 2) + c, 0:ns], AX, ALU.max))
                                nc.vector.tensor_scalar(nm[:, j:j + 1], mx[:, j:j + 1], -scale, None, ALU.mult).then_inc(nm_done, 1)

                        def diagonals(n):
                            for c in range(ncomp[n]):
                                j = c0[n] + c
                                dve.wait_ge(exp_done, j + 1)
                                step(nc.vector.reciprocal(rinv[:, j:j + 1], rsum[:, j:j + 1]))
                                if n >= 2:
                                    dve.wait_ge(t_done, n - 1)
                                if c == 0:
                                    nc.vector.tensor_scalar(dg[:, n % 2, c], ident[:], rinv[:, j:j + 1], None, ALU.mult).then_inc(diag_done, 1)
                                else:
                                    nc.vector.tensor_scalar(dg[:, n % 2, c], ident[:], rinv[:, j:j + 1], nlam[:], ALU.mult, ALU.mult)\
                                        .then_inc(diag_done, 1)

                        maxima(0)
                        maxima(1)
                        diagonals(0)
                        for n in range(NUN):
                            if n + 1 < NUN:
                                diagonals(n + 1)
                            if n + 2 < NUN:
                                maxima(n + 2)

        def phase_post(l, lo, fm, mix, ada_part):
            lam_init = 0.8 - 0.6 * math.exp(-0.3 * l)
            chunks = [0, 1, 2, 3, 6, 7]
            loaded, sq_done, sum_done, root_done = (sem(f"post_{x}{l}") for x in ("loaded", "sq_done", "sum_done", "root_done"))
            with ExitStack() as st:
                sq = sb(st, f"post_sq{l}", [P, 6, T])
                g = sb(st, f"post_g{l}", [P, 3])
                ada = AdaPart(st, *ada_part, (6, 7, 0)) if ada_part else None
                with nc.Block() as block:
                    @block.sync
                    def _(sp):
                        sp.dma_start(g[:], d["g_head"][l]).then_inc(loaded, 16)
                        if ada:
                            for i in range(ada.n):
                                ada.load(sp, i)

                    @block.scalar
                    def _(act):
                        for j, c in enumerate(chunks):
                            nc.scalar.activation(sq[:, j, lo:], mix[:, c, lo:], ACT.Square).then_inc(sq_done, 1)
                        for j in range(6):
                            act.wait_ge(sum_done, j + 1)
                            nc.scalar.activation(sq[:, j, lo:], ps[:, j, lo:], ACT.Sqrt, bias=epscol[:]).then_inc(root_done, 1)
                        if ada:
                            for i in range(ada.n):
                                ada.evac(act, i)

                    @block.tensor
                    def _(pe):
                        for j in range(6):
                            pe.wait_ge(sq_done, j + 1)
                            nc.tensor.matmul(ps[:, j, lo:], mean64[:], sq[:, j, lo:], start=True, stop=True).then_inc(sum_done, 1)
                        if ada:
                            pe.wait_ge(root_done, 1)
                            for i in range(ada.n):
                                ada.rows(pe, i)
                            ada.columns(pe, ada.n - 1)

                    @block.vector
                    def _(dve):
                        def step(ins):
                            dve_chain(dve, ins)
                        dve.wait_ge(loaded, 16)
                        step(nc.vector.tensor_scalar(g[:, 2:3], g[:, 2:3], 1.0 - lam_init, None, ALU.mult))
                        for j, c in enumerate(chunks):
                            dve.wait_ge(root_done, j + 1)
                            step(nc.vector.reciprocal(sq[:, j, lo:], sq[:, j, lo:]))
                            step(nc.vector.scalar_tensor_tensor(out=mix[:, c, lo:], in0=mix[:, c, lo:], scalar=g[:, j // 2:j // 2 + 1],
                                                                in1=sq[:, j, lo:], op0=ALU.mult, op1=ALU.mult))
                            if c < 4:
                                nc.vector.tensor_tensor(mix[:, c, lo:], mix[:, c, lo:], fm[:, GATE0 + c, lo:], ALU.mult)
                        if ada:
                            ada.add_bias(dve)

        def add_gated(l, k, which, src, lo):
            n = []
            for v, (a, b) in enumerate(((lo, CTX), (max(lo, CTX), T))):
                if a < b:
                    w = 1 - v
                    n.append(nc.vector.scalar_tensor_tensor(out=xT[:, k, a:b], in0=src[:, a - lo:b - lo],
                                                            scalar=mods[l][:, which * DC + k, w:w + 1], in1=xT[:, k, a:b],
                                                            op0=ALU.mult, op1=ALU.add))
            return n[-1]

        def phase_out(l, lo, mix):
            RW = 4
            w_in = [sem(f"out_w_in{l}_{r}") for r in range(RW)]
            xhi_done, xlo_done, hi_done, lo_done, mm_done, ev_done = (
                sem(f"out_{x}{l}") for x in ("xhi", "xlo", "hi", "lo", "mm", "ev"))
            with ExitStack() as st:
                slab = sb(st, f"out_slab{l}", [P, RW, DC, P])
                wh = sb(st, f"out_wh{l}", [P, 2, DC, P], F32R)
                wl = sb(st, f"out_wl{l}", [P, 2, DC, P], F32R)
                xh = sb(st, f"out_xh{l}", [P, DC, T - lo], F32R)
                xl = sb(st, f"out_xl{l}", [P, DC, T - lo], F32R)
                with nc.Block() as block:
                    @block.sync
                    def _(sp):
                        for c in range(DC):
                            if c >= RW:
                                sp.wait_ge(lo_done, c - RW + 1)
                            sp.dma_start(slab[:, c % RW], d["w_out"][l, c]).then_inc(w_in[c % RW], 16)

                    @block.tensor
                    def _(pe):
                        for c in range(DC):
                            pe.wait_ge(lo_done, c + 1)
                            if c >= 4:
                                pe.wait_ge(ev_done, c - 3)
                            for k in range(DC):
                                if c == 0:
                                    pe.wait_ge(xlo_done, k + 1)
                                mm = product(nc, ps[:, c % 4, 0:T - lo], (wh[:, c % 2, k, :], wl[:, c % 2, k, :]),
                                             (xh[:, k, :], xl[:, k, :]), k == 0, k == DC - 1)
                            mm.then_inc(mm_done, 1)

                    @block.scalar
                    def _(act):
                        for k in range(DC):
                            nc.scalar.activation(xh[:, k, :], mix[:, k, lo:], ACT.Copy).then_inc(xhi_done, 1)
                        for c in range(DC):
                            act.wait_ge(w_in[c % RW], 16 * (c // RW + 1))
                            if c >= 2:
                                act.wait_ge(mm_done, c - 1)
                            nc.scalar.activation(wh[:, c % 2], slab[:, c % RW], ACT.Copy).then_inc(hi_done, 1)

                    @block.gpsimd
                    def _(pool):
                        for c in range(DC):
                            pool.wait_ge(hi_done, c + 1)
                            nc.gpsimd.tensor_tensor(wl[:, c % 2], slab[:, c % RW], f32(wh[:, c % 2]), ALU.subtract).then_inc(lo_done, 1)

                    @block.vector
                    def _(dve):
                        for k in range(DC):
                            dve.wait_ge(xhi_done, k + 1)
                            nc.vector.tensor_tensor(xl[:, k, :], mix[:, k, lo:], f32(xh[:, k, :]), ALU.subtract).then_inc(xlo_done, 1)
                        for c in range(DC):
                            dve.wait_ge(mm_done, c + 1)
                            add_gated(l, c, 2, ps[:, c % 4, :], lo).then_inc(ev_done, 1)

        def phase_route(l, lo, hp, iT, jT, gT, ada_part):
            RW = 4
            nt = (T - lo) // P
            n = T - lo
            HP = 2 * PH
            w_in = [sem(f"route_w_in{l}_{r}") for r in range(RW)]
            (k_in, hi_done, lo_done, q_mm, q_ev, s_mm, s_ev, s_used, b_done, x_done, tr_in, tr_mm, tr_ev) = (
                sem(f"route_{x}{l}") for x in ("k_in", "hi", "lo", "q_mm", "q_ev", "s_mm", "s_ev", "s_used", "b_done", "x_done",
                                               "tr_in", "tr_mm", "tr_ev"))
            with ExitStack() as st:
                slab = sb(st, f"route_slab{l}", [P, RW, DC, P])
                wh = sb(st, f"route_wh{l}", [P, 2, DC, P], F32R)
                wl = sb(st, f"route_wl{l}", [P, 2, DC, P], F32R)
                kT = sb(st, f"route_keys{l}", [P, HP, NKEY])
                qT = sb(st, f"route_q{l}", [P, 2, n])
                s_sb = sb(st, f"route_s{l}", [P, 2, nt, NKEY])
                s2 = sb(st, f"route_s2{l}", [P, nt, 2 * NKEY])
                top = sb(st, f"route_top{l}", [P, nt, HP, TOPK])
                idx = sb(st, f"route_idx{l}", [P, nt, HP, TOPK], U32)
                idf = sb(st, f"route_idf{l}", [P, nt, HP, TOPK])
                cand = sb(st, f"route_cand{l}", [P, nt, TOPK, TOPK])
                best = sb(st, f"route_best{l}", [P, nt, PH, TOPK])
                sel = sb(st, f"route_sel{l}", [P, nt, PH, TOPK], U32)
                sela = sb(st, f"route_sela{l}", [P, 2, PH * TOPK], U32)
                self_ = sb(st, f"route_self{l}", [P, 2, PH * TOPK])
                eq = sb(st, f"route_eq{l}", [P, PH * TOPK, TOPK])
                ijg = sb(st, f"route_ijg{l}", [P, 2, 3, PH * TOPK])
                esum = sb(st, f"route_esum{l}", [P, PH])
                ada = AdaPart(st, *ada_part, (5, 6, 7)) if ada_part else None
                per_tile = 2
                with_q = ada.n - per_tile * nt if ada else 0
                ADA0 = HP - with_q

                def tile_chunks(t):
                    return range(with_q + per_tile * t, with_q + per_tile * (t + 1)) if ada else ()
                with nc.Block() as block:
                    @block.sync
                    def _(sp):
                        for c in range(HP):
                            if c >= RW:
                                sp.wait_ge(lo_done, c - RW + 1)
                            sp.dma_start(slab[:, c % RW], d["w_pq"][l, c]).then_inc(w_in[c % RW], 16)
                            if c == 0:
                                sp.dma_start(kT[:], d["keysT"][l]).then_inc(k_in, 16)
                            if c >= ADA0 + 2:
                                ada.load(sp, c - ADA0 - 2)
                        for i in range(with_q - 2, ada.n) if ada else ():
                            ada.load(sp, i)

                    @block.tensor
                    def _(pe):
                        def sub_scores(c):
                            pe.wait_ge(q_ev, c + 1)
                            pe.wait_ge(k_in, 16)
                            if c >= 2:
                                pe.wait_ge(s_ev, c - 1)
                            for t in range(nt):
                                mm = nc.tensor.matmul(ps[:, 2 + c % 2, t * P:(t + 1) * P], qT[:, c % 2, t * P:(t + 1) * P], kT[:, c, :],
                                                      start=True, stop=True)
                            mm.then_inc(s_mm, 1)

                        for c in range(HP):
                            pe.wait_ge(lo_done, c + 1)
                            if c >= 2:
                                pe.wait_ge(q_ev, c - 1)
                            for k in range(DC):
                                mm = product(nc, ps[:, c % 2, 0:n], (wh[:, c % 2, k, :], wl[:, c % 2, k, :]),
                                             (hp[0][:, k, :], hp[1][:, k, :]), k == 0, k == DC - 1)
                            mm.then_inc(q_mm, 1)
                            if c:
                                sub_scores(c - 1)
                            if c > ADA0:
                                ada.rows(pe, c - 1 - ADA0)
                        sub_scores(HP - 1)
                        if ada:
                            ada.rows(pe, with_q - 1)
                        for t in range(nt):
                            for i in tile_chunks(t):
                                ada.rows(pe, i)
                                if i == ada.n - 1:
                                    ada.columns(pe, i)
                            pe.wait_ge(tr_in, t + 1)
                            if t >= 1:
                                pe.wait_ge(tr_ev, t)
                            for j in range(3):
                                mm = nc.tensor.transpose(ps[:, 4, j * P:(j + 1) * P], ijg[:, t % 2, j, :], ident[:])
                            mm.then_inc(tr_mm, 1)

                    @block.scalar
                    def _(act):
                        def s_copy(c):
                            act.wait_ge(s_mm, c + 1)
                            if c >= 2:
                                act.wait_ge(s_used, c - 1)
                            nc.scalar.activation(s_sb[:, c % 2], ps[:, 2 + c % 2, 0:n].rearrange("p (a k) -> p a k", a=nt),
                                                 ACT.Copy).then_inc(s_ev, 1)
                        def w_hi(c):
                            act.wait_ge(w_in[c % RW], 16 * (c // RW + 1))
                            if c >= 2:
                                act.wait_ge(q_mm, c - 1)
                            nc.scalar.activation(wh[:, c % 2], slab[:, c % RW], ACT.Copy).then_inc(hi_done, 1)

                        w_hi(0)
                        w_hi(1)
                        for c in range(HP):
                            act.wait_ge(q_mm, c + 1)
                            if c + 2 < HP:
                                w_hi(c + 2)
                            if c >= 2:
                                act.wait_ge(s_mm, c - 1)
                            nc.scalar.activation(qT[:, c % 2, :], ps[:, c % 2, 0:n], ACT.Copy).then_inc(q_ev, 1)
                            if c:
                                s_copy(c - 1)
                            if c > ADA0:
                                ada.evac(act, c - 1 - ADA0)
                        s_copy(HP - 1)
                        if ada:
                            ada.evac(act, with_q - 1)
                        for t in range(nt):
                            for i in tile_chunks(t):
                                ada.evac(act, i)
                            act.wait_ge(b_done, t + 1)
                            nc.scalar.activation(best[:, t], best[:, t], ACT.Exp).then_inc(x_done, 1)

                    @block.gpsimd
                    def _(pool):
                        for c in range(HP):
                            pool.wait_ge(hi_done, c + 1)
                            nc.gpsimd.tensor_tensor(wl[:, c % 2], slab[:, c % RW], f32(wh[:, c % 2]), ALU.subtract).then_inc(lo_done, 1)

                    @block.vector
                    def _(dve):
                        def step(ins):
                            dve_chain(dve, ins)

                        def top16(vals, ids, src, tmp):
                            tiles = range(nt)
                            best8 = [dve_chain.mark(nc.vector.max(vals(t)[:, 0:8], src(t))) for t in tiles]
                            for t in tiles:
                                dve.wait_ge(dve_chain.sem, best8[t])
                                nc.vector.max_index(ids(t)[:, 0:8], vals(t)[:, 0:8], src(t))
                            rest = [dve_chain.mark(nc.vector.match_replace(tmp(t), vals(t)[:, 0:8], src(t), NEG)) for t in tiles]
                            next8 = []
                            for t in tiles:
                                dve.wait_ge(dve_chain.sem, rest[t])
                                next8.append(dve_chain.mark(nc.vector.max(vals(t)[:, 8:16], tmp(t))))
                            for t in tiles:
                                dve.wait_ge(dve_chain.sem, next8[t])
                                last = nc.vector.max_index(ids(t)[:, 8:16], vals(t)[:, 8:16], tmp(t))
                            return last

                        for c in range(HP):
                            dve.wait_ge(s_ev, c + 1)
                            if c:
                                dve.wait_ge(s_used, c)
                            top16(lambda t: top[:, t, c], lambda t: idx[:, t, c], lambda t: s_sb[:, c % 2, t],
                                  lambda t: s2[:, t, 0:NKEY]).then_inc(s_used, 1)
                            if c % 2:
                                h = c // 2
                                dve.wait_ge(s_used, c + 1)
                                step(nc.vector.tensor_tensor(cand[:], bc(top[:, :, c - 1], 3, TOPK), bc(top[:, :, c], 2, TOPK), ALU.add))
                                step(top16(lambda t: best[:, t, h], lambda t: sel[:, t, h],
                                           lambda t: cand[:, t].rearrange("p a b -> p (a b)"), lambda t: s2[:, t]))
                        step(nc.vector.tensor_copy(idf[:], idx[:]))
                        for t in range(nt):
                            f = idf[:, t].rearrange("p (h two) k -> p h two k", two=2)
                            nc.vector.tensor_copy(esum[:], best[:, t, :, 0])
                            step(nc.vector.tensor_copy(s2[:, t, 0:PH], best[:, t, :, 0]))
                            nc.vector.tensor_tensor(best[:, t], best[:, t], bc(s2[:, t, 0:PH], 2, TOPK), ALU.subtract).then_inc(b_done, 1)
                            flat = sel[:, t].rearrange("p h k -> p (h k)")
                            nc.vector.tensor_scalar(sela[:, 0], flat, 4, None, ALU.logical_shift_right)
                            step(nc.vector.tensor_scalar(sela[:, 1], flat, 15, None, ALU.bitwise_and))
                            step(nc.vector.tensor_copy(self_[:], sela[:]))
                            r = t % 2
                            for j in range(2):
                                step(nc.vector.tensor_tensor(eq[:], bc(self_[:, j], 2, TOPK), bc(iota[:, 0:TOPK], 1, PH * TOPK), ALU.is_equal))
                                e4 = eq[:].rearrange("p (h k) a -> p h k a", h=PH)
                                step(nc.vector.tensor_tensor(e4, e4, bc(f[:, :, j], 2, TOPK), ALU.mult))
                                step(nc.vector.tensor_reduce(ijg[:, r, j], eq[:], AX, ALU.add))
                            dve.wait_ge(x_done, t + 1)
                            step(nc.vector.tensor_reduce(esum[:], best[:, t], AX, ALU.add))
                            step(nc.vector.reciprocal(esum[:], esum[:]))
                            g3 = ijg[:, r, 2].rearrange("p (h k) -> p h k", h=PH)
                            nc.vector.tensor_tensor(g3, best[:, t], bc(esum[:], 2, TOPK), ALU.mult).then_inc(tr_in, 1)
                            dve.wait_ge(tr_mm, t + 1)
                            cols = slice(t * P, (t + 1) * P)
                            nc.vector.tensor_copy(iT[:, cols], ps[:, 4, 0:P])
                            nc.vector.tensor_copy(jT[:, cols], ps[:, 4, P:2 * P])
                            nc.vector.tensor_copy(gT[:, cols], ps[:, 4, 2 * P:3 * P]).then_inc(tr_ev, 1)
                        if ada:
                            ada.add_bias(dve)

        def phase_dense(l, lo, iT, jT, gT):
            n = T - lo
            U = 16
            UB = 4
            UJ = 10
            a_done, b_done, g_mm, g_ev, neg_done, dist_done, c_done = (
                sem(f"dense_{x}{l}") for x in ("a", "b", "mm", "ev", "neg", "dist", "c"))
            stored = [sem(f"dense_stored{l}_{r}") for r in range(2)]
            with ExitStack() as st:
                hot_i = sb(st, f"hot_i{l}", [P, 2, U, NKEY])
                hot_j = sb(st, f"hot_j{l}", [P, 2, U, NKEY])
                stage = sb(st, f"dense_stage{l}", [P, 2, NKEY, TB])
                njT = sb(st, f"dense_nj{l}", [P, n + U])
                with nc.Block() as block:
                    @block.vector
                    def _(dve):
                        def body(it, first):
                            for q in range(UB):
                                u = UB * it + q
                                r = q % 2
                                if not (first and q < 2):
                                    dve.wait_ge(g_mm, u - 1)
                                nc.vector.tensor_tensor(hot_j[:, r, 0:UJ], bc(jT[:, bass.ds(u * U, UJ)], 2, NKEY),
                                                        bc(iota[:], 1, UJ), ALU.is_equal).then_inc(b_done, 1)
                                for t in range(U):
                                    at = bass.ds(u * U + t, 1)
                                    last = nc.vector.tensor_scalar(hot_i[:, r, t], iota[:], iT[:, at], gT[:, at],
                                                                   ALU.is_equal, ALU.mult)
                                last.then_inc(a_done, 1)
                        nc.vector.memset(njT[:, n:], 0.0).then_inc(neg_done, 1)
                        nc.vector.tensor_scalar(njT[:, 0:n], jT[:], -1.0, None, ALU.mult).then_inc(neg_done, 1)
                        body(0, True)
                        with dve.Fori(1, n // (U * UB)) as it:
                            body(it, False)

                    @block.tensor
                    def _(pe):
                        def body(it, first):
                            for q in range(UB):
                                u = UB * it + q
                                r = q % 2
                                pe.wait_ge(b_done, u + 1)
                                pe.wait_ge(a_done, u + 1)
                                pe.wait_ge(c_done, u + 1)
                                if not (first and q < 2):
                                    pe.wait_ge(g_ev, u - 1)
                                for t in range(U):
                                    mm = nc.tensor.matmul(ps[:, 4 * r + t // 4, (t % 4) * P:(t % 4 + 1) * P],
                                                          hot_j[:, r, t], hot_i[:, r, t], start=True, stop=True)
                                mm.then_inc(g_mm, 1)
                        body(0, True)
                        with pe.Fori(1, n // (U * UB)) as it:
                            body(it, False)

                    @block.scalar
                    def _(act):
                        def columns(u, r):
                            for t in range(UJ, U):
                                last = nc.scalar.activation(hot_j[:, r, t], iota[:], ACT.Abs, bias=njT[:, bass.ds(u * U + t, 1)])
                            last.then_inc(dist_done, 1)
                            act.wait_ge(dist_done, u + 1)
                            nc.scalar.activation(hot_j[:, r, UJ:], hot_j[:, r, UJ:], ACT.Relu, scale=-1.0,
                                                 bias=onecol[:]).then_inc(c_done, 1)

                        def body(it, first):
                            for q in range(UB):
                                u = UB * it + q
                                if not (first and q == 0):
                                    act.wait_ge(g_mm, u)
                                columns(u + 1, (q + 1) % 2)
                                act.wait_ge(g_mm, u + 1)
                                if q % 2 == 0 and not first:
                                    act.wait_ge(stored[q // 2], 16 * it)
                                got = ps[:, 4 * (q % 2):4 * (q % 2) + 4, :].rearrange("p b (t i) -> p i (b t)", i=NKEY)
                                o = (q % 2) * U
                                nc.scalar.activation(stage[:, q // 2, :, o:o + U], got, ACT.Copy).then_inc(g_ev, 1)
                        act.wait_ge(neg_done, 2)
                        columns(0, 0)
                        body(0, True)
                        with act.Fori(1, n // (U * UB)) as it:
                            body(it, False)

                    @block.sync
                    def _(sp):
                        with sp.Fori(0, n // (U * UB)) as it:
                            for r in range(2):
                                sp.wait_ge(g_ev, UB * it + 2 * r + 2)
                                sp.dma_start(gates_dram[bass.ds(2 * it + r, 1)].rearrange("a p i t -> p (a i) t"),
                                             stage[:, r]).then_inc(stored[r], 16)
                        for r in range(2):
                            sp.wait_ge(stored[r], 16 * (n // (U * UB)))

        def phase_peer(l, lo, hp, gates_dram):
            n = T - lo
            ntb = n // TB
            ITE = 8
            NIT = NKEY // ITE
            CPS = DC // GE
            OB = 4
            u_in = [sem(f"peer_u_in{l}_{r}") for r in range(2)]
            v_in = [sem(f"peer_v_in{l}_{r}") for r in range(2)]
            g_in = [sem(f"peer_g_in{l}_{r}") for r in range(2)]
            (uhi, ulo, vhi, vlo, whi, wlo, act_mm, gelu_done, w_done, out_mm, x_done) = (
                sem(f"peer_{x}{l}") for x in ("uhi", "ulo", "vhi", "vlo", "whi", "wlo", "act_mm", "gelu", "w", "out_mm", "x"))
            with ExitStack() as st:
                us = sb(st, f"peer_u{l}", [P, 2, DC, GE * P])
                uh = sb(st, f"peer_uh{l}", [P, 2, DC, P], F32R)
                ul = sb(st, f"peer_ul{l}", [P, 2, DC, P], F32R)
                vs = sb(st, f"peer_v{l}", [P, 2, GE, D_MODEL])
                vh = sb(st, f"peer_vh{l}", [P, 2, GE, D_MODEL], F32R)
                vl = sb(st, f"peer_vl{l}", [P, 2, GE, D_MODEL], F32R)
                gs = sb(st, f"peer_gates{l}", [P, 2, ntb, GROWS, TB])
                ga = sb(st, f"peer_act{l}", [P, 2, n])
                wt = sb(st, f"peer_wt{l}", [P, 2, n])
                wh = sb(st, f"peer_wh{l}", [P, 2, GE, n], F32R)
                wl = sb(st, f"peer_wl{l}", [P, 2, GE, n], F32R)

                with nc.Block() as block:
                    @block.sync
                    def _(sp):
                        def body(it, first):
                            for g in range(ITE // GE):
                                gg = (ITE // GE) * it + g
                                if not (first and g < 2):
                                    sp.wait_ge(ulo, GE * (gg - 1))
                                sp.dma_start(us[:, g % 2], d["uT"][l, bass.ds(gg, 1)].rearrange("a p k e -> p (a k) e")).then_inc(u_in[g % 2], 16)
                                if g % 2 == 0:
                                    r = g // 2
                                    if not first:
                                        sp.wait_ge(w_done, GROWS * (2 * it + r - 1))
                                    src = gates_dram[0:ntb, :, bass.ds(GROWS * (2 * it + r), GROWS), :].rearrange("b p i t -> p b (i t)")
                                    sp.dma_start(gs[:, r].rearrange("p b i t -> p b (i t)"), src).then_inc(g_in[r], 16)
                                if not (first and g < 2):
                                    sp.wait_ge(vlo, GE * (gg - 1))
                                sp.dma_start(vs[:, g % 2], d["v"][l, bass.ds(gg, 1)].rearrange("a p j n -> p (a j) n")).then_inc(v_in[g % 2], 16)
                        body(0, True)
                        with sp.Fori(1, NIT) as it:
                            body(it, False)

                    @block.gpsimd
                    def _(pool):
                        def body(it):
                            for e in range(ITE):
                                pool.wait_ge(uhi, ITE * it + e + 1)
                                src = us[:, (e // GE) % 2, :, (e % GE) * P:(e % GE + 1) * P]
                                nc.gpsimd.tensor_tensor(ul[:, e % 2], src, f32(uh[:, e % 2]), ALU.subtract).then_inc(ulo, 1)
                        with pool.Fori(0, NIT) as it:
                            body(it)

                    @block.tensor
                    def _(pe):
                        def outputs(g, r, j, first):
                            if j == 0:
                                pe.wait_ge(vlo, GE * (g + 1))
                                pe.wait_ge(wlo, GE * (g + 1))
                            for c in range(CPS * j, CPS * (j + 1)):
                                if not (first and c < OB):
                                    pe.wait_ge(x_done, DC * g + c - OB + 1)
                                for q in range(GE):
                                    mm = product(nc, ps[:, 2 + c % OB, 0:n], (vh[:, r, q, c * P:(c + 1) * P], vl[:, r, q, c * P:(c + 1) * P]),
                                                 (wh[:, r, q, :], wl[:, r, q, :]), q == 0, q == GE - 1)
                                mm.then_inc(out_mm, 1)

                        def body(it, first):
                            for e in range(ITE):
                                eg = ITE * it + e
                                pe.wait_ge(ulo, eg + 1)
                                if not (first and e < 2):
                                    pe.wait_ge(gelu_done, eg - 1)
                                for k in range(DC):
                                    mm = product(nc, ps[:, e % 2, 0:n], (uh[:, e % 2, k, :], ul[:, e % 2, k, :]),
                                                 (hp[0][:, k, :], hp[1][:, k, :]), k == 0, k == DC - 1)
                                mm.then_inc(act_mm, 1)
                                g = e // GE
                                if not (first and g == 0):
                                    outputs((ITE // GE) * it + g - 1, (g + 1) % 2, e % GE, first and g == 1)
                        body(0, True)
                        with pe.Fori(1, NIT) as it:
                            body(it, False)
                        for j in range(GE):
                            outputs(NG - 1, (NG - 1) % 2, j, False)

                    @block.scalar
                    def _(act):
                        def finish(eg, e, first):
                            act.wait_ge(act_mm, eg + 1)
                            if not (first and e < 2):
                                act.wait_ge(w_done, eg - 1)
                            nc.scalar.activation(ga[:, e % 2], ps[:, e % 2, 0:n], ACT.Gelu_apprx_tanh).then_inc(gelu_done, 1)
                            act.wait_ge(w_done, eg + 1)
                            nc.scalar.activation(wh[:, (e // GE) % 2, e % GE], wt[:, e % 2], ACT.Copy).then_inc(whi, 1)

                        def body(it, first):
                            for e in range(ITE):
                                eg = ITE * it + e
                                g = e // GE
                                loads = 2 * it + g // 2 + 1
                                if e % GE == 0:
                                    act.wait_ge(u_in[g % 2], 16 * loads)
                                if not (first and e < 2):
                                    act.wait_ge(act_mm, eg - 1)
                                nc.scalar.activation(uh[:, e % 2], us[:, g % 2, :, (e % GE) * P:(e % GE + 1) * P], ACT.Copy).then_inc(uhi, 1)
                                if not (first and e == 0):
                                    finish(eg - 1, (e - 1) % ITE, first)
                                if e % GE == 0:
                                    act.wait_ge(v_in[g % 2], 16 * loads)
                                    if not (first and g < 2):
                                        act.wait_ge(out_mm, DC * ((ITE // GE) * it + g - 1))
                                nc.scalar.activation(vh[:, g % 2, e % GE], vs[:, g % 2, e % GE], ACT.Copy).then_inc(vhi, 1)
                        body(0, True)
                        with act.Fori(1, NIT) as it:
                            body(it, False)
                        finish(NKEY - 1, ITE - 1, False)

                    @block.vector
                    def _(dve):
                        def add_outputs(g, j, first):
                            for c in range(CPS * j, CPS * (j + 1)):
                                dve.wait_ge(out_mm, DC * g + c + 1)
                                if c == 0 and not first:
                                    dve.wait_ge(x_done, DC * g)
                                add_gated(l, c, 5, ps[:, 2 + c % OB, :], lo).then_inc(x_done, 1)

                        def finish(it, eg, e, first):
                            g = e // GE
                            if e % GROWS == 0:
                                dve.wait_ge(g_in[e // GROWS], 16 * (it + 1))
                            dve.wait_ge(gelu_done, eg + 1)
                            if not (first and e < 2):
                                dve.wait_ge(wlo, eg - 1)
                            nc.vector.tensor_tensor(wt[:, e % 2].rearrange("p (b t) -> p b t", t=TB), ga[:, e % 2].rearrange("p (b t) -> p b t", t=TB),
                                                    gs[:, e // GROWS, :, e % GROWS, :], ALU.mult).then_inc(w_done, 1)
                            dve.wait_ge(whi, eg + 1)
                            nc.vector.tensor_tensor(wl[:, g % 2, e % GE], wt[:, e % 2], f32(wh[:, g % 2, e % GE]), ALU.subtract).then_inc(wlo, 1)
                            if not (first and g == 0):
                                add_outputs((ITE // GE) * it + g - 1, e % GE, first and g == 1)

                        def body(it, first):
                            for e in range(ITE):
                                eg = ITE * it + e
                                if not (first and e == 0):
                                    if e == 0:
                                        finish(it - 1, eg - 1, ITE - 1, False)
                                    else:
                                        finish(it, eg - 1, e - 1, first)
                                dve.wait_ge(vhi, eg + 1)
                                g = e // GE
                                nc.vector.tensor_tensor(vl[:, g % 2, e % GE], vs[:, g % 2, e % GE], f32(vh[:, g % 2, e % GE]), ALU.subtract).then_inc(vlo, 1)
                        body(0, True)
                        with dve.Fori(1, NIT) as it:
                            body(it, False)
                        finish(NIT - 1, NKEY - 1, ITE - 1, False)
                        for j in range(GE):
                            add_outputs(NG - 1, j, False)

        phase_start()
        for l in range(DEPTH):
            last_layer = l == DEPTH - 1
            lo = CTX if last_layer else 0
            if l == 0:
                phase_ada(0, 0, 4)
            with ExitStack() as st:
                mix = sb(st, f"mix{l}", [P, DC, T])
                with ExitStack() as st1:
                    fm = sb(st1, f"fm{l}", [P, FM, T])
                    tm = sb(st1, f"tm{l}", [P, TT, TMC])
                    with ExitStack() as st2:
                        hp = [sb(st2, f"h_{x}{l}", [P, DC, T], F32R) for x in ("hi", "lo")]
                        phase_norm(f"norm_mix{l}", d["norm_mix_g"][l], mods[l], 0, 0, mix, hp)
                        phase_proj(l, lo, hp, fm, tm)
                    with ExitStack() as st2:
                        hk = sb(st2, f"hk{l}", [P, 4, T])
                        cum = sb(st2, f"cum{l}", [P, 6, TT, P + 1])
                        phase_gates(l, fm, hk, cum, (0, 4, 4) if l == 0 else None)
                        phase_scan(l, lo, fm, tm, hk, cum, mix)
                    phase_attn(l, lo, fm, tm, mix)
                    phase_post(l, lo, fm, mix, (0, 8, 4) if l == 0 else None)
                phase_out(l, lo, mix)
            with ExitStack() as st:
                hp = [sb(st, f"h2_{x}{l}", [P, DC, T - lo], F32R) for x in ("hi", "lo")]
                with ExitStack() as st1:
                    h2 = sb(st1, f"h2{l}", [P, DC, T])
                    phase_norm(f"norm_ffn{l}", d["norm_ffn_g"][l], mods[l], 3, lo, h2, hp)
                with ExitStack() as st1:
                    iT, jT, gT = (sb(st1, f"{x}T{l}", [P, T - lo]) for x in "ijg")
                    phase_route(l, lo, hp, iT, jT, gT, (l + 1, 0, 12) if not last_layer else None)
                    phase_dense(l, lo, iT, jT, gT)
                phase_peer(l, lo, hp, gates_dram)
            clear_layer_sems()
        with ExitStack() as st:
            y = sb(st, "y", [P, DC, T])
            phase_norm("norm_final", d["final_norm_g"], None, None, CTX, y)
            stored = sem("stored")
            with nc.Block() as block:
                @block.sync
                def _(sp):
                    sp.dma_start(out, y[:, :, CTX:T]).then_inc(stored, 16)
                    sp.wait_ge(stored, 16)


def constants():
    c = {}
    c["ident"] = np.eye(P, dtype=np.float32)
    c["iota"] = np.tile(np.arange(P, dtype=np.float32), (P, 1))
    c["mean64"] = np.kron(np.eye(2), np.full((64, 64), 1.0 / 64)).astype(np.float32)
    f = np.arange(P)
    partner = (f // 16) * 16 + (f + 8) % 16
    rotp = np.zeros((P, P), np.float32)
    rotp[partner, f] = 1.0
    c["rotp"] = rotp
    freqs = np.float32(ROPE_BASE) ** (-np.arange(8, dtype=np.float32) / np.float32(8))
    n = np.arange(SEQ)
    pos = np.stack([n // GRID_W, n % GRID_W]).astype(np.float32)
    ang = (pos[(f // 16) % 2] * freqs[f % 8][:, None]).astype(np.float32)
    c["cosT"] = np.cos(ang).astype(np.float32)
    c["sinT"] = (np.sin(ang) * np.where(f % 16 < 8, -1.0, 1.0)[:, None]).astype(np.float32)
    mask = np.zeros((P, 2 * NL, HALF), np.int32)
    s = np.arange(P)[:, None]
    for dr in range(2):
        for i, L in enumerate(LEVELS):
            j = np.arange(HALF)[None, :]
            mask[:, NL * dr + i] = (s // (2 * L) == j // L) & ((s // L) % 2 == dr)
    c["mask"] = mask
    c["maskd"] = np.eye(P, dtype=np.int32)
    return c


def lay_out(x, c, ctx, c_ctx, ada_w, ada_b, norm_mix_g, norm_ffn_g, w_in, w_out,
            gla_gate_w, gla_gate_b, gla_norm_g, hgrn_lb_raw, hgrn_norm_g,
            mla_q_norm_g, mla_kv_norm_g, mla_w_uq, mla_w_ukv, diff_lambda, diff_norm_g,
            peer_wq, peer_keys, peer_u, peer_v, final_norm_g):
    a = constants()
    cols = lambda v: np.swapaxes(v.reshape(*v.shape[:-1], -1, P), -1, -2)
    tokens = np.concatenate([ctx[0], x[0]], axis=0)
    a["xT"] = tokens.T.reshape(DC, P, T).transpose(1, 0, 2)
    a["cvec"] = np.stack([c[0], c_ctx], axis=-1).reshape(DC, P, 2).transpose(1, 0, 2)
    a["ada_w"], a["ada_b"] = ada_w, cols(ada_b)
    a["norm_mix_g"], a["norm_ffn_g"], a["final_norm_g"] = cols(norm_mix_g), cols(norm_ffn_g), cols(final_norm_g)
    g, h, m, f = 0, 800, 2080, 2432
    fm_cols = [(g + 512, 256), (h + 512, 256), (h, 256), (g, 128), (g + 128, 128), (h + 768, 512),
               (m, 192), (m + 320, 32), (g + 768, 32), (m + 192, 128), (f, 512)]
    tm_cols = [(g + 256, 256), (h + 256, 256), (f + 512, 256)]
    w = np.concatenate([w_in[:, :, o:o + n] for o, n in fm_cols], axis=-1)
    a["w_fm"] = w.reshape(DEPTH, DC, P, FM, P).transpose(0, 3, 2, 1, 4)
    w = np.concatenate([w_in[:, :, o:o + n] for o, n in tm_cols], axis=-1)
    a["w_tm"] = w.reshape(DEPTH, DC, P, TMC).transpose(0, 2, 1, 3)
    a["w_out"] = w_out.reshape(DEPTH, DC, P, DC, P).transpose(0, 3, 2, 1, 4)
    zero = np.zeros_like(gla_gate_w[:, 0])
    a["gate_w"] = np.concatenate([np.stack([gla_gate_w[:, 0], zero], axis=2),
                                  np.stack([zero, gla_gate_w[:, 1]], axis=2)], axis=1)
    a["gate_b"] = gla_gate_b.transpose(0, 2, 1)
    a["lb_raw"] = cols(hgrn_lb_raw).transpose(1, 0, 2)
    a["g_head"] = np.stack([np.tile(v, (1, 2)) for v in (gla_norm_g, hgrn_norm_g, diff_norm_g)], axis=-1)
    a["g_q0"], a["g_q1"] = mla_q_norm_g[:, 0:P, None], mla_q_norm_g[:, P:, None]
    a["g_kv"] = mla_kv_norm_g[:, :, None]
    a["w_uq"] = mla_w_uq.reshape(DEPTH, MLA_Q, HEADS, MLA_DQ)
    a["w_ukv"] = mla_w_ukv.reshape(DEPTH, MLA_KV, HEADS, P)
    a["lam"] = diff_lambda
    a["w_pq"] = peer_wq.reshape(DEPTH, DC, P, 2 * PH, P).transpose(0, 3, 2, 1, 4)
    a["keysT"] = peer_keys.reshape(DEPTH, 2 * PH, NKEY, P).transpose(0, 3, 1, 2)
    a["uT"] = peer_u.reshape(DEPTH, NG, GE * P, DC, P).transpose(0, 1, 4, 3, 2)
    a["v"] = peer_v.reshape(DEPTH, NG, GE, P, D_MODEL).transpose(0, 1, 3, 2, 4)
    return a


def kernel(**inputs):
    import concourse.bacc as _bacc
    from concourse.bass_utils import run_bass_kernel_spmd as _run

    nc = _bacc.Bacc("TRN2", target_bir_lowering=False, num_devices=1)
    arrays, d = {}, {}
    for name, a in lay_out(**{k: np.asarray(v) for k, v in inputs.items()}).items():
        a = np.ascontiguousarray(a)
        arrays[f"in_{name}"] = a
        d[name] = nc.dram_tensor(f"in_{name}", a.shape, mybir.dt.from_np(a.dtype), kind="ExternalInput").ap()
    out = nc.dram_tensor("out_yT", (P, DC, SEQ), F32, kind="ExternalOutput").ap()
    build(nc, d, out)
    r = _run(nc, [arrays], core_ids=[0])
    y = r.results[0]["out_yT"]
    return y.transpose(2, 1, 0).reshape(1, SEQ, D_MODEL)
```
